# Optimizing a Trainium2 kernel written in Bass

```python
import math
import jax, jax.numpy as jnp
from jax import lax
import numpy as np

D_MODEL = 1024
BATCH = 1
SEQ = 256
DEPTH = 2

N_MIXERS = 2
N_DIFF_LAYERS = (DEPTH + 1) // 2
N_NSA_LAYERS = DEPTH // 2

DEEPNORM_ALPHA = (2 * DEPTH) ** 0.25
DEEPNORM_BETA = (8 * DEPTH) ** -0.25
LN_EPS = 1e-5
RMS_EPS = 1e-5
NEG_INF = -1e30
FORCED_SCORE = 1e6

DIFF_HEADS = 8
DIFF_HEAD_DIM = 64
DIFF_V_DIM = 2 * DIFF_HEAD_DIM
DIFF_Q_BLOCK = 128

NSA_HEADS = 16
NSA_GROUPS = 4
NSA_HEAD_DIM = 64
NSA_CMP_LEN = 32
NSA_CMP_STRIDE = 16
NSA_CMP_HIDDEN = 128
NSA_SLC_LEN = 64
NSA_SLC_TOPK = 16
NSA_WINDOW = 512
NSA_Q_BLOCK = 64

FFN_HIDDEN = -(-8 * D_MODEL // (3 * 256)) * 256

kernel_name = 'hybrid_diffattn_nsa_deepnorm_adaln'

def layer_norm(x, g, b):
    xf = x.astype(jnp.float32)
    mu = jnp.mean(xf, axis=-1, keepdims=True)
    var = jnp.mean(jnp.square(xf - mu), axis=-1, keepdims=True)
    return ((xf - mu) * lax.rsqrt(var + LN_EPS) * g.astype(jnp.float32) + b.astype(jnp.float32)).astype(x.dtype)

def rms_norm(x, g):
    xf = x.astype(jnp.float32)
    y = xf * lax.rsqrt(jnp.mean(jnp.square(xf), axis=-1, keepdims=True) + RMS_EPS)
    return (y * g.astype(jnp.float32)).astype(x.dtype)

def alibi_slopes(n_heads):
    return 2.0 ** (-8.0 * jnp.arange(1, n_heads + 1, dtype=jnp.float32) / n_heads)

def masked_softmax(s, mask):
    p = jax.nn.softmax(jnp.where(mask, s, NEG_INF), axis=-1)
    return jnp.where(mask, p, 0.0)

def diff_attention(h, w_in, w_out, lam_q1, lam_k1, lam_q2, lam_k2, subln_g, layer_idx):
    B, T, _ = h.shape
    H, dh = DIFF_HEADS, DIFF_HEAD_DIM
    q, k, v = jnp.split(h @ w_in, 3, axis=-1)
    q = q.reshape(B, T, H, 2, dh)
    k = k.reshape(B, T, H, 2, dh)
    v = v.reshape(B, T, H, DIFF_V_DIM)
    lam_init = 0.8 - 0.6 * math.exp(-0.3 * layer_idx)
    f32 = jnp.float32
    lam = (jnp.exp(jnp.sum(lam_q1.astype(f32) * lam_k1.astype(f32)))
           - jnp.exp(jnp.sum(lam_q2.astype(f32) * lam_k2.astype(f32))) + lam_init)
    slopes = alibi_slopes(H)[:, None, None, None]
    scale = dh ** -0.5
    outs = []
    for qb in range(T // DIFF_Q_BLOCK):
        start = qb * DIFF_Q_BLOCK
        end = start + DIFF_Q_BLOCK
        qi = q[:, start:end]
        kj = k[:, :end]
        vj = v[:, :end]
        dist = (jnp.arange(start, end)[:, None] - jnp.arange(end)[None, :]).astype(f32)
        s = jnp.einsum('bqhcd,bkhcd->bhcqk', qi, kj).astype(f32) * scale - slopes * dist
        p = masked_softmax(s, dist >= 0)
        a = p[:, :, 0] - lam * p[:, :, 1]
        outs.append(jnp.einsum('bhqk,bkhe->bqhe', a.astype(vj.dtype), vj))
    o = jnp.concatenate(outs, axis=1)
    o = rms_norm(o, subln_g) * (1.0 - lam_init)
    return o.reshape(B, T, H * DIFF_V_DIM) @ w_out

def compress_blocks(x, win_idx, pos, w1, w2):
    B, _, G, d = x.shape
    n_cmp, L = win_idx.shape
    blk = x[:, win_idx] + pos[:, None, :]
    blk = blk.transpose(0, 1, 3, 2, 4).reshape(B, n_cmp, G, L * d)
    return jax.nn.gelu(blk @ w1) @ w2

def cmp_to_slc_weights(n_cmp, n_slc):
    c_start = jnp.arange(n_cmp) * NSA_CMP_STRIDE
    s_start = jnp.arange(n_slc) * NSA_SLC_LEN
    ov = (jnp.minimum(c_start[:, None] + NSA_CMP_LEN, s_start[None, :] + NSA_SLC_LEN)
          - jnp.maximum(c_start[:, None], s_start[None, :]))
    return jnp.clip(ov, 0).astype(jnp.float32) / NSA_CMP_LEN

def nsa_attention(h, w_in, cmp_pos_k, cmp_pos_v, cmp_k_w1, cmp_k_w2, cmp_v_w1, cmp_v_w2, w_out):
    B, T, _ = h.shape
    H, G, d = NSA_HEADS, NSA_GROUPS, NSA_HEAD_DIM
    hpg = H // G
    QB, W, LS = NSA_Q_BLOCK, NSA_WINDOW, NSA_SLC_LEN
    f32 = jnp.float32
    sizes = [H * d] + [G * d] * 6 + [H * 3]
    parts = jnp.split(h @ w_in, np.cumsum(sizes)[:-1].tolist(), axis=-1)
    q = parts[0].reshape(B, T, G, hpg, d)
    k_c, v_c, k_s, v_s, k_w, v_w = [p.reshape(B, T, G, d) for p in parts[1:7]]
    gates = jax.nn.sigmoid(parts[7].astype(f32)).astype(h.dtype).reshape(B, T, G, hpg, 3)

    n_cmp = (T - NSA_CMP_LEN) // NSA_CMP_STRIDE + 1
    n_slc = T // LS
    k_sel = min(NSA_SLC_TOPK, n_slc)
    win_idx = jnp.arange(n_cmp)[:, None] * NSA_CMP_STRIDE + jnp.arange(NSA_CMP_LEN)[None, :]
    kc = compress_blocks(k_c, win_idx, cmp_pos_k, cmp_k_w1, cmp_k_w2)
    vc = compress_blocks(v_c, win_idx, cmp_pos_v, cmp_v_w1, cmp_v_w2)
    kpos_c = win_idx[:, -1]
    overlap = cmp_to_slc_weights(n_cmp, n_slc)
    ksb = k_s.reshape(B, n_slc, LS, G, d).transpose(0, 3, 1, 2, 4)
    vsb = v_s.reshape(B, n_slc, LS, G, d).transpose(0, 3, 1, 2, 4)
    kw_pad = jnp.pad(k_w, ((0, 0), (W, 0), (0, 0), (0, 0)))
    vw_pad = jnp.pad(v_w, ((0, 0), (W, 0), (0, 0), (0, 0)))
    slopes = alibi_slopes(H).reshape(G, hpg)
    scale = d ** -0.5
    b_ix = jnp.arange(B)[:, None, None, None]
    g_ix = jnp.arange(G)[None, :, None, None]
    blk_ids = jnp.arange(n_slc)

    def one_block(qb):
        start = qb * QB
        qi = lax.dynamic_slice_in_dim(q, start, QB, axis=1)
        gi = lax.dynamic_slice_in_dim(gates, start, QB, axis=1)
        qpos = start + jnp.arange(QB)
        dist_c = (qpos[:, None] - kpos_c[None, :]).astype(f32)
        s_c = (jnp.einsum('bqghd,bngd->bghqn', qi, kc).astype(f32) * scale
               - slopes[:, :, None, None] * dist_c)
        p_c = masked_softmax(s_c, dist_c >= 0)
        o_c = jnp.einsum('bghqn,bngd->bqghd', p_c.astype(vc.dtype), vc)
        imp = jnp.einsum('bghqn,nj->bgqj', p_c, overlap)
        q_blk = qpos // LS
        forced = ((blk_ids[None, :] == 0) | (blk_ids[None, :] == q_blk[:, None])
                  | (blk_ids[None, :] == q_blk[:, None] - 1))
        causal_blk = blk_ids[None, :] * LS <= qpos[:, None]
        imp = jnp.where(causal_blk, jnp.where(forced, FORCED_SCORE, imp), NEG_INF)
        _, top_idx = lax.top_k(imp, k_sel)
        ksel = ksb[b_ix, g_ix, top_idx]
        vsel = vsb[b_ix, g_ix, top_idx].reshape(B, G, QB, k_sel * LS, d)
        kpos_s = top_idx[..., None] * LS + jnp.arange(LS)
        dist_s = (qpos[None, None, :, None, None] - kpos_s).astype(f32).reshape(B, G, 1, QB, k_sel * LS)
        s_s = (jnp.einsum('bqghd,bgqkld->bghqkl', qi, ksel).astype(f32).reshape(B, G, hpg, QB, k_sel * LS)
               * scale - slopes[None, :, :, None, None] * dist_s)
        p_s = masked_softmax(s_s, dist_s >= 0)
        o_s = jnp.einsum('bghqm,bgqmd->bqghd', p_s.astype(vsel.dtype), vsel)
        kw = lax.dynamic_slice_in_dim(kw_pad, start, W + QB, axis=1)
        vw = lax.dynamic_slice_in_dim(vw_pad, start, W + QB, axis=1)
        kpos_w = start - W + jnp.arange(W + QB)
        dist_w = qpos[:, None] - kpos_w[None, :]
        mask_w = (dist_w >= 0) & (dist_w < W) & (kpos_w[None, :] >= 0)
        s_w = (jnp.einsum('bqghd,bkgd->bghqk', qi, kw).astype(f32) * scale
               - slopes[:, :, None, None] * dist_w.astype(f32))
        p_w = masked_softmax(s_w, mask_w)
        o_w = jnp.einsum('bghqk,bkgd->bqghd', p_w.astype(vw.dtype), vw)
        o = gi[..., 0:1] * o_c + gi[..., 1:2] * o_s + gi[..., 2:3] * o_w
        return o.reshape(B, QB, H * d)

    o = lax.map(one_block, jnp.arange(T // QB))
    o = o.transpose(1, 0, 2, 3).reshape(B, T, H * d)
    return o @ w_out

def swiglu(h, w_gu, w_down):
    g, u = jnp.split(h @ w_gu, 2, axis=-1)
    return (jax.nn.silu(g) * u) @ w_down

def setup_inputs(seed: int = 0) -> dict:
    key = jax.random.key(seed)
    ks = iter(jax.random.split(key, 32))
    f32 = jnp.float32

    def nrm(shape, scale):
        return jax.random.normal(next(ks), shape, f32) * scale

    D, beta = D_MODEL, DEEPNORM_BETA
    Hd, dh = DIFF_HEADS, DIFF_HEAD_DIM
    Hn, G, d = NSA_HEADS, NSA_GROUPS, NSA_HEAD_DIM
    Lc = NSA_CMP_LEN
    x = nrm((BATCH, SEQ, D), 1.0)
    c = nrm((BATCH, D), 1.0)
    diff_w_in = jnp.concatenate([nrm((N_DIFF_LAYERS, D, 2 * Hd * dh), D ** -0.5),
                                 nrm((N_DIFF_LAYERS, D, 2 * Hd * dh), D ** -0.5),
                                 nrm((N_DIFF_LAYERS, D, Hd * DIFF_V_DIM), beta * D ** -0.5)], axis=-1)
    diff_w_out = nrm((N_DIFF_LAYERS, Hd * DIFF_V_DIM, D), beta * (Hd * DIFF_V_DIM) ** -0.5)
    diff_lam_q1 = nrm((N_DIFF_LAYERS, dh), 0.1)
    diff_lam_k1 = nrm((N_DIFF_LAYERS, dh), 0.1)
    diff_lam_q2 = nrm((N_DIFF_LAYERS, dh), 0.1)
    diff_lam_k2 = nrm((N_DIFF_LAYERS, dh), 0.1)
    diff_subln_g = 1.0 + nrm((N_DIFF_LAYERS, DIFF_V_DIM), 0.02)
    col_scale = jnp.concatenate([jnp.ones((Hn * d,), f32)]
                                + [jnp.full((G * d,), s, f32) for s in (1.0, beta, 1.0, beta, 1.0, beta)]
                                + [jnp.ones((Hn * 3,), f32)])
    nsa_w_in = nrm((N_NSA_LAYERS, D, col_scale.shape[0]), D ** -0.5) * col_scale
    nsa_cmp_pos_k = nrm((N_NSA_LAYERS, Lc, d), 0.1)
    nsa_cmp_pos_v = nrm((N_NSA_LAYERS, Lc, d), 0.1)
    nsa_cmp_k_w1 = nrm((N_NSA_LAYERS, Lc * d, NSA_CMP_HIDDEN), (Lc * d) ** -0.5)
    nsa_cmp_k_w2 = nrm((N_NSA_LAYERS, NSA_CMP_HIDDEN, d), NSA_CMP_HIDDEN ** -0.5)
    nsa_cmp_v_w1 = nrm((N_NSA_LAYERS, Lc * d, NSA_CMP_HIDDEN), (Lc * d) ** -0.5)
    nsa_cmp_v_w2 = nrm((N_NSA_LAYERS, NSA_CMP_HIDDEN, d), NSA_CMP_HIDDEN ** -0.5)
    nsa_w_out = nrm((N_NSA_LAYERS, Hn * d, D), beta * (Hn * d) ** -0.5)
    ada_w = nrm((DEPTH, D, 6 * D), 0.1 * D ** -0.5)
    ada_b = nrm((DEPTH, 6 * D), 0.01)
    ln_mix_g = 1.0 + nrm((DEPTH, D), 0.02)
    ln_mix_b = nrm((DEPTH, D), 0.02)
    ln_ffn_g = 1.0 + nrm((DEPTH, D), 0.02)
    ln_ffn_b = nrm((DEPTH, D), 0.02)
    ffn_w_gu = nrm((DEPTH, D, 2 * FFN_HIDDEN), beta * D ** -0.5)
    ffn_w_down = nrm((DEPTH, FFN_HIDDEN, D), beta * FFN_HIDDEN ** -0.5)
    return {'x': x, 'c': c,
            'diff_w_in': diff_w_in, 'diff_w_out': diff_w_out,
            'diff_lam_q1': diff_lam_q1, 'diff_lam_k1': diff_lam_k1,
            'diff_lam_q2': diff_lam_q2, 'diff_lam_k2': diff_lam_k2, 'diff_subln_g': diff_subln_g,
            'nsa_w_in': nsa_w_in, 'nsa_cmp_pos_k': nsa_cmp_pos_k, 'nsa_cmp_pos_v': nsa_cmp_pos_v,
            'nsa_cmp_k_w1': nsa_cmp_k_w1, 'nsa_cmp_k_w2': nsa_cmp_k_w2,
            'nsa_cmp_v_w1': nsa_cmp_v_w1, 'nsa_cmp_v_w2': nsa_cmp_v_w2, 'nsa_w_out': nsa_w_out,
            'ada_w': ada_w, 'ada_b': ada_b,
            'ln_mix_g': ln_mix_g, 'ln_mix_b': ln_mix_b, 'ln_ffn_g': ln_ffn_g, 'ln_ffn_b': ln_ffn_b,
            'ffn_w_gu': ffn_w_gu, 'ffn_w_down': ffn_w_down}

def reference(x, c, diff_w_in, diff_w_out, diff_lam_q1, diff_lam_k1, diff_lam_q2, diff_lam_k2,
              diff_subln_g, nsa_w_in, nsa_cmp_pos_k, nsa_cmp_pos_v, nsa_cmp_k_w1, nsa_cmp_k_w2,
              nsa_cmp_v_w1, nsa_cmp_v_w2, nsa_w_out, ada_w, ada_b, ln_mix_g, ln_mix_b,
              ln_ffn_g, ln_ffn_b, ffn_w_gu, ffn_w_down):
    for i in range(DEPTH):
        mod = jax.nn.silu(c) @ ada_w[i] + ada_b[i]
        sh_a, sc_a, g_a, sh_f, sc_f, g_f = jnp.split(mod[:, None, :], 6, axis=-1)
        h = x * (1.0 + sc_a) + sh_a
        j = i // N_MIXERS
        if i % N_MIXERS == 0:
            y = diff_attention(h, diff_w_in[j], diff_w_out[j], diff_lam_q1[j], diff_lam_k1[j],
                               diff_lam_q2[j], diff_lam_k2[j], diff_subln_g[j], i)
        else:
            y = nsa_attention(h, nsa_w_in[j], nsa_cmp_pos_k[j], nsa_cmp_pos_v[j], nsa_cmp_k_w1[j],
                              nsa_cmp_k_w2[j], nsa_cmp_v_w1[j], nsa_cmp_v_w2[j], nsa_w_out[j])
        x = layer_norm(DEEPNORM_ALPHA * x + (1.0 + g_a) * y, ln_mix_g[i], ln_mix_b[i])
        h = x * (1.0 + sc_f) + sh_f
        x = layer_norm(DEEPNORM_ALPHA * x + (1.0 + g_f) * swiglu(h, ffn_w_gu[i], ffn_w_down[i]),
                       ln_ffn_g[i], ln_ffn_b[i])
    return x


_drawn_inputs = setup_inputs


def setup_inputs(seed=0):
    import zlib

    import numpy as np

    out = dict(_drawn_inputs(seed))
    spreads = {}
    factors = {'diff_lam_q1': 200.0,
     'diff_lam_k1': 2.861,
     'diff_lam_k2': 107.744,
     'diff_subln_g': 21.66,
     'nsa_cmp_pos_k': 8.0,
     'nsa_cmp_pos_v': 6.264,
     'nsa_cmp_k_w1': 6.555,
     'nsa_cmp_k_w2': 6.728,
     'ada_b': 4.253}
    for name, (base, spread) in spreads.items():
        noise = np.random.default_rng([zlib.crc32(name.encode()), seed]).standard_normal(out[name].shape)
        drawn = base * np.exp(spread * noise) if base else spread * noise
        out[name] = __import__('jax').numpy.asarray(drawn.astype(out[name].dtype))
    for name, factor in factors.items():
        out[name] = (out[name] * factor).astype(out[name].dtype)
    return out
```

```python
from contextlib import ExitStack

import concourse.bass as bass
from concourse import mybir

F32 = mybir.dt.float32
F32R = mybir.dt.float32r
ALU = mybir.AluOpType
ACT = mybir.ActivationFunctionType
AX = mybir.AxisListType

P = 128
D = 1024
T = 256
KT = D // P
QT = T // P
HID = 2816
HT = HID // P
HEADS = 8
TILES = 8
N_CMP = 15
BANK = 512
ALPHA = 4.0 ** 0.25
LN_EPS = 1e-5
RMS_EPS = 1e-5
SCALE = 0.125
LAM_INIT = 0.8 - 0.6
FAR_BELOW = -3.0e38

C_HEAD = 0
C_FFN = (8, 42)
C_NSA = 30
C_W1 = 36
C_Q = 38
N_COL = 64
R_V, R_OUT, R_DOWN = 0, (8, 38), (16, 46)
N_ROW = 68
RING = 4
ADA_RING = 3
SPLIT = 2


def decoder(nc, col_w, row_w, ada_w, ada_bias, cols, xT, x_nat, ln_rows, lam, subln, gate_w, pos, w2, consts, out):
    ctx = ExitStack()
    with ctx:
        def sb(name, shape, dt=F32):
            return ctx.enter_context(nc.sbuf_tensor(name, shape, dt))

        def sem(name):
            return ctx.enter_context(nc.semaphore(name))

        col_raw = sb("col_raw", [P, RING, KT * 256])
        row_raw = sb("row_raw", [P, RING, D])
        ada_raw = sb("ada_raw", [P, ADA_RING, D])
        col_hi = sb("col_hi", [P, SPLIT, KT * 256], F32R)
        col_lo = sb("col_lo", [P, SPLIT, KT * 256], F32R)
        row_hi = sb("row_hi", [P, SPLIT, D], F32R)
        row_lo = sb("row_lo", [P, SPLIT, D], F32R)
        x_sb = sb("x_sb", [P, QT, D])
        xn = sb("xn", [P, QT, D])
        h_f = sb("h_f", [P, KT, T])
        h_hi = sb("h_hi", [P, KT, T], F32R)
        h_lo = sb("h_lo", [P, KT, T], F32R)
        o_hi = sb("o_hi", [P, KT, T], F32R)
        o_lo = sb("o_lo", [P, KT, T], F32R)
        kv_sb = sb("kv_sb", [P, 2 * D])
        scratch = sb("scratch", [P, 3072])
        bias_t = sb("bias_t", [P, 2, 384])
        modrow = sb("modrow", [P, 3, 256])
        bias_rows = sb("bias_rows", [P, 2, 256])
        consts_sb = sb("consts_sb", [P, 128 + 384 + 512 + 8])
        cols_sb = sb("cols_sb", [P, 9, KT])
        c_rep = sb("c_rep", [P, KT, 32])
        zeros = sb("zeros", [P, P], F32R)
        modcol = sb("modcol", [P, 12, KT])
        fold = sb("fold", [P, 4, 2, KT])
        gate_sb = sb("gate_sb", [P, QT * 48])
        gate_wsb = sb("gate_wsb", [P, KT, 48])
        pos_sb = sb("pos_sb", [P, 2, 16])
        w2_sb = sb("w2_sb", [P, 192])
        gel = sb("gel", [P, 2, 4, 16])
        kcT = sb("kcT", [P, 2, 16])
        sml = sb("sml", [P, 8, 40])
        stats = sb("stats", [P, QT, 24])
        silu_sb8 = sb("silu_c_cols", [P, KT])
        lam_t = sb("lam_t", [P, 5])
        lam_sums, lam_exps, neg_lam = lam_t[:, 0:2], lam_t[:, 2:4], lam_t[:, 4:5]
        half = sb("half", [P, 1])
        og = sb("og", [P, 8, 64])

        ident = consts_sb[:, 0:128]
        dist = consts_sb[:, 128:512]
        dist_c = consts_sb[:, 512:1024]
        own_block = consts_sb[:, 1024:1032]
        gate_row = scratch[:, 0:1024]
        silu_sb = scratch[:, 1024:1536].rearrange("p (s n) -> p s n", s=2)
        hid_sb = scratch[:, 1536:2048].rearrange("p (s n) -> p s n", s=2)
        v_sb = xn
        lam_sb, subln_sb = og[:, 4:8, :], og[:, 2:4, :].rearrange("p a n -> p (a n)")
        gel_rep = og[:, :, :].rearrange("p a n -> p (a n)").rearrange("p (g n) -> p g n", g=4)
        gate_flat = gate_wsb[:, :, :].rearrange("p k n -> p (k n)")
        vrep = gate_flat[:, 0:256]
        smc = gate_flat[:, 256:384].rearrange("p (a n) -> p a n", a=4)
        s_diff = scratch[:, 0:1536].rearrange("p (s c n) -> p s c n", s=2, c=2)
        at_diff = scratch[:, 1536:2304].rearrange("p (s n) -> p s n", s=2)
        o_diff = scratch[:, 2304:2560].rearrange("p (q n) -> p q n", q=2)
        sq_junk = scratch[:, 2560:3072].rearrange("p (s q n) -> p s q n", s=2, q=2)
        q_all = h_f
        kk = kv_sb[:, 0:1024].rearrange("p (b g n) -> p b g n", b=2, g=2)
        vv = kv_sb[:, 1024:2048].rearrange("p (b q n) -> p b q n", b=2, q=2)
        s_nsa = scratch[:, 0:1536].rearrange("p (u b n) -> p u b n", u=2, b=2)
        at_nsa = scratch[:, 1536:3072].rearrange("p (u b n) -> p u b n", u=2, b=2)
        kvc = scratch[:, 0:1024].rearrange("p (v g n) -> p v g n", v=2, g=2)
        kvs = scratch[:, 1024:2048].rearrange("p (v g n) -> p v g n", v=2, g=2)
        blk = xn[:, :, :].rearrange("p q n -> p (q n)")[:, 0:1920]
        blk_hi = o_hi[:, :, :].rearrange("p k n -> p (k n)")[:, 0:1920]
        blk_lo = o_lo[:, :, :].rearrange("p k n -> p (k n)")[:, 0:1920]
        sc = scratch[:, 0:512]
        pc = scratch[:, 512:1024]
        pct = scratch[:, 1024:1536]
        vcp = kv_sb[:, 0:1024].rearrange("p (g n) -> p g n", g=2)

        psum = ctx.enter_context(nc.psum_tensor("psum", [P, 8 * BANK], F32))

        def bank(i, n=1):
            return psum[:, i * BANK:(i + n) * BANK]

        col_loaded = [sem(f"col_loaded{i}") for i in range(RING)]
        row_loaded = [sem(f"row_loaded{i}") for i in range(RING)]
        ada_loaded = [sem(f"ada_loaded{i}") for i in range(ADA_RING)]
        bias_loaded = [sem(f"bias_loaded{i}") for i in range(2)]
        cols_in, xT_in, x_in, consts_in, lnrow_in = (sem(n) for n in ("cols_in", "xT_in", "x_in", "consts_in", "lnrow_in"))
        small_in = sem("small_in")
        c_ready, zero_ready = sem("c_ready"), sem("zero_ready")
        silu_c = sem("silu_c")
        col_hi_made, col_lo_made, col_used = sem("col_hi_made"), sem("col_lo_made"), sem("col_used")
        row_hi_made, row_lo_made, row_used = sem("row_hi_made"), sem("row_lo_made"), sem("row_used")
        ada_used, modrow_made, modT_done, modcol_made = (sem(n) for n in ("ada_used", "modrow_made", "modT_done", "modcol_made"))
        gate_spread, gate_made = sem("gate_spread"), sem("gate_made")
        fold_made = sem("fold_made")
        aff_dve, aff_act, h_hi_made, h_made = (sem(n) for n in ("aff_dve", "aff_act", "h_hi_made", "h_made"))
        v_act, v_dve = sem("v_act"), sem("v_dve")
        lam_ready, lam_sum, lam_exp = sem("lam_ready"), sem("lam_sum"), sem("lam_exp")
        qk_made, scored, biased, bias_ready, max_made, exp_made, mixed = (
            sem(n) for n in ("qk_made", "scored", "biased", "bias_ready", "max_made", "exp_made", "mixed"))
        at_done, at_act, at_dve, pv_done, squared, ms_made, rstd_made, o_made, ot_done, o_hi_made, o_lo_made = (
            sem(n) for n in ("at_done", "at_act", "at_dve", "pv_done", "squared", "ms_made", "rstd_made", "o_made",
                             "ot_done", "o_hi_made", "o_lo_made"))
        y_read, z_made, var_made, ln_rstd, xn_made, xt_done, x_updated, x_scaled = (
            sem(n) for n in ("y_read", "z_made", "var_made", "ln_rstd", "xn_made", "xt_done", "x_updated", "x_scaled"))
        silu_made, hid_made, act_hi_made, act_lo_made = (sem(n) for n in ("silu_made", "hid_made", "act_hi_made", "act_lo_made"))
        gates_done, gates_exp, gates_made = sem("gates_done"), sem("gates_exp"), sem("gates_made")
        kv_evac, swapped, blk_made, blk_hi_made, blk_lo_made = (
            sem(n) for n in ("kv_evac", "swapped", "blk_made", "blk_hi_made", "blk_lo_made"))
        gel_zeroed, gelu_made, gel_spread, w2_done, cmp_evac = (
            sem(n) for n in ("gel_zeroed", "gelu_made", "gel_spread", "w2_done", "cmp_evac"))
        c_scored, c_biased, c_exp, c_made, c_tr, c_evac, c_out, c_added = (
            sem(n) for n in ("c_scored", "c_biased", "c_exp", "c_made", "c_tr", "c_evac", "c_out", "c_added"))
        vcp_made = sem("vcp_made")
        first_scored = sem("first_scored")
        dve_done = sem("dve_done")
        pool_done = sem("pool_done")
        out_stored = sem("out_stored")

        def at(base, b):
            return base if b is None else b * 4 + base

        def loads(c, b):
            n = 16 * (c // RING + 1)
            return n if b is None else b * 16 + n

        block = ctx.enter_context(nc.Block())

        @block.sync
        def _(sp):
            def load_col(c, b=None):
                if c >= RING:
                    sp.wait_ge(col_lo_made, at(c - RING + 1, b))
                src = col_w[c, :, :] if b is None else col_w[bass.ds(b * 4 + c, 1), :, :].rearrange("a p n -> p (a n)")
                sp.dma_start(col_raw[:, c % RING, :], src).then_inc(col_loaded[c % RING], 16)

            def load_row(c, b=None):
                if c >= RING:
                    sp.wait_ge(row_lo_made, at(c - RING + 1, b))
                src = row_w[c, :, :] if b is None else row_w[bass.ds(b * 4 + c, 1), :, :].rearrange("a p n -> p (a n)")
                sp.dma_start(row_raw[:, c % RING, :], src).then_inc(row_loaded[c % RING], 16)

            def load_ada(c):
                if c % 8 == 0:
                    load_bias(c // 8)
                if c >= ADA_RING:
                    sp.wait_ge(ada_used, c - ADA_RING + 1)
                sp.dma_start(ada_raw[:, c % ADA_RING, :], ada_w[c, :, :]).then_inc(ada_loaded[c % ADA_RING], 16)

            def load_bias(e):
                if e >= 2:
                    sp.wait_ge(modrow_made, e - 1)
                sp.dma_start(bias_rows[:, e % 2, :], ada_bias[e, :, :]).then_inc(bias_loaded[e % 2], 16)

            def load_ln_rows(n):
                sp.dma_start(kv_sb[:, :], ln_rows[n, :].partition_broadcast(P)).then_inc(lnrow_in, 16)

            for c in range(16):
                load_ada(c)
            for c in range(8):
                load_row(R_V + c)
                if c == 3:
                    sp.dma_start(x_sb[:, :, :], x_nat).then_inc(x_in, 16)
            load_col(C_HEAD)
            load_col(C_HEAD + 1)
            for h in range(HEADS):
                if h < HEADS - 2:
                    load_col(C_HEAD + h + 2)
                if 2 <= h < 6:
                    load_row(R_OUT[0] + h - 2)
                for i in range(4):
                    load_ada(16 + 4 * h + i)
            for layer in range(2):
                for c in range(4, 8):
                    load_row(R_OUT[layer] + c)
                if layer == 0:
                    sp.wait_ge(scored, HEADS)
                    load_ln_rows(0)
                else:
                    sp.wait_ge(c_out, 4)
                    load_ln_rows(2)
                c0, r0 = C_FFN[layer], R_DOWN[layer]
                load_col(c0)
                load_col(c0 + 1)

                def ffn_loads(i, b=None):
                    load_col(c0 + 2 * i, b)
                    load_col(c0 + 2 * i + 1, b)
                    load_row(r0 + 2 * i - 2, b)
                    load_row(r0 + 2 * i - 1, b)

                with sp.Fori(0, 4) as b:
                    for i in (1, 2):
                        ffn_loads(i, b)
                ffn_loads(9)
                ffn_loads(10)
                if layer == 0:
                    for c in range(48, 56):
                        load_ada(c)
                load_row(r0 + 20)
                load_row(r0 + 21)
                if layer == 0:
                    for c in range(56, 64):
                        load_ada(c)
                sp.wait_ge(x_updated, 4 * layer + 2)
                load_ln_rows(2 * layer + 1)
                if layer == 0:
                    for c in range(C_NSA, C_Q):
                        load_col(c)
                    for i in range(4):
                        load_col(C_Q + i)
                        load_row(R_OUT[1] + i)
                    for t in range(TILES):
                        for i in range(4):
                            load_ada(64 + 4 * t + i)
            for q in range(QT):
                sp.wait_ge(x_updated, 6 + q + 1)
                sp.dma_start(out[q, :, :], x_sb[:, q, :]).then_inc(out_stored, 16)
            sp.wait_ge(out_stored, 32)

        @block.tensor
        def _(pe):
            def three(dst, sh, sl, mh, ml, start, stop, **kw):
                nc.tensor.matmul(dst, sh, mh, start=start, stop=False, **kw)
                nc.tensor.matmul(dst, sh, ml, start=False, stop=False, **kw)
                return nc.tensor.matmul(dst, sl, mh, start=False, stop=stop, **kw)

            def col_views(c):
                return (col_hi[:, c % SPLIT, :].rearrange("p (k n) -> p k n", k=KT),
                        col_lo[:, c % SPLIT, :].rearrange("p (k n) -> p k n", k=KT))

            def col_product(c, dst, b=None, stage=None):
                pe.wait_ge(col_lo_made, at(c + 1, b))
                wh, wl = col_views(c)
                for i in range(2):
                    for k in range(KT):
                        if stage is not None and i == 0:
                            pe.wait_ge(h_made, 8 * stage + k + 1)
                        last = three(dst[:, 256 * i:256 * i + 256], wh[:, k, 128 * i:128 * i + 128],
                                     wl[:, k, 128 * i:128 * i + 128], h_hi[:, k, :], h_lo[:, k, :],
                                     k == 0, k == KT - 1)
                last.then_inc(col_used, 1)

            def col_product_natural(c, dst):
                pe.wait_ge(col_lo_made, c + 1)
                wh, wl = col_views(c)
                for q in range(QT):
                    for k in range(KT):
                        last = three(dst[:, 256 * q:256 * q + 256], h_hi[:, k, 128 * q:128 * q + 128],
                                     h_lo[:, k, 128 * q:128 * q + 128], wh[:, k, :], wl[:, k, :], k == 0, k == KT - 1)
                last.then_inc(col_used, 1)

            def row_product(c, sh, sl, y0, start, stop, b=None, **kw):
                pe.wait_ge(row_lo_made, at(c + 1, b))
                for q in range(QT):
                    for j in range(2):
                        last = three(bank(y0 + 2 * q + j), sh[:, 128 * q:128 * q + 128], sl[:, 128 * q:128 * q + 128],
                                     row_hi[:, c % SPLIT, BANK * j:BANK * j + BANK],
                                     row_lo[:, c % SPLIT, BANK * j:BANK * j + BANK], start, stop, **kw)
                last.then_inc(row_used, 1)

            def ada_chunk(c, dst):
                pe.wait_ge(ada_loaded[c % ADA_RING], 16 * (c // ADA_RING + 1))
                k = c % 8
                for j in range(4):
                    last = nc.tensor.matmul(dst[32 * j:32 * j + 32, :], c_rep[:, k, :],
                                            ada_raw[:, c % ADA_RING, 256 * j:256 * j + 256],
                                            start=(k == 0), stop=(k == 7), tile_position=(0, 32 * j))
                last.then_inc(ada_used, 1)

            def mod_transpose(slot, dst):
                for i in range(2):
                    last = nc.tensor.transpose(dst[:, 128 * i:128 * i + 128], modrow[:, slot, 128 * i:128 * i + 128], ident)
                last.then_inc(modT_done, 1)

            def gate_part(slot, dst, r):
                for i in range(2):
                    j = 2 * r + i
                    last = nc.tensor.matmul(dst[:, 256 * i:256 * i + 256], ident[:, 32 * j:32 * j + 1].broadcast_to([P, P]),
                                            modrow[:, slot, :], start=True, stop=True)
                last.then_inc(gate_spread, 1)

            pe.wait_ge(c_ready, 1)
            for k in range(8):
                ada_chunk(k, bank(0)[:, 0:256])
            for k in range(8):
                ada_chunk(8 + k, bank(1)[:, 0:256])
            pe.wait_ge(consts_in, 16)
            pe.wait_ge(modrow_made, 1)
            mod_transpose(0, bank(2))
            pe.wait_ge(modrow_made, 2)
            mod_transpose(1, bank(3))

            for k in range(KT):
                pe.wait_ge(h_made, k + 1)
                if k == 0:
                    pe.wait_ge(modcol_made, 2)
                row_product(R_V + k, h_hi[:, k, :], h_lo[:, k, :], 0, k == 0, k == KT - 1)

            def project(h):
                if h >= 2:
                    pe.wait_ge(qk_made, h - 1)
                col_product(C_HEAD + h, bank(4 + h % 2))

            def score(h):
                pe.wait_ge(qk_made, h + 1)
                if h >= 1:
                    pe.wait_ge(biased, 4 * h)
                qk = qk_diff[:, h % 2, :]
                for q, lo, n in ((0, 0, 128), (1, 128, 256)):
                    for c in range(2):
                        rows = slice(64 * c, 64 * c + 64)
                        last = nc.tensor.matmul(bank(6 + c)[:, lo:lo + n], qk[rows, 128 * q:128 * q + 128],
                                                qk[rows, 256:256 + n], start=True, stop=True)
                last.then_inc(scored, 1)

            def transpose_probs(h):
                pe.wait_ge(mixed, h + 1)
                if h >= 1:
                    pe.wait_ge(at_act, h)
                for i in range(3):
                    last = nc.tensor.transpose(bank(2)[:, 128 * i:128 * i + 128], s_diff[:, h % 2, 0, 128 * i:128 * i + 128], ident)
                last.then_inc(at_done, 1)

            def weigh_values(h):
                pe.wait_ge(at_act, h + 1)
                if h >= 1:
                    pe.wait_ge(o_made, h)
                a = at_diff[:, h % 2, :]
                v = slice(P * h, P * h + P)
                nc.tensor.matmul(bank(3)[:, 0:128], a[:, 0:128], v_sb[:, 0, v], start=True, stop=True)
                nc.tensor.matmul(bank(3)[:, 128:256], a[:, 128:256], v_sb[:, 0, v], start=True, stop=False)
                nc.tensor.matmul(bank(3)[:, 128:256], a[:, 256:384], v_sb[:, 1, v], start=False, stop=True).then_inc(pv_done, 1)

            def transpose_out(h):
                pe.wait_ge(o_made, h + 1)
                if h >= 1:
                    pe.wait_ge(o_lo_made, h)
                for q in range(QT):
                    last = nc.tensor.transpose(bank(1)[:, 128 * q:128 * q + 128], o_diff[:, q, :], ident)
                last.then_inc(ot_done, 1)

            def attention_ada(layer, t, modcols):
                if t % 2 == 0 and t > 0:
                    e = 6 * layer + 1 + t // 2
                    pe.wait_ge(modrow_made, e + 1)
                    if modcols:
                        pe.wait_ge(modcol_made, modcols)
                for i in range(4):
                    ada_chunk(48 * layer + 16 + 4 * t + i, bank(0)[:, 0:256])

            def step_mod_transpose(layer, t):
                if t in (4, 6):
                    pe.wait_ge(modrow_made, 6 * layer + t // 2 + 2)
                    mod_transpose(0, bank(0)[:, 256:512])

            qk_diff = kv_sb[:, 0:1024].rearrange("p (s n) -> p s n", s=2)
            for t in range(9):
                if t < HEADS:
                    project(t)
                if t >= 2:
                    transpose_probs(t - 2)
                if 1 <= t:
                    score(t - 1)
                step_mod_transpose(0, t)
                if t >= 3:
                    transpose_out(t - 3)
                if t < HEADS:
                    if t == 0:
                        pe.wait_ge(v_act, 1)
                        pe.wait_ge(v_dve, 1)
                    attention_ada(0, t, {4: 3, 6: 4}.get(t, 0))
                if t >= 2:
                    weigh_values(t - 2)

            def out_product(layer, k, lo_needed):
                c = R_OUT[layer] + k
                pe.wait_ge(o_lo_made, lo_needed)
                row_product(c, o_hi[:, k, :], o_lo[:, k, :], 4, k == 0, k == KT - 1)

            pe.wait_ge(biased, 4 * HEADS)
            pe.wait_ge(modrow_made, 6)
            gate_part(1, bank(0), 0)
            out_product(0, 0, 1)
            transpose_probs(7)
            out_product(0, 1, 2)
            transpose_out(6)
            weigh_values(7)
            pe.wait_ge(gate_made, 1)
            gate_part(1, bank(0), 1)
            for k in range(2, 6):
                out_product(0, k, k + 1)
            transpose_out(7)
            out_product(0, 6, 7)
            out_product(0, 7, 8)

            def transpose_rows(n, y0):
                for q in range(QT):
                    pe.wait_ge(xn_made, 2 * n + q + 1)
                    for k in range(KT):
                        o = 128 * (k % 4)
                        last = nc.tensor.transpose(bank(y0 + 2 * (k // 4) + q)[:, o:o + 128], xn[:, q, 128 * k:128 * k + 128], ident)
                    last.then_inc(xt_done, 1)

            def ffn(layer):
                c0, r0, j0 = C_FFN[layer], R_DOWN[layer], HT * layer

                def hidden(j, b=None, stage=None):
                    if j >= 2:
                        pe.wait_ge(hid_made, at(j0 + j - 1, b))
                    col_product(c0 + j, bank(4 + j % 2), b, stage)

                def down(j, b=None):
                    pe.wait_ge(act_lo_made, at(j0 + j + 1, b))
                    s = j % 4
                    row_product(r0 + j, o_hi[:, s, :], o_lo[:, s, :], 0, False, False, b, skip_group_check=True)

                def steps(i, b=None, group=None):
                    for n, step in enumerate((lambda: hidden(2 * i, b), lambda: hidden(2 * i + 1, b),
                                              lambda: down(2 * i - 2, b), lambda: down(2 * i - 1, b))):
                        step()
                        if group is not None:
                            if n == 0 and group == 7:
                                pe.wait_ge(modrow_made, 7)
                            for k in (2 * n, 2 * n + 1):
                                ada_chunk(8 * group + k, bank(6)[:, 256 * (group % 2):256 * (group % 2) + 256])

                hidden(0, stage=2 * layer + 1)
                if layer == 0:
                    pe.wait_ge(zero_ready, 1)
                for i in range(4):
                    nc.tensor.matmul(bank(i), zeros[:, :], h_hi[:, 0:2, :].rearrange("p k n -> p (k n)"), start=True, stop=False, skip_group_check=True)
                gate_part(2, bank(7), 0)
                hidden(1)
                pe.wait_ge(gate_made, 4 * layer + 3)
                gate_part(2, bank(7), 1)
                with pe.Fori(0, 4) as b:
                    for i in (1, 2):
                        steps(i, b)
                steps(9, None, 6 if layer == 0 else None)
                steps(10, None, 7 if layer == 0 else None)
                down(20)
                if layer == 0:
                    pe.wait_ge(gate_made, 4)
                    mod_transpose(0, bank(7))
                down(21)
                if layer == 0:
                    pe.wait_ge(modrow_made, 8)
                    mod_transpose(1, bank(5))

            transpose_rows(0, 0)
            ffn(0)
            pe.wait_ge(modcol_made, 6)
            transpose_rows(1, 4)

            def kv_product(i, natural, stage=None):
                if i >= 2:
                    pe.wait_ge(kv_evac, i - 1)
                if natural:
                    col_product_natural(C_NSA + i, bank(i % 2))
                else:
                    col_product(C_NSA + i, bank(i % 2), None, stage)

            kv_product(0, False, 2)
            pe.wait_ge(small_in, 80)
            for q in range(QT):
                for k in range(KT):
                    last = nc.tensor.matmul(bank(2)[:, 48 * q:48 * q + 48], h_f[:, k, 128 * q:128 * q + 128],
                                            gate_wsb[:, k, :], start=(k == 0), stop=(k == KT - 1))
            last.then_inc(gates_done, 1)
            for i in range(1, 4):
                kv_product(i, False)
            for i in range(4, 6):
                kv_product(i, True)
            for v in range(2):
                c = C_W1 + v
                pe.wait_ge(col_lo_made, c + 1)
                pe.wait_ge(blk_lo_made, 1)
                wh = col_hi[:, c % SPLIT, :].rearrange("p (l n) -> p l n", l=16)
                wl = col_lo[:, c % SPLIT, :].rearrange("p (l n) -> p l n", l=16)
                bh = blk_hi.rearrange("p (v n l) -> p v n l", v=2, l=16)
                bl = blk_lo.rearrange("p (v n l) -> p v n l", v=2, l=16)
                for l in range(16):
                    last = three(bank(3)[:, 64 * v:64 * v + 60], wh[:, l, :], wl[:, l, :], bh[:, v, :, l], bl[:, v, :, l],
                                 l == 0, l == 15)
                last.then_inc(col_used, 1)

            def q_product(i):
                if i >= 1:
                    pe.wait_ge(qk_made, HEADS + i)
                col_product(C_Q + i, bank(4))

            q_product(0)
            pe.wait_ge(gelu_made, 2)
            nc.tensor.matmul(bank(3)[:, 128:192], w2_sb[:, 0:128], gel[:, 0, :, :].rearrange("p g n -> p (g n)"),
                             start=True, stop=True)
            pe.wait_ge(gel_spread, 1)
            for g in range(4):
                last = nc.tensor.matmul(bank(3)[:, 192 + 64 * g:256 + 64 * g],
                                        gel_rep[:, g, :],
                                        w2_sb[:, 128:192], start=True, stop=True)
            last.then_inc(w2_done, 1)

            def nsa_score(t):
                pe.wait_ge(qk_made, HEADS + t // 2 + 1)
                if t == 0:
                    pe.wait_ge(kv_evac, 6)
                if t >= 1:
                    pe.wait_ge(biased, 4 * HEADS + 8 * t)
                gp = t // 4

                def keys(u, q):
                    rows = slice(64 * u, 64 * u + 64)
                    for s in range(2):
                        if q == 0:
                            dst = bank(5)[:, 256 * u + 128 * s:256 * u + 128 * s + 128]
                        else:
                            dst = bank(6 + u)[:, 256 * s:256 * s + 256]
                        last = nc.tensor.matmul(dst, q_all[rows, t, 128 * q:128 * q + 128],
                                                kk[rows, s, gp, 0:128 * (q + 1)], start=True, stop=True)
                    return last

                keys(0, 0).then_inc(first_scored, 1)
                keys(1, 1)
                keys(0, 1)
                pe.wait_ge(first_scored, t + 1)
                keys(1, 0).then_inc(scored, 1)

            def nsa_transpose(t, u):
                pe.wait_ge(exp_made, 4 * HEADS + 8 * t + 4 * u + 4)
                if u == 1:
                    pe.wait_ge(at_act, HEADS + t + 1)
                elif t >= 1:
                    pe.wait_ge(at_dve, t)
                for s in range(2):
                    for i in range(3):
                        last = nc.tensor.transpose(bank(1 + s)[:, 128 * i:128 * i + 128],
                                                   s_nsa[:, u, s, 128 * i:128 * i + 128], ident)
                last.then_inc(at_done, 1)

            def nsa_weigh(t, u):
                if u == 0:
                    if t >= 1:
                        pe.wait_ge(o_made, HEADS + t)
                    else:
                        pe.wait_ge(cmp_evac, 1)
                else:
                    pe.wait_ge(at_dve, t + 1)
                cols = slice(64 * (2 * (t // 4) + u), 64 * (2 * (t // 4) + u) + 64)
                for q in range(QT):
                    for s in range(2):
                        o = 64 * ((2 * u + q) * 2 + s)
                        dst = bank(3)[:, o:o + 64]
                        if q == 0:
                            last = nc.tensor.matmul(dst, at_nsa[:, u, s, 0:128], vv[:, s, 0, cols], start=True, stop=True)
                        else:
                            nc.tensor.matmul(dst, at_nsa[:, u, s, 128:256], vv[:, s, 0, cols], start=True, stop=False)
                            last = nc.tensor.matmul(dst, at_nsa[:, u, s, 256:384], vv[:, s, 1, cols], start=False, stop=True)
                if u == 1:
                    last.then_inc(pv_done, 1)

            for t in range(TILES + 1):
                if t < TILES:
                    nsa_score(t)
                if t >= 1:
                    nsa_transpose(t - 1, 0)
                if t % 2 == 1 and t < 7:
                    q_product((t + 1) // 2)
                step_mod_transpose(1, t)
                if t < TILES:
                    attention_ada(1, t, {4: 7, 6: 8}.get(t, 0))
                if t >= 1:
                    nsa_transpose(t - 1, 1)
                    nsa_weigh(t - 1, 0)
                    nsa_weigh(t - 1, 1)
                if t == TILES - 1:
                    for tt in range(TILES):
                        for q in range(QT):
                            for u in range(2):
                                rows = slice(64 * u, 64 * u + 64)
                                if u == 1 and tt == 0 and q == 0:
                                    pe.wait_ge(biased, 4 * HEADS + 8 * TILES)
                                last = nc.tensor.matmul(bank(4 + u)[:, 128 * q + 16 * tt:128 * q + 16 * tt + 16],
                                                        q_all[rows, tt, 128 * q:128 * q + 128],
                                                        kcT[rows, tt // 4, :], start=True, stop=True)
                    last.then_inc(c_scored, 1)

            pe.wait_ge(c_made, 1)
            for gp in range(2):
                for q in range(QT):
                    i = 2 * gp + q
                    last = nc.tensor.transpose(bank(6)[:, 128 * i:128 * i + 128], pc[:, 256 * q + 128 * gp:256 * q + 128 * gp + 128], ident)
            last.then_inc(c_tr, 1)
            pe.wait_ge(c_evac, 1)
            pe.wait_ge(vcp_made, 2)
            pe.wait_ge(modrow_made, 12)
            pe.wait_ge(o_made, HEADS + TILES)
            for gp in range(2):
                for q in range(QT):
                    i = 2 * gp + q
                    nc.tensor.matmul(bank(i), pct[:, 128 * i:128 * i + 128], vcp[:, gp, :], start=True, stop=True).then_inc(c_out, 1)

            def nsa_out_transpose(r):
                pe.wait_ge(c_added, 2 * (r // 2) + 2)
                for i in range(2):
                    for q in range(QT):
                        o = 256 * i + 128 * q
                        last = nc.tensor.transpose(bank(r)[:, o:o + 128], xn[:, q, 128 * (2 * r + i):128 * (2 * r + i) + 128], ident)
                last.then_inc(ot_done, 1)

            nsa_out_transpose(0)
            nsa_out_transpose(1)
            for k in range(KT):
                if k in (1, 2):
                    nsa_out_transpose(k + 1)
                out_product(1, k, HEADS + k // 2 + 1)
                if k == 2:
                    pe.wait_ge(o_lo_made, HEADS + 1)
                    gate_part(1, bank(0), 0)
                if k == 4:
                    pe.wait_ge(gate_made, 5)
                    gate_part(1, bank(0), 1)
            pe.wait_ge(gate_made, 6)
            transpose_rows(2, 0)
            ffn(1)

        @block.scalar
        def _(act):
            def split_col(c, b=None):
                if c >= N_COL:
                    return
                act.wait_ge(col_loaded[c % RING], loads(c, b))
                if c >= SPLIT:
                    act.wait_ge(col_used, at(c - SPLIT + 1, b))
                nc.scalar.activation(col_hi[:, c % SPLIT, :], col_raw[:, c % RING, :], ACT.Copy).then_inc(col_hi_made, 1)

            def split_row(c, b=None):
                if c >= N_ROW:
                    return
                act.wait_ge(row_loaded[c % RING], loads(c, b))
                if c >= SPLIT:
                    act.wait_ge(row_used, at(c - SPLIT + 1, b))
                nc.scalar.activation(row_hi[:, c % SPLIT, :], row_raw[:, c % RING, :], ACT.Copy).then_inc(row_hi_made, 1)

            act.dma_start(cols_sb[:, :, :], cols).then_inc(cols_in, 16)
            act.dma_start(h_f[:, :, :], xT).then_inc(xT_in, 16)
            act.dma_start(consts_sb[:, :], consts).then_inc(consts_in, 16)
            act.wait_ge(cols_in, 16)
            nc.scalar.activation(silu_sb8[:, :], cols_sb[:, 0, :], ACT.Silu).then_inc(silu_c, 1)
            act.wait_ge(lam_sum, 1)
            nc.scalar.activation(lam_exps, lam_sums, ACT.Exp).then_inc(lam_exp, 1)

            def input_tiles(stage):
                act.wait_ge(fold_made, stage + 1)
                if stage == 0:
                    act.wait_ge(xT_in, 16)
                else:
                    act.wait_ge(xt_done, 2 * stage)
                    y0 = 4 if stage == 2 else 0
                def affine(k):
                    src = h_f[:, k, :] if stage == 0 else \
                        bank(y0 + 2 * (k // 4), 2).rearrange("p (q n) -> p q n", q=2)[:, :, 128 * (k % 4):128 * (k % 4) + 128]
                    dst = h_f[:, k, :] if stage == 0 else h_f[:, k, :].rearrange("p (q n) -> p q n", q=2)
                    nc.scalar.activation(dst, src, ACT.Identity, scale=fold[:, stage, 0, k:k + 1],
                                         bias=fold[:, stage, 1, k:k + 1]).then_inc(aff_act, 1)

                for k in range(KT):
                    if k < 4:
                        act.wait_ge(aff_dve, 4 * stage + k + 1)
                    else:
                        act.wait_ge(aff_act, 4 * stage + k - 3)
                    nc.scalar.activation(h_hi[:, k, :], h_f[:, k, :], ACT.Copy).then_inc(h_hi_made, 1)
                    if k < 4:
                        affine(4 + k)

            input_tiles(0)
            for c in range(8):
                split_row(c)
            split_col(0)
            split_col(1)
            act.wait_ge(row_used, 8)
            nc.scalar.activation(v_sb[:, 0, :], bank(0, 2), ACT.Copy).then_inc(v_act, 1)

            qk_diff = kv_sb[:, 0:1024].rearrange("p (s n) -> p s n", s=2)

            def copy_probs(h):
                act.wait_ge(at_done, h + 1)
                if h >= 2:
                    act.wait_ge(pv_done, h - 1)
                nc.scalar.activation(at_diff[:, h % 2, :], bank(2)[:, 0:384], ACT.Copy).then_inc(at_act, 1)

            def exps(h):
                act.wait_ge(max_made, h + 1)
                for c in range(2):
                    for q, lo, n in ((0, 0, 128), (1, 128, 256)):
                        s = s_diff[:, h % 2, c, lo:lo + n]
                        i = 2 * c + q
                        nc.scalar.activation(s, s, ACT.Exp, scale=SCALE, bias=sml[:, h, 4 + i:5 + i],
                                             accum_out=sml[:, h, 8 + i:9 + i]).then_inc(exp_made, 1)

            def squares(h):
                act.wait_ge(pv_done, h + 1)
                for q in range(QT):
                    nc.scalar.activation(sq_junk[:, h % 2, q, :], bank(3)[:, 128 * q:128 * q + 128], ACT.Square,
                                         scale=sml[:, h, 12 + q:13 + q], accum_out=sml[:, h, 18 + q:19 + q]).then_inc(squared, 1)

            def out_hi(h):
                act.wait_ge(ot_done, h + 1)
                nc.scalar.activation(o_hi[:, h, :], bank(1)[:, 0:256], ACT.Copy).then_inc(o_hi_made, 1)

            for t in range(9):
                if t < HEADS:
                    act.wait_ge(col_used, t + 1)
                    if t >= 2:
                        act.wait_ge(scored, t - 1)
                    nc.scalar.activation(qk_diff[:, t % 2, :], bank(4 + t % 2), ACT.Copy).then_inc(qk_made, 1)
                if t >= 2:
                    copy_probs(t - 2)
                if t < HEADS - 2:
                    split_col(C_HEAD + t + 2)
                elif t < HEADS:
                    split_row(R_OUT[0] + t + 2 - HEADS)
                if t >= 3:
                    out_hi(t - 3)
                if t >= 1:
                    exps(t - 1)
                if t >= 2:
                    squares(t - 2)

            def copy_gate(i, src, r):
                act.wait_ge(gate_spread, i + 1)
                nc.scalar.activation(gate_row[:, BANK * r:BANK * r + BANK], src, ACT.Copy).then_inc(gate_made, 1)

            split_row(R_OUT[0] + 2)
            copy_probs(7)
            split_row(R_OUT[0] + 3)
            out_hi(6)
            squares(7)
            copy_gate(0, bank(0), 0)
            copy_gate(1, bank(0), 1)
            for c in range(4, 7):
                split_row(R_OUT[0] + c)
            out_hi(7)
            split_row(R_OUT[0] + 7)
            split_col(C_FFN[0])
            split_col(C_FFN[0] + 1)

            def ffn(layer):
                c0, r0, j0 = C_FFN[layer], R_DOWN[layer], HT * layer

                def silu(j, b=None):
                    act.wait_ge(col_used, at(c0 + j + 1, b))
                    if j >= 2:
                        act.wait_ge(hid_made, at(j0 + j - 1, b))
                    nc.scalar.activation(silu_sb[:, j % 2, :], bank(4 + j % 2)[:, 0:256], ACT.Silu).then_inc(silu_made, 1)

                def hid_hi(j, b=None):
                    act.wait_ge(hid_made, at(j0 + j + 1, b))
                    if j >= 4:
                        act.wait_ge(row_used, at(r0 + j - 3, b))
                    nc.scalar.activation(o_hi[:, j % 4, :], hid_sb[:, j % 2, :], ACT.Copy).then_inc(act_hi_made, 1)

                def steps(i, b=None):
                    silu(2 * i, b)
                    if i < 10:
                        split_col(c0 + 2 * i + 2, b)
                    hid_hi(2 * i - 1, b)
                    silu(2 * i + 1, b)
                    if i < 10:
                        split_col(c0 + 2 * i + 3, b)
                    hid_hi(2 * i, b)
                    split_row(r0 + 2 * i, b)
                    split_row(r0 + 2 * i + 1, b)

                silu(0)
                split_col(c0 + 2)
                copy_gate(4 * layer + 2, bank(7), 0)
                silu(1)
                split_col(c0 + 3)
                hid_hi(0)
                copy_gate(4 * layer + 3, bank(7), 1)
                split_row(r0)
                split_row(r0 + 1)
                with act.Fori(0, 4) as b:
                    for i in (1, 2):
                        steps(i, b)
                steps(9)
                steps(10)
                hid_hi(21)
                if layer == 0:
                    split_col(C_NSA)
                    split_col(C_NSA + 1)

            input_tiles(1)
            ffn(0)
            input_tiles(2)

            def copy_kv(i):
                act.wait_ge(col_used, C_NSA + i + 1)
                if i < 2:
                    dst = kvc[:, i, :, :].rearrange("p g n -> p (g n)")
                elif i < 4:
                    dst = kk[:, i - 2, :, :].rearrange("p g n -> p (g n)")
                else:
                    dst = vv[:, i - 4, :, :].rearrange("p q n -> p (q n)")
                if i == 2:
                    act.wait_ge(x_updated, 4)
                nc.scalar.activation(dst, bank(i % 2), ACT.Copy).then_inc(kv_evac, 1)

            for i in range(6):
                copy_kv(i)
                split_col(C_NSA + i + 2)
                if i == 0:
                    act.wait_ge(gates_done, 1)
                    nc.scalar.activation(gate_sb[:, :], bank(2)[:, 0:96], ACT.Exp, scale=-1.0).then_inc(gates_exp, 1)
                if i == 3:
                    act.wait_ge(blk_made, 8)
                    nc.scalar.activation(blk_hi, blk, ACT.Copy).then_inc(blk_hi_made, 1)
            for v in range(2):
                split_col(C_W1 + v + 2)
            act.wait_ge(gel_zeroed, 1)
            for v in range(2):
                nc.scalar.activation(gel[:, v, :, 0:N_CMP], bank(3)[:, 64 * v:64 * v + 60].rearrange("p (g n) -> p g n", g=4),
                                     ACT.Gelu_apprx_tanh).then_inc(gelu_made, 1)

            def copy_q(i):
                act.wait_ge(col_used, C_Q + i + 1)
                nc.scalar.activation(q_all[:, 2 * i:2 * i + 2, :].rearrange("p t n -> p (t n)"), bank(4), ACT.Copy).then_inc(qk_made, 1)
                if i < 2:
                    split_col(C_Q + i + 2)
                else:
                    split_row(R_OUT[1] + i - 2)

            def nsa_exps(t, u):
                act.wait_ge(max_made, HEADS + 2 * t + u + 1)
                for q, lo, n in ((0, 0, 128), (1, 128, 256)):
                    for s in range(2):
                        x = s_nsa[:, u, s, lo:lo + n]
                        i = (2 * u + q) * 2 + s
                        nc.scalar.activation(x, x, ACT.Exp, scale=SCALE, bias=sml[:, t, 8 + i:9 + i],
                                             accum_out=sml[:, t, 16 + i:17 + i]).then_inc(exp_made, 1)

            act.wait_ge(gates_done, 1)
            copy_q(0)
            for t in range(TILES + 1):
                if t >= 1:
                    act.wait_ge(at_done, HEADS + 2 * (t - 1) + 1)
                    if t >= 2:
                        act.wait_ge(pv_done, HEADS + t - 1)
                    nc.scalar.activation(at_nsa[:, 0, :, :], bank(1, 2).rearrange("p (s n) -> p s n", s=2)[:, :, 0:384],
                                         ACT.Copy).then_inc(at_act, 1)
                if t < TILES:
                    nsa_exps(t, 0)
                if t % 2 == 1 and t < 7:
                    copy_q((t + 1) // 2)
                if t < TILES:
                    nsa_exps(t, 1)
            act.wait_ge(c_biased, 1)
            nc.scalar.activation(sc, sc, ACT.Exp, scale=SCALE).then_inc(c_exp, 1)
            act.wait_ge(c_tr, 1)
            nc.scalar.activation(pct, bank(6), ACT.Copy).then_inc(c_evac, 1)

            def nsa_out_hi(r):
                act.wait_ge(ot_done, HEADS + r + 1)
                nc.scalar.activation(o_hi[:, 2 * r:2 * r + 2, :].rearrange("p t n -> p (t n)"), bank(r), ACT.Copy).then_inc(o_hi_made, 1)

            nsa_out_hi(0)
            nsa_out_hi(1)
            split_row(R_OUT[1] + 2)
            nsa_out_hi(2)
            split_row(R_OUT[1] + 3)
            nsa_out_hi(3)
            split_row(R_OUT[1] + 4)
            copy_gate(4, bank(0), 0)
            split_row(R_OUT[1] + 5)
            split_row(R_OUT[1] + 6)
            copy_gate(5, bank(0), 1)
            split_row(R_OUT[1] + 7)
            split_col(C_FFN[1])
            split_col(C_FFN[1] + 1)
            input_tiles(3)
            ffn(1)

        @block.vector
        def _(dve):
            own = [0]

            def then(ins):
                own[0] += 1
                ins.then_inc(dve_done, 1)
                dve.wait_ge(dve_done, own[0])

            def split_col(c, b=None):
                if c >= N_COL:
                    return
                dve.wait_ge(col_hi_made, at(c + 1, b))
                nc.vector.tensor_tensor(col_lo[:, c % SPLIT, :], col_raw[:, c % RING, :], col_hi[:, c % SPLIT, :].bitcast(F32),
                                        ALU.subtract).then_inc(col_lo_made, 1)

            def split_row(c, b=None):
                if c >= N_ROW:
                    return
                dve.wait_ge(row_hi_made, at(c + 1, b))
                nc.vector.tensor_tensor(row_lo[:, c % SPLIT, :], row_raw[:, c % RING, :], row_hi[:, c % SPLIT, :].bitcast(F32),
                                        ALU.subtract).then_inc(row_lo_made, 1)

            def make_modrow(e, src, slot):
                one = 0.0 if e % 6 in (0, 3) else 1.0
                dve.wait_ge(bias_loaded[e % 2], 16 * (e // 2 + 1))
                dve.wait_ge(ada_used, 8 * e + 8)
                nc.vector.scalar_tensor_tensor(modrow[:, slot, :], src, one, bias_rows[:, e % 2, :], ALU.add, ALU.add)\
                    .then_inc(modrow_made, 1)

            def make_modcol(n, e, src):
                dve.wait_ge(modT_done, n + 1)
                nc.vector.tensor_copy(modcol[:, e, :].rearrange("p (j i) -> p j i", j=4),
                                      src[:, 0:256].rearrange("p (i j r) -> p j i r", i=2, j=4)[:, :, :, 0]).then_inc(modcol_made, 1)

            def make_fold(stage, shift, scale, ncol):
                a, b = fold[:, stage, 0, :], fold[:, stage, 1, :]
                dve.wait_ge(modcol_made, ncol)
                if stage == 0:
                    nc.vector.tensor_copy(a, modcol[:, scale, :])
                    nc.vector.tensor_copy(b, modcol[:, shift, :]).then_inc(fold_made, 1)
                    return
                g, s = cols_sb[:, 2 * stage - 1, :], cols_sb[:, 2 * stage, :]
                nc.vector.tensor_tensor(a, g, modcol[:, scale, :], ALU.mult)
                then(nc.vector.tensor_tensor(b, s, modcol[:, scale, :], ALU.mult))
                nc.vector.tensor_tensor(b, b, modcol[:, shift, :], ALU.add).then_inc(fold_made, 1)

            def input_tiles(stage):
                if stage == 0:
                    dve.wait_ge(xT_in, 16)
                    dve.wait_ge(fold_made, 1)
                else:
                    dve.wait_ge(xt_done, 2 * stage)
                    dve.wait_ge(fold_made, stage + 1)
                    y0 = 4 if stage == 2 else 0

                def affine(k):
                    src = h_f[:, k, :] if stage == 0 else \
                        bank(y0 + 2 * (k // 4), 2).rearrange("p (q n) -> p q n", q=2)[:, :, 128 * (k % 4):128 * (k % 4) + 128]
                    dst = h_f[:, k, :] if stage == 0 else h_f[:, k, :].rearrange("p (q n) -> p q n", q=2)
                    nc.vector.tensor_scalar(dst, src, fold[:, stage, 0, k:k + 1], fold[:, stage, 1, k:k + 1],
                                            ALU.mult, ALU.add).then_inc(aff_dve, 1)

                affine(0)
                for k in range(KT):
                    if k < 3:
                        affine(k + 1)
                    dve.wait_ge(h_hi_made, 8 * stage + k + 1)
                    nc.vector.tensor_tensor(h_lo[:, k, :], h_f[:, k, :], h_hi[:, k, :].bitcast(F32), ALU.subtract)\
                        .then_inc(h_made, 1)

            def norm(n, y0):
                row_end = (R_OUT[0] + 8, R_DOWN[0] + 22, R_OUT[1] + 8, R_DOWN[1] + 22)[n]
                dve.wait_ge(row_used, row_end)
                dve.wait_ge(gate_made, 2 * n + 2)
                dve.wait_ge(x_in, 16)
                if n >= 1:
                    dve.wait_ge(x_updated, 2 * n)
                if n in (0, 2):
                    dve.wait_ge(ot_done, HEADS if n == 0 else HEADS + 4)
                for q in range(QT):
                    z = xn[:, q, :]
                    st = stats[:, q, :]
                    nc.vector.tensor_tensor(z, bank(y0 + 2 * q, 2), gate_row, ALU.mult).then_inc(y_read, 1)
                    dve.wait_ge(y_read, 2 * n + q + 1)
                    nc.vector.scalar_tensor_tensor(z, x_sb[:, q, :], ALPHA, z, ALU.mult, ALU.add).then_inc(z_made, 1)
                    dve.wait_ge(z_made, 2 * n + q + 1)
                    nc.vector.bn_stats(st[:, 0:6], z[:, 0:512])
                    then(nc.vector.bn_stats(st[:, 6:12], z[:, 512:1024]))
                    then(nc.vector.bn_aggr(st[:, 12:14], st[:, 0:12]))
                    nc.vector.tensor_scalar(st[:, 14:15], st[:, 13:14], LN_EPS, None, ALU.add).then_inc(var_made, 1)
                    dve.wait_ge(ln_rstd, 2 * n + q + 1)
                    nc.vector.tensor_scalar(z, z, st[:, 12:13], st[:, 15:16], ALU.subtract, ALU.mult).then_inc(xn_made, 1)

            dve.wait_ge(silu_c, 1)
            nc.vector.tensor_copy(c_rep[:, :, :], silu_sb8[:, :].unsqueeze(2).broadcast_to([P, KT, 32])).then_inc(c_ready, 1)
            nc.vector.memset(gel[:, :, :, :], 0.0).then_inc(gel_zeroed, 1)
            dve.wait_ge(small_in, 80)
            then(nc.vector.tensor_tensor(og[:, 0:2, :], lam_sb[:, 0:4:2, :], lam_sb[:, 1:4:2, :], ALU.mult))
            nc.vector.tensor_reduce(lam_sums, og[:, 0:2, :], op=ALU.add, axis=AX.X).then_inc(lam_sum, 1)
            dve.wait_ge(lam_exp, 1)
            then(nc.vector.tensor_tensor(neg_lam, lam_exps[:, 1:2], lam_exps[:, 0:1], ALU.subtract))
            then(nc.vector.tensor_scalar(neg_lam, neg_lam, -LAM_INIT, None, ALU.add))
            then(nc.vector.tensor_scalar(subln_sb, subln_sb, 1.0 - LAM_INIT, None, ALU.mult))
            make_modrow(0, bank(0)[:, 0:256], 0)
            make_modrow(1, bank(1)[:, 0:256], 1)
            make_modcol(0, 0, bank(2))
            make_modcol(1, 1, bank(3))
            make_fold(0, 0, 1, 2)
            input_tiles(0)
            for c in range(8):
                split_row(c)
            split_col(0)
            split_col(1)
            dve.wait_ge(row_used, 8)
            nc.vector.tensor_copy(v_sb[:, 1, :], bank(2, 2)).then_inc(v_dve, 1)

            def bias_max(h):
                dve.wait_ge(scored, h + 1)
                dve.wait_ge(bias_ready, h + 1)
                if h >= 2:
                    dve.wait_ge(at_done, h - 1)
                for c in range(2):
                    for q, lo, n in ((0, 0, 128), (1, 128, 256)):
                        i = 2 * c + q
                        nc.vector.tensor_tensor_reduce(out=s_diff[:, h % 2, c, lo:lo + n], in0=bank(6 + c)[:, lo:lo + n],
                                                       in1=bias_t[:, h % 2, lo:lo + n], scale=1.0, scalar=FAR_BELOW,
                                                       op0=ALU.add, op1=ALU.max, accum_out=sml[:, h, i:i + 1]).then_inc(biased, 1)
                dve.wait_ge(biased, 4 * h + 4)
                nc.vector.tensor_scalar(sml[:, h, 4:8], sml[:, h, 0:4], -SCALE, None, ALU.mult).then_inc(max_made, 1)

            def mix(h):
                s = sml[:, h, :]
                dve.wait_ge(exp_made, 4 * h + 4)
                then(nc.vector.reciprocal(s[:, 12:16], s[:, 8:12]))
                then(nc.vector.scalar_tensor_tensor(s[:, 16:18], s[:, 8:10], neg_lam, s[:, 14:16], ALU.mult, ALU.mult))
                for q, lo, n in ((0, 0, 128), (1, 128, 256)):
                    p0 = s_diff[:, h % 2, 0, lo:lo + n]
                    last = nc.vector.scalar_tensor_tensor(p0, s_diff[:, h % 2, 1, lo:lo + n], s[:, 16 + q:17 + q], p0,
                                                          ALU.mult, ALU.add)
                last.then_inc(mixed, 1)

            def normalise(h):
                s = sml[:, h, :]
                dve.wait_ge(squared, 2 * h + 2)
                nc.vector.tensor_scalar(s[:, 20:22], s[:, 18:20], 1.0 / P, RMS_EPS, ALU.mult, ALU.add).then_inc(ms_made, 1)
                dve.wait_ge(rstd_made, h + 1)
                then(nc.vector.tensor_tensor(s[:, 24:26], s[:, 22:24], s[:, 12:14], ALU.mult))
                if h >= 1:
                    dve.wait_ge(ot_done, h)
                for q in range(QT):
                    last = nc.vector.scalar_tensor_tensor(o_diff[:, q, :], bank(3)[:, 128 * q:128 * q + 128],
                                                          s[:, 24 + q:25 + q], subln_sb, ALU.mult, ALU.mult)
                last.then_inc(o_made, 1)

            def out_lo(h):
                dve.wait_ge(o_hi_made, h + 1)
                nc.vector.tensor_tensor(o_lo[:, h, :], bank(1)[:, 0:256], o_hi[:, h, :].bitcast(F32), ALU.subtract)\
                    .then_inc(o_lo_made, 1)

            def step_mod(layer, t, col0):
                if t % 2 == 0 and t > 0:
                    e = 6 * layer + 1 + t // 2
                    make_modrow(e, bank(0)[:, 0:256], {2: 1, 8: 2}.get(t, 0))

            def step_modcol(layer, t, col0):
                if t in (4, 6):
                    make_modcol(col0 + (t == 6), 6 * layer + 1 + t // 2, bank(0)[:, 256:512])

            for t in range(9):
                step_mod(0, t, 2)
                if t >= 1:
                    bias_max(t - 1)
                if t < HEADS - 2:
                    split_col(C_HEAD + t + 2)
                elif t < HEADS:
                    split_row(R_OUT[0] + t + 2 - HEADS)
                step_modcol(0, t, 2)
                if t >= 3:
                    out_lo(t - 3)
                if t >= 1:
                    mix(t - 1)
                if t >= 2:
                    normalise(t - 2)
            make_fold(1, 3, 4, 4)
            split_row(R_OUT[0] + 2)
            split_row(R_OUT[0] + 3)
            out_lo(6)
            normalise(7)
            for c in range(4, 7):
                split_row(R_OUT[0] + c)
            out_lo(7)
            split_row(R_OUT[0] + 7)
            split_col(C_FFN[0])
            split_col(C_FFN[0] + 1)

            def ffn(layer):
                c0, r0, j0 = C_FFN[layer], R_DOWN[layer], HT * layer

                def hid(j, b=None):
                    dve.wait_ge(silu_made, at(j0 + j + 1, b))
                    if j >= 2:
                        dve.wait_ge(act_lo_made, at(j0 + j - 1, b))
                    nc.vector.tensor_tensor(hid_sb[:, j % 2, :], bank(4 + j % 2)[:, 256:512], silu_sb[:, j % 2, :], ALU.mult)\
                        .then_inc(hid_made, 1)

                def hid_lo(j, b=None):
                    dve.wait_ge(act_hi_made, at(j0 + j + 1, b))
                    nc.vector.tensor_tensor(o_lo[:, j % 4, :], hid_sb[:, j % 2, :], o_hi[:, j % 4, :].bitcast(F32), ALU.subtract)\
                        .then_inc(act_lo_made, 1)

                def steps(i, b=None):
                    hid(2 * i, b)
                    if i < 10:
                        split_col(c0 + 2 * i + 2, b)
                    hid_lo(2 * i - 1, b)
                    hid(2 * i + 1, b)
                    if i < 10:
                        split_col(c0 + 2 * i + 3, b)
                    hid_lo(2 * i, b)
                    split_row(r0 + 2 * i, b)
                    split_row(r0 + 2 * i + 1, b)

                hid(0)
                split_col(c0 + 2)
                hid(1)
                split_col(c0 + 3)
                hid_lo(0)
                split_row(r0)
                split_row(r0 + 1)
                with dve.Fori(0, 4) as b:
                    for i in (1, 2):
                        steps(i, b)
                steps(9)
                if layer == 0:
                    make_modrow(6, bank(6)[:, 0:256], 0)
                steps(10)
                hid_lo(21)
                if layer == 0:
                    make_modrow(7, bank(6)[:, 256:512], 1)
                    make_modcol(4, 6, bank(7))
                    make_modcol(5, 7, bank(5))
                    make_fold(2, 6, 7, 6)
                    split_col(C_NSA)
                    split_col(C_NSA + 1)

            norm(0, 4)
            input_tiles(1)
            ffn(0)
            norm(1, 0)
            input_tiles(2)

            dve.wait_ge(small_in, 80)
            for c in range(6):
                if c == 1:
                    dve.wait_ge(gates_exp, 1)
                    then(nc.vector.tensor_scalar(gate_sb[:, :], gate_sb[:, :], 1.0, None, ALU.add))
                    nc.vector.reciprocal(gate_sb[:, :], gate_sb[:, :]).then_inc(gates_made, 1)
                if c == 3:
                    dve.wait_ge(swapped, 32)
                    dve.wait_ge(x_updated, 4)
                    for v in range(2):
                        for par in range(2):
                            rows = slice(64 * par, 64 * par + 64)
                            for u in range(2):
                                src = (kvc if u == par else kvs)[rows, v, :, :]
                                for gp in range(2):
                                    win = src[:, gp, :]
                                    o = (v * 4 + 2 * gp + u) * 240
                                    dst = blk[rows, o:o + 240].rearrange("p (n l) -> p n l", l=16)
                                    lo_half = win[:, 0:240].rearrange("p (n l e) -> p n l e", l=8, e=2)[:, :, :, par]
                                    hi_half = win[:, 16:256].rearrange("p (n l e) -> p n l e", l=8, e=2)[:, :, :, par]
                                    pb = pos_sb[rows, v, :]
                                    nc.vector.tensor_tensor(dst[:, :, 0:8], lo_half, pb[:, 0:8].unsqueeze(1).broadcast_to([64, N_CMP, 8]), ALU.add)
                                    last = nc.vector.tensor_tensor(dst[:, :, 8:16], hi_half, pb[:, 8:16].unsqueeze(1).broadcast_to([64, N_CMP, 8]), ALU.add)
                                if u == 1:
                                    last.then_inc(blk_made, 2)
                split_col(C_NSA + c + 2)
                if c == 3:
                    dve.wait_ge(blk_hi_made, 1)
                    nc.vector.tensor_tensor(blk_lo, blk, blk_hi.bitcast(F32), ALU.subtract).then_inc(blk_lo_made, 1)
            split_col(C_W1 + 2)
            split_col(C_W1 + 3)
            dve.wait_ge(gelu_made, 2)
            nc.vector.tensor_copy(gel_rep.rearrange("p g (r n) -> p g r n", r=8),
                                  gel[:, 1, :, :].unsqueeze(2).broadcast_to([P, 4, 8, 16])).then_inc(gel_spread, 1)
            split_col(C_Q + 2)

            def nsa_bias_max(t, u):
                dve.wait_ge(scored, HEADS + t + 1)
                dve.wait_ge(bias_ready, HEADS + 2 * t + u + 1)
                if t >= 1:
                    dve.wait_ge(at_done, HEADS + 2 * (t - 1) + u + 1)
                for q, lo, n in ((0, 0, 128), (1, 128, 256)):
                    for s in range(2):
                        i = (2 * u + q) * 2 + s
                        src = bank(5)[:, 256 * u + 128 * s:256 * u + 128 * s + 128] if q == 0 else bank(6 + u)[:, 256 * s:256 * s + 256]
                        nc.vector.tensor_tensor_reduce(out=s_nsa[:, u, s, lo:lo + n], in0=src, in1=bias_t[:, u, lo:lo + n],
                                                       scale=1.0, scalar=FAR_BELOW, op0=ALU.add, op1=ALU.max,
                                                       accum_out=sml[:, t, i:i + 1]).then_inc(biased, 1)
                dve.wait_ge(biased, 4 * HEADS + 8 * t + 4 * u + 4)
                nc.vector.tensor_scalar(sml[:, t, 8 + 4 * u:12 + 4 * u], sml[:, t, 4 * u:4 * u + 4], -SCALE, None, ALU.mult)\
                    .then_inc(max_made, 1)

            def combine(t):
                s = sml[:, t, :]
                dve.wait_ge(exp_made, 4 * HEADS + 8 * t + 8)
                then(nc.vector.reciprocal(s[:, 24:32], s[:, 16:24]))
                for u in range(2):
                    g = gate_sb[:, :].rearrange("p (q s h) -> p q s h", q=2, s=3)[:, :, 1:3, 2 * t + u]
                    last = nc.vector.tensor_tensor(s[:, 32 + 4 * u:36 + 4 * u].rearrange("p (q s) -> p q s", q=2),
                                                   s[:, 24 + 4 * u:28 + 4 * u].rearrange("p (q s) -> p q s", q=2), g, ALU.mult)
                then(last)
                dve.wait_ge(pv_done, HEADS + t + 1)
                nc.vector.tensor_tensor(og[:, :, :], bank(3).rearrange("p (i d) -> p i d", i=8),
                                        s[:, 32:40].unsqueeze(2).broadcast_to([P, 8, 64]), ALU.mult).then_inc(o_made, 1)
                dve.wait_ge(o_made, HEADS + t + 1)
                o4 = og[:, :, :].rearrange("p (u q s) d -> p u q s d", u=2, q=2)
                for q in range(QT):
                    last = nc.vector.tensor_tensor(xn[:, q, P * t:P * t + P].rearrange("p (u d) -> p u d", u=2),
                                                   o4[:, :, q, 0, :], o4[:, :, q, 1, :], ALU.add)
                then(last)

            for t in range(TILES + 1):
                if t < TILES:
                    nsa_bias_max(t, 0)
                if t == 0:
                    dve.wait_ge(w2_done, 1)
                    for u in range(2):
                        rows = slice(64 * u, 64 * u + 64)
                        nc.vector.tensor_copy(kcT[rows, :, :],
                                              bank(3)[rows, 128:192].rearrange("p (g u n) -> p g u n", g=2, u=2)[:, :, u, :])
                    nc.vector.tensor_copy(vrep[:, :], bank(3)[:, 192:448]).then_inc(cmp_evac, 1)
                step_mod(1, t, 6)
                step_modcol(1, t, 6)
                if t == 1:
                    split_col(C_Q + 3)
                elif t in (3, 5):
                    split_row(R_OUT[1] + (t - 3) // 2)
                if t < TILES:
                    nsa_bias_max(t, 1)
                if t >= 1:
                    dve.wait_ge(at_done, HEADS + 2 * (t - 1) + 2)
                    if t >= 2:
                        dve.wait_ge(pv_done, HEADS + t - 1)
                    nc.vector.tensor_copy(at_nsa[:, 1, :, :], bank(1, 2).rearrange("p (s n) -> p s n", s=2)[:, :, 0:384])\
                        .then_inc(at_dve, 1)
                    combine(t - 1)
            make_fold(3, 9, 10, 8)

            dve.wait_ge(c_scored, 1)
            for u in range(2):
                last = nc.vector.tensor_tensor(sc[:, 256 * u:256 * u + 256], bank(4 + u)[:, 0:256], dist_c[:, 256 * u:256 * u + 256], ALU.add)
            then(last)
            s3 = sc.rearrange("p (h n) -> p h n", n=16)
            then(nc.vector.tensor_reduce(smc[:, 0, :], s3, op=ALU.max, axis=AX.X))
            nc.vector.tensor_tensor(s3, s3, smc[:, 0, :].unsqueeze(2).broadcast_to([P, 32, 16]), ALU.subtract).then_inc(c_biased, 1)
            dve.wait_ge(pv_done, HEADS + TILES)
            for gp in range(2):
                nc.vector.tensor_tensor(vcp[:, gp, :].rearrange("p (i u d) -> p i u d", i=4, u=2),
                                        vrep[:, 128 * gp:128 * gp + 128].rearrange("p (u d) -> p u d", u=2).unsqueeze(1).broadcast_to([P, 4, 2, 64]),
                                        own_block.rearrange("p (i u) -> p i u", i=4).unsqueeze(3).broadcast_to([P, 4, 2, 64]),
                                        ALU.mult).then_inc(vcp_made, 1)
            dve.wait_ge(c_exp, 1)
            then(nc.vector.tensor_reduce(smc[:, 1, :], s3, op=ALU.add, axis=AX.X))
            then(nc.vector.reciprocal(smc[:, 2, :], smc[:, 1, :]))
            for u in range(2):
                for q in range(QT):
                    o = 16 * u + 8 * q
                    g = gate_sb[:, 48 * q:48 * q + 16].rearrange("p (t u) -> p t u", u=2)[:, :, u]
                    last = nc.vector.tensor_tensor(smc[:, 3, o:o + 8], smc[:, 2, o:o + 8], g, ALU.mult)
            then(nc.vector.scalar_tensor_tensor(sc, dist_c, -1.0e29, sc, ALU.is_gt, ALU.mult))
            for u in range(2):
                last = nc.vector.tensor_tensor(
                    pc.rearrange("p (h u n) -> p h u n", u=2, n=16)[:, :, u, :], s3[:, 16 * u:16 * u + 16, :],
                    smc[:, 3, 16 * u:16 * u + 16].unsqueeze(2).broadcast_to([P, 16, 16]), ALU.mult)
            last.then_inc(c_made, 1)
            for gp in range(2):
                for q in range(QT):
                    i = 2 * gp + q
                    dve.wait_ge(c_out, i + 1)
                    o = xn[:, q, 512 * gp:512 * gp + 512]
                    nc.vector.tensor_tensor(o, bank(i), o, ALU.add).then_inc(c_added, 1)

            def nsa_out_lo(r):
                dve.wait_ge(o_hi_made, HEADS + r + 1)
                nc.vector.tensor_tensor(o_lo[:, 2 * r:2 * r + 2, :].rearrange("p t n -> p (t n)"), bank(r),
                                        o_hi[:, 2 * r:2 * r + 2, :].rearrange("p t n -> p (t n)").bitcast(F32), ALU.subtract)\
                    .then_inc(o_lo_made, 1)

            nsa_out_lo(0)
            nsa_out_lo(1)
            split_row(R_OUT[1] + 2)
            nsa_out_lo(2)
            split_row(R_OUT[1] + 3)
            nsa_out_lo(3)
            for c in range(4, 8):
                split_row(R_OUT[1] + c)
            split_col(C_FFN[1])
            split_col(C_FFN[1] + 1)
            norm(2, 4)
            input_tiles(3)
            ffn(1)
            norm(3, 0)
            dve.wait_ge(lnrow_in, 64)
            for q in range(QT):
                dve.wait_ge(xn_made, 6 + q + 1)
                then(nc.vector.tensor_tensor(xn[:, q, :], xn[:, q, :], kv_sb[:, 0:D], ALU.mult))
                nc.vector.tensor_tensor(x_sb[:, q, :], xn[:, q, :], kv_sb[:, D:2 * D], ALU.add).then_inc(x_updated, 1)

        @block.gpsimd
        def _(pool):
            own = [0]

            def then(ins):
                own[0] += 1
                ins.then_inc(pool_done, 1)
                pool.wait_ge(pool_done, own[0])

            pool.dma_start(lam_sb.rearrange("p a n -> p (a n)"), lam[0, :].partition_broadcast(P)).then_inc(small_in, 16)
            pool.dma_start(subln_sb, subln[0, :].partition_broadcast(P)).then_inc(small_in, 16)
            pool.dma_start(gate_wsb[:, :, :], gate_w).then_inc(small_in, 16)
            pool.dma_start(pos_sb[:, :, :], pos).then_inc(small_in, 16)
            pool.dma_start(w2_sb[:, :], w2).then_inc(small_in, 16)
            nc.gpsimd.memset(zeros[:, :].bitcast(F32), 0.0).then_inc(zero_ready, 1)
            then(nc.gpsimd.memset(half[:, :], -0.5))
            pool.wait_ge(consts_in, 16)

            def bias(slot, slope, n):
                nc.gpsimd.tensor_scalar(bias_t[:, slot, :], dist, slope / SCALE, 1.0, ALU.mult, ALU.mult).then_inc(bias_ready, 1)

            def rstd(dst, src):
                return nc.gpsimd.tensor_tensor(dst, src, half[:, :].broadcast_to([P, dst.shape[1]]), ALU.pow)

            def row_rstd(h):
                pool.wait_ge(ms_made, h + 1)
                rstd(sml[:, h, 22:24], sml[:, h, 20:22]).then_inc(rstd_made, 1)

            for h in range(HEADS):
                if h >= 2:
                    pool.wait_ge(biased, 4 * (h - 1))
                bias(h % 2, 2.0 ** -(h + 1), h)
                if h >= 3:
                    row_rstd(h - 3)
            for h in range(HEADS - 3, HEADS):
                row_rstd(h)

            def norm(n, update):
                for q in range(QT):
                    pool.wait_ge(var_made, 2 * n + q + 1)
                    rstd(stats[:, q, 15:16], stats[:, q, 14:15]).then_inc(ln_rstd, 1)
                if update:
                    pool.wait_ge(lnrow_in, 16 * (n + 1))
                    for q in range(QT):
                        pool.wait_ge(xn_made, 2 * n + q + 1)
                        nc.gpsimd.tensor_tensor(x_sb[:, q, :], xn[:, q, :], kv_sb[:, 0:D], ALU.mult).then_inc(x_scaled, 1)
                        pool.wait_ge(x_scaled, 2 * n + q + 1)
                        nc.gpsimd.tensor_tensor(x_sb[:, q, :], x_sb[:, q, :], kv_sb[:, D:2 * D], ALU.add).then_inc(x_updated, 1)

            norm(0, True)
            norm(1, True)
            pool.wait_ge(kv_evac, 2)
            pool.dma_start(kvs[64:128, :, :, :].rearrange("p v g n -> p (v g n)"), kvc[0:64, :, :, :].rearrange("p v g n -> p (v g n)")).then_inc(swapped, 16)
            pool.dma_start(kvs[0:64, :, :, :].rearrange("p v g n -> p (v g n)"), kvc[64:128, :, :, :].rearrange("p v g n -> p (v g n)")).then_inc(swapped, 16)
            for t in range(TILES):
                for u in range(2):
                    if t >= 1:
                        pool.wait_ge(biased, 4 * HEADS + 8 * (t - 1) + 4 * u + 4)
                    else:
                        pool.wait_ge(biased, 4 * HEADS)
                    head = 4 * (2 * (t // 4) + u) + t % 4
                    bias(u, 2.0 ** (-0.5 * (head + 1)), t)
            norm(2, True)
            norm(3, False)


def kernel(x, c, diff_w_in, diff_w_out, diff_lam_q1, diff_lam_k1, diff_lam_q2, diff_lam_k2, diff_subln_g,
           nsa_w_in, nsa_cmp_pos_k, nsa_cmp_pos_v, nsa_cmp_k_w1, nsa_cmp_k_w2, nsa_cmp_v_w1, nsa_cmp_v_w2,
           nsa_w_out, ada_w, ada_b, ln_mix_g, ln_mix_b, ln_ffn_g, ln_ffn_b, ffn_w_gu, ffn_w_down):
    import numpy as np
    import concourse.bacc as bacc
    from concourse.bass_utils import run_bass_kernel_spmd

    def arr(a):
        return np.asarray(a)

    def pairs(w, blocks):
        cols = np.concatenate([w[:, a:a + n] for a, n in blocks], axis=1)
        return cols.reshape(KT, P, 256).transpose(1, 0, 2).reshape(P, KT * 256)

    def column(v):
        return v.reshape(-1, P).T

    w_in, w_nsa = arr(diff_w_in)[0], arr(nsa_w_in)[0]
    gu, dn = arr(ffn_w_gu), arr(ffn_w_down)
    heads = [(8 * (t // 4) + t % 4, 8 * (t // 4) + 4 + t % 4) for t in range(TILES)]
    flat_heads = [h for pair in heads for h in pair]
    col_chunks = [pairs(w_in, [(P * h, P), (D + P * h, P)]) for h in range(HEADS)]
    col_chunks += [pairs(gu[0], [(P * j, P), (HID + P * j, P)]) for j in range(HT)]
    col_chunks += [pairs(w_nsa, [(o, 256)]) for o in (1024, 1280, 1536, 2048, 1792, 2304)]
    for w1 in (nsa_cmp_k_w1, nsa_cmp_v_w1):
        col_chunks.append(arr(w1)[0].reshape(16, P, P).transpose(1, 0, 2).reshape(P, 2048))
    for i in range(4):
        a, b, e, f = heads[2 * i] + heads[2 * i + 1]
        col_chunks.append(pairs(w_nsa, [(64 * a, 64), (64 * b, 64), (64 * e, 64), (64 * f, 64)]))
    col_chunks += [pairs(gu[1], [(P * j, P), (HID + P * j, P)]) for j in range(HT)]
    w_o = np.concatenate([arr(nsa_w_out)[0][64 * h:64 * h + 64] for h in flat_heads], axis=0)
    row_chunks = np.concatenate([w_in[:, 2 * D:3 * D], arr(diff_w_out)[0], dn[0], w_o, dn[1]], axis=0).reshape(N_ROW, P, D)
    ada = arr(ada_w).reshape(2, KT, P, 6, D).transpose(0, 3, 1, 2, 4).reshape(96, P, D)
    ada_bias = np.repeat(arr(ada_b).reshape(12, 4, 256), 32, axis=1)
    norms = [(arr(g)[i], arr(b)[i]) for i in range(2) for g, b in ((ln_mix_g, ln_mix_b), (ln_ffn_g, ln_ffn_b))]
    cols = np.stack([column(arr(c)[0])] + [column(v) for pair in norms for v in pair], axis=1)
    xs = arr(x)[0]
    gate_cols = [2560 + 3 * h + s for s in range(3) for h in flat_heads]
    gate_w = np.stack([w_nsa[:, i] for i in gate_cols], axis=1).reshape(KT, P, 48).transpose(1, 0, 2)
    pos = np.stack([arr(p)[0].reshape(16, P).T for p in (nsa_cmp_pos_k, nsa_cmp_pos_v)], axis=1)
    k2, v2 = arr(nsa_cmp_k_w2)[0], arr(nsa_cmp_v_w2)[0]
    w2 = np.concatenate([k2, k2, v2], axis=1)
    lam = np.concatenate([arr(v) for v in (diff_lam_q1, diff_lam_k1, diff_lam_q2, diff_lam_k2)], axis=1)
    ln_rows = np.stack([np.concatenate(pair) for pair in norms])

    p = np.arange(P)

    def masked(d):
        return np.where(d >= 0, -d, -1e30)

    dist = np.concatenate([masked(p[:, None] - p[None, :]), masked(P + p[:, None] - np.arange(T)[None, :])], axis=1)
    dist_c = np.full((P, 2, QT, TILES, 16), -1e30)
    for u in range(2):
        for q in range(QT):
            for t in range(TILES):
                d = (P * q + p)[:, None] - (16 * np.arange(N_CMP) + 31)[None, :]
                slope = 2.0 ** (-0.5 * (heads[t][u] + 1)) / SCALE
                dist_c[:, u, q, t, :N_CMP] = np.where(d >= 0, -d * slope, -1e30)
    own = (p[:, None] // 16 == np.arange(8)[None, :]) * 1.0
    consts = np.concatenate([np.eye(P), dist, dist_c.reshape(P, 512), own], axis=1).astype(np.float32)

    arrays = {
        "col_w": np.stack(col_chunks), "row_w": row_chunks, "ada": ada, "ada_bias": ada_bias, "cols": cols,
        "xT": xs.T.reshape(KT, P, T).transpose(1, 0, 2), "x_nat": xs.reshape(QT, P, D).transpose(1, 0, 2),
        "ln_rows": ln_rows, "lam": lam, "subln": arr(diff_subln_g), "gate_w": gate_w, "pos": pos, "w2": w2, "consts": consts,
    }
    arrays = {f"in_{n}": np.ascontiguousarray(a) for n, a in arrays.items()}
    nc = bacc.Bacc("TRN2", target_bir_lowering=False, num_devices=1)
    args = [nc.dram_tensor(n, a.shape, mybir.dt.from_np(a.dtype), kind="ExternalInput").ap() for n, a in arrays.items()]
    args.append(nc.dram_tensor("out_x", (QT, P, D), F32, kind="ExternalOutput").ap())
    decoder(nc, *args)
    r = run_bass_kernel_spmd(nc, [arrays], core_ids=[0])
    return r.results[0]["out_x"].reshape(1, T, D)
```

```python
from contextlib import ExitStack

import concourse.bass as bass
from concourse import mybir

F32 = mybir.dt.float32
F32R = mybir.dt.float32r
ALU = mybir.AluOpType
ACT = mybir.ActivationFunctionType
AX = mybir.AxisListType

P = 128
D = 1024
T = 256
KT = D // P
QT = T // P
HID = 2816
HT = HID // P
HEADS = 8
TILES = 8
N_CMP = 15
BANK = 512
ALPHA = 4.0 ** 0.25
LN_EPS = 1e-5
RMS_EPS = 1e-5
SCALE = 0.125
LAM_INIT = 0.8 - 0.6
FAR_BELOW = -3.0e38

C_HEAD = 0
C_FFN = (8, 40)
C_NSA = 30
C_Q = 36
N_COL = 62
R_V, R_OUT, R_DOWN = 0, (8, 38), (16, 46)
N_ROW = 68
SIDE_W1 = 72
COL_RING, ROW_RING, SIDE_RING = 3, 3, 4
COL_SPLIT, ROW_SPLIT = 2, 3
FFN_SLOTS = 6
LOOP_TILES = 6
GROUP_BESIDE_NORM = {0: 6, 1: 8, 2: 11}
LAST = 3


def side(e):
    return 8 * e if 8 * e < SIDE_W1 else 8 * e + 4


def decoder(nc, col_w, row_w, side_w, ada_bias, cols, xT, x_nat, ln_rows, lam, subln, gate_w, pos, w2, consts, out):
    ctx = ExitStack()
    with ctx:
        def sb(name, shape, dt=F32):
            return ctx.enter_context(nc.sbuf_tensor(name, shape, dt))

        def sem(name):
            return ctx.enter_context(nc.semaphore(name))

        col_raw = sb("col_raw", [P, COL_RING, KT * 256])
        row_raw = sb("row_raw", [P, ROW_RING, D])
        col_hi = sb("col_hi", [P, COL_SPLIT, KT * 256], F32R)
        col_lo = sb("col_lo", [P, COL_SPLIT, KT * 256], F32R)
        row_hi = sb("row_hi", [P, ROW_SPLIT, D], F32R)
        row_lo = sb("row_lo", [P, ROW_SPLIT, D], F32R)
        side_raw = sb("side_raw", [P, SIDE_RING, D])
        x_sb = sb("x_sb", [P, QT, D])
        xn = sb("xn", [P, QT, D])
        h_f = sb("h_f", [P, KT, T])
        h_hi = sb("h_hi", [P, KT, T], F32R)
        h_lo = sb("h_lo", [P, KT, T], F32R)
        o_hi = sb("o_hi", [P, KT, T], F32R)
        o_lo = sb("o_lo", [P, KT, T], F32R)
        kv_sb = sb("kv_sb", [P, 2 * D])
        scratch = sb("scratch", [P, 3072])
        bias_t = sb("bias_t", [P, 2, 384])
        modrow = sb("modrow", [P, 3, 256])
        bias_rows = sb("bias_rows", [P, 2, 256])
        consts_sb = sb("consts_sb", [P, 128 + 384 + 512 + 2])
        cols_sb = sb("cols_sb", [P, 9, KT])
        c_rep = sb("c_rep", [P, KT, 32])
        zeros = sb("zeros", [P, P], F32R)
        modcol = sb("modcol", [P, 12, KT])
        fold = sb("fold", [P, 4, 2, KT])
        gate_sb = sb("gate_sb", [P, QT * 48])
        gate_wsb = sb("gate_wsb", [P, KT, 48])
        pos_sb = sb("pos_sb", [P, 2, 16])
        w2_sb = sb("w2_sb", [P, 192])
        gel = sb("gel", [P, 2, 4, 16])
        kcb = sb("kcb", [P, 2, 2, 16])
        sc = sb("sc", [P, 512])
        sml = sb("sml", [P, 8, 40])
        stats = sb("stats", [P, QT, 20])
        silu_sb8 = sb("silu_c_cols", [P, KT])
        lam_t = sb("lam_t", [P, 5])
        lam_sums, lam_exps, neg_lam = lam_t[:, 0:2], lam_t[:, 2:4], lam_t[:, 4:5]
        half = sb("half", [P, 1])
        og = sb("og", [P, 8, 64])

        ident = consts_sb[:, 0:128]
        dist = consts_sb[:, 128:512]
        dist_c = consts_sb[:, 512:1024]
        own_half = consts_sb[:, 1024:1026]
        gate_row = scratch[:, 0:1024]
        silu_sb = scratch[:, 1024:1536].rearrange("p (s n) -> p s n", s=2)
        hid_sb = scratch[:, 1536:2048].rearrange("p (s n) -> p s n", s=2)
        v_sb = xn
        lam_sb, subln_sb = og[:, 4:8, :], og[:, 2:4, :].rearrange("p a n -> p (a n)")
        gel_rep = og[:, :, :].rearrange("p a n -> p (a n)").rearrange("p (g n) -> p g n", g=4)
        gate_flat = gate_wsb[:, :, :].rearrange("p k n -> p (k n)")
        vcb = gate_flat[:, 0:256].rearrange("p (g n) -> p g n", g=2)
        smc = gate_flat[:, 256:384].rearrange("p (a n) -> p a n", a=4)
        s_diff = scratch[:, 0:1536].rearrange("p (s c n) -> p s c n", s=2, c=2)
        at_diff = scratch[:, 1536:2304].rearrange("p (s n) -> p s n", s=2)
        o_diff = scratch[:, 2304:2560].rearrange("p (q n) -> p q n", q=2)
        sq_junk = scratch[:, 2560:3072].rearrange("p (s q n) -> p s q n", s=2, q=2)
        q_all = h_f
        kk = kv_sb[:, 0:1024].rearrange("p (b g n) -> p b g n", b=2, g=2)
        vv = kv_sb[:, 1024:2048].rearrange("p (b q n) -> p b q n", b=2, q=2)
        s_nsa = scratch[:, 0:1536].rearrange("p (u b n) -> p u b n", u=2, b=2)
        at_nsa = scratch[:, 1536:3072].rearrange("p (u b n) -> p u b n", u=2, b=2)
        kvc = scratch[:, 0:1024].rearrange("p (v g n) -> p v g n", v=2, g=2)
        kvs = scratch[:, 1024:2048].rearrange("p (v g n) -> p v g n", v=2, g=2)
        blk = xn[:, :, :].rearrange("p q n -> p (q n)")[:, 0:1920]

        psum = ctx.enter_context(nc.psum_tensor("psum", [P, 8 * BANK], F32))

        def bank(i, n=1):
            return psum[:, i * BANK:(i + n) * BANK]

        col_loaded = [sem(f"col_loaded{i}") for i in range(COL_RING)]
        row_loaded = [sem(f"row_loaded{i}") for i in range(ROW_RING)]
        side_loaded = [sem(f"side_loaded{i}") for i in range(SIDE_RING)]
        bias_loaded = [sem(f"bias_loaded{i}") for i in range(2)]
        cols_in, xT_in, x_in, consts_in, lnrow_in = (sem(n) for n in ("cols_in", "xT_in", "x_in", "consts_in", "lnrow_in"))
        small_in, masks_in, nsa_small_in = sem("small_in"), sem("masks_in"), sem("nsa_small_in")
        c_ready, zero_ready = sem("c_ready"), sem("zero_ready")
        silu_c = sem("silu_c")
        col_hi_made, col_lo_made, col_used = sem("col_hi_made"), sem("col_lo_made"), sem("col_used")
        row_hi_made, row_lo_made, row_used = sem("row_hi_made"), sem("row_lo_made"), sem("row_used")
        side_used, modrow_made, modT_done, modcol_made = (sem(n) for n in ("side_used", "modrow_made", "modT_done", "modcol_made"))
        gate_spread, gate_made = sem("gate_spread"), sem("gate_made")
        fold_made = sem("fold_made")
        aff_dve, aff_act, h_hi_made, h_made = (sem(n) for n in ("aff_dve", "aff_act", "h_hi_made", "h_made"))
        v_act, v_dve = sem("v_act"), sem("v_dve")
        lam_ready, lam_sum, lam_exp = sem("lam_ready"), sem("lam_sum"), sem("lam_exp")
        qk_made, scored, biased, bias_ready, max_made, exp_made, mixed = (
            sem(n) for n in ("qk_made", "scored", "biased", "bias_ready", "max_made", "exp_made", "mixed"))
        at_done, at_act, pv_done, squared, ms_made, rstd_made, o_made, ot_done, o_hi_made, o_lo_made = (
            sem(n) for n in ("at_done", "at_act", "pv_done", "squared", "ms_made", "rstd_made", "o_made",
                             "ot_done", "o_hi_made", "o_lo_made"))
        y_done, y_read, z_made, var_made, ln_rstd, shift_made, rows0_made, rows1_made, rows1_end_made, xt_done, x_updated, x_scaled = (
            sem(n) for n in ("y_done", "y_read", "z_made", "var_made", "ln_rstd", "shift_made", "rows0_made", "rows1_made", "rows1_end_made", "xt_done", "x_updated", "x_scaled"))
        silu_made, hid_made, act_hi_made, act_lo_made = (sem(n) for n in ("silu_made", "hid_made", "act_hi_made", "act_lo_made"))
        gates_done, gates_exp, gates_made = sem("gates_done"), sem("gates_exp"), sem("gates_made")
        kv_evac, swapped, blk_made = sem("kv_evac"), sem("swapped"), sem("blk_made")
        last_rows = sem("last_rows")
        cmp_zeroed, gelu_made, gel_spread, w2_done, cmp_evac = (
            sem(n) for n in ("cmp_zeroed", "gelu_made", "gel_spread", "w2_done", "cmp_evac"))
        c_scored, c_biased, c_exp, c_made, c_tr, c_evac = (
            sem(n) for n in ("c_scored", "c_biased", "c_exp", "c_made", "c_tr", "c_evac"))
        p_scaled = sem("p_scaled")
        first_scored = sem("first_scored")
        dve_done = sem("dve_done")
        pool_done = sem("pool_done")
        out_stored = sem("out_stored")

        def at(base, b):
            return base if b is None else b * LOOP_TILES + base

        def loads(c, ring, b):
            n = 16 * (c // ring + 1)
            return n if b is None else b * (16 * LOOP_TILES // ring) + n

        head_groups = []
        for n in (3, 3, 2, 3, 3, 2, 4, 4):
            first = side(2) if not head_groups else head_groups[-1][-1] + 1
            head_groups.append(range(first, first + n))

        block = ctx.enter_context(nc.Block())

        @block.sync
        def _(sp):
            def load_col(c, b=None):
                if c >= COL_RING:
                    sp.wait_ge(col_lo_made, at(c - COL_RING + 1, b))
                src = col_w[c, :, :] if b is None else \
                    col_w[bass.ds(b * LOOP_TILES + c, 1), :, :].rearrange("a p n -> p (a n)")
                sp.dma_start(col_raw[:, c % COL_RING, :], src).then_inc(col_loaded[c % COL_RING], 16)

            def load_row(c, b=None):
                if c >= ROW_RING:
                    sp.wait_ge(row_lo_made, at(c - ROW_RING + 1, b))
                src = row_w[c, :, :] if b is None else \
                    row_w[bass.ds(b * LOOP_TILES + c, 1), :, :].rearrange("a p n -> p (a n)")
                sp.dma_start(row_raw[:, c % ROW_RING, :], src).then_inc(row_loaded[c % ROW_RING], 16)

            def load_side(*chunks):
                for c in chunks:
                    for e in range(12):
                        if c == side(e):
                            if e >= 2:
                                sp.wait_ge(modrow_made, e - 1)
                            sp.dma_start(bias_rows[:, e % 2, :], ada_bias[e, :, :]).then_inc(bias_loaded[e % 2], 16)
                    if c >= SIDE_RING:
                        sp.wait_ge(side_used, c - SIDE_RING + 1)
                    sp.dma_start(side_raw[:, c % SIDE_RING, :], side_w[c, :, :]).then_inc(side_loaded[c % SIDE_RING], 16)

            def load_ln_rows(n):
                sp.dma_start(kv_sb[:, :], ln_rows[n, :].partition_broadcast(P)).then_inc(lnrow_in, 16)

            load_side(*range(12))
            load_row(R_V)
            load_side(12, 13)
            load_row(R_V + 1)
            load_side(14, 15)
            for c in (2, 3, 4, 5, 6, 7):
                load_row(R_V + c)
                if c in (4, 6):
                    load_col(C_HEAD + c // 2 - 2)
            sp.dma_start(consts_sb[:, P:], consts[:, P:]).then_inc(masks_in, 16)
            sp.dma_start(gate_wsb[:, :, :], gate_w).then_inc(nsa_small_in, 16)
            sp.dma_start(pos_sb[:, :, :], pos).then_inc(nsa_small_in, 16)
            sp.dma_start(w2_sb[:, :], w2).then_inc(nsa_small_in, 16)
            sp.dma_start(x_sb[:, :, :], x_nat).then_inc(x_in, 16)
            for h in range(HEADS):
                load_col(C_HEAD + h + 2)
                if h in (2, 3, 4):
                    load_row(R_OUT[0] + h - 2)
                load_side(*head_groups[h])
            load_side(*range(side(5), side(5) + 2))
            load_row(R_OUT[0] + 3)
            load_side(*range(side(5) + 2, side(5) + 4))

            def ffn_loads(layer, i, b=None):
                c0, r0 = C_FFN[layer], R_DOWN[layer]
                load_row(r0 + 2 * i - 2, b)
                load_row(r0 + 2 * i - 1, b)
                load_col(c0 + 2 * i + 2, b)
                load_col(c0 + 2 * i + 3, b)

            for layer in range(2):
                c0, r0 = C_FFN[layer], R_DOWN[layer]
                load_row(R_OUT[layer] + 4)
                if layer == 0:
                    load_side(*range(side(5) + 4, side(5) + 6))
                load_row(R_OUT[layer] + 5)
                if layer == 0:
                    load_side(*range(side(5) + 6, side(5) + 8))
                if layer == 0:
                    sp.wait_ge(scored, HEADS)
                else:
                    sp.wait_ge(pv_done, HEADS + TILES)
                load_ln_rows(2 * layer)
                load_row(R_OUT[layer] + 6)
                load_row(R_OUT[layer] + 7)
                load_col(c0 + 2)
                load_side(*range(side(GROUP_BESIDE_NORM[2 * layer]), side(GROUP_BESIDE_NORM[2 * layer]) + 4))
                load_row(r0)
                load_row(r0 + 1)
                load_side(*range(side(GROUP_BESIDE_NORM[2 * layer]) + 4, side(GROUP_BESIDE_NORM[2 * layer]) + 8))
                load_col(c0 + 3)
                with sp.Fori(0, 3) as b:
                    for i in (1, 2, 3):
                        load_col(c0 + 2 * i + 2, b)
                        load_row(r0 + 2 * i, b)
                        load_row(r0 + 2 * i + 1, b)
                        load_col(c0 + 2 * i + 3, b)
                load_row(r0 + 20)
                sp.wait_ge(x_updated, 4 * layer + 2)
                load_ln_rows(2 * layer + 1)
                if layer == 0:
                    load_side(*range(side(7), side(7) + 4))
                    load_col(C_NSA)
                load_row(r0 + 21)
                if layer == 0:
                    load_side(*range(side(7) + 4, side(7) + 8))
                    load_col(C_NSA + 1)
                    load_side(*range(side(8), side(8) + 4))
                    load_col(C_NSA + 2)
                    load_side(*range(side(8) + 4, side(8) + 8))
                    for c in range(C_NSA + 3, C_NSA + 6):
                        load_col(c)
                    load_side(*range(SIDE_W1, SIDE_W1 + 4))
                    for i in range(3):
                        load_row(R_OUT[1] + i)
                    for i in range(4):
                        load_col(C_Q + i)
                    load_side(*range(side(9), side(9) + 4))
                    load_col(C_FFN[1])
                    load_col(C_FFN[1] + 1)
                    load_row(R_OUT[1] + 3)
                    load_side(*range(side(9) + 4, side(10) + 8))
            sp.wait_ge(last_rows, 1)
            sp.wait_ge(x_updated, 7)
            sp.dma_start(out[0, :, :], x_sb[:, 0, :]).then_inc(out_stored, 16)
            for i, cols in enumerate((slice(0, BANK), slice(BANK, D))):
                sp.wait_ge(last_rows, 2 + i)
                sp.dma_start(out[1, :, cols], x_sb[:, 1, cols]).then_inc(out_stored, 16)
            sp.wait_ge(out_stored, 48)

        @block.tensor
        def _(pe):
            def three(dst, sh, sl, mh, ml, start, stop, **kw):
                nc.tensor.matmul(dst, sh, mh, start=start, stop=False, **kw)
                nc.tensor.matmul(dst, sh, ml, start=False, stop=False, **kw)
                return nc.tensor.matmul(dst, sl, mh, start=False, stop=stop, **kw)

            def col_views(c):
                return (col_hi[:, c % COL_SPLIT, :].rearrange("p (k n) -> p k n", k=KT),
                        col_lo[:, c % COL_SPLIT, :].rearrange("p (k n) -> p k n", k=KT))

            def col_product(c, dst, b=None, stage=None):
                pe.wait_ge(col_lo_made, at(c + 1, b))
                wh, wl = col_views(c)
                order = [(i, k) for i in range(2) for k in range(KT)]
                if stage is not None:
                    order = [(i, k) for k in range(KT) for i in range(2)]
                for i, k in order:
                    if stage is not None and i == 0:
                        pe.wait_ge(h_made, 8 * stage + k + 1)
                    last = three(dst[:, 256 * i:256 * i + 256], wh[:, k, 128 * i:128 * i + 128],
                                 wl[:, k, 128 * i:128 * i + 128], h_hi[:, k, :], h_lo[:, k, :],
                                 k == 0 and (stage is None or i == 0), k == KT - 1, skip_group_check=stage is not None)
                last.then_inc(col_used, 1)

            def col_product_natural(c, dst):
                pe.wait_ge(col_lo_made, c + 1)
                wh, wl = col_views(c)
                for q in range(QT):
                    for k in range(KT):
                        last = three(dst[:, 256 * q:256 * q + 256], h_hi[:, k, 128 * q:128 * q + 128],
                                     h_lo[:, k, 128 * q:128 * q + 128], wh[:, k, :], wl[:, k, :], k == 0, k == KT - 1)
                last.then_inc(col_used, 1)

            def row_tile(c, q, j, sh, sl, y0, start, stop, **kw):
                cols = slice(BANK * j, BANK * j + BANK)
                return three(bank(y0 + 2 * q + j), sh[:, 128 * q:128 * q + 128], sl[:, 128 * q:128 * q + 128],
                             row_hi[:, c % ROW_SPLIT, cols], row_lo[:, c % ROW_SPLIT, cols], start, stop, **kw)

            def row_product(c, sh, sl, y0, start, stop, b=None, **kw):
                pe.wait_ge(row_lo_made, at(c + 1, b))
                for q in range(QT):
                    for j in range(2):
                        last = row_tile(c, q, j, sh, sl, y0, start, stop, **kw)
                last.then_inc(row_used, 1)

            def last_row_products(chunks, slots, y0, ready, first_ready, **kw):
                for q in range(QT):
                    for j in range(2):
                        for n, c in enumerate(chunks):
                            if q == 0 and j == 0:
                                pe.wait_ge(row_lo_made, c + 1)
                                pe.wait_ge(ready, first_ready + n)
                            last = row_tile(c, q, j, o_hi[:, slots[n], :], o_lo[:, slots[n], :], y0, False,
                                            n == len(chunks) - 1, **kw)
                        if q == 0 or j == 0:
                            last.then_inc(y_done, 1)
                        else:
                            last.then_inc(row_used, len(chunks))

            def ada_chunk(e, k, dst):
                c = side(e) + k
                pe.wait_ge(side_loaded[c % SIDE_RING], 16 * (c // SIDE_RING + 1))
                for j in range(4):
                    last = nc.tensor.matmul(dst[32 * j:32 * j + 32, :], c_rep[:, k, :],
                                            side_raw[:, c % SIDE_RING, 256 * j:256 * j + 256],
                                            start=(k == 0), stop=(k == 7), tile_position=(0, 32 * j))
                last.then_inc(side_used, 1)

            def mod_transpose(slot, dst):
                for i in range(2):
                    last = nc.tensor.matmul(dst[:, 4 * i:4 * i + 4], modrow[:, slot, 128 * i:128 * i + 128],
                                            ident[:, 0:P:32], start=True, stop=True)
                last.then_inc(modT_done, 1)

            def gate_part(slot, dst, r):
                for i in range(2):
                    j = 2 * r + i
                    last = nc.tensor.matmul(dst[:, 256 * i:256 * i + 256], ident[:, 32 * j:32 * j + 1].broadcast_to([P, P]),
                                            modrow[:, slot, :], start=True, stop=True)
                last.then_inc(gate_spread, 1)

            pe.wait_ge(c_ready, 1)
            for k in range(8):
                ada_chunk(0, k, bank(0)[:, 0:256])
            for k in range(8):
                ada_chunk(1, k, bank(1)[:, 0:256])
            pe.wait_ge(consts_in, 16)
            pe.wait_ge(modrow_made, 1)
            mod_transpose(0, bank(2))
            pe.wait_ge(modrow_made, 2)
            mod_transpose(1, bank(3))

            for k in range(KT):
                pe.wait_ge(h_made, k + 1)
                if k == 0:
                    pe.wait_ge(modcol_made, 2)
                row_product(R_V + k, h_hi[:, k, :], h_lo[:, k, :], 0, k == 0, k == KT - 1)

            def project(h):
                if h >= 2:
                    pe.wait_ge(qk_made, h - 1)
                col_product(C_HEAD + h, bank(4 + h % 2))

            def score(h):
                pe.wait_ge(qk_made, h + 1)
                if h >= 1:
                    pe.wait_ge(biased, 4 * h)
                qk = qk_diff[:, h % 2, :]
                for q, lo, n in ((0, 0, 128), (1, 128, 256)):
                    for c in range(2):
                        rows = slice(64 * c, 64 * c + 64)
                        last = nc.tensor.matmul(bank(6 + c)[:, lo:lo + n], qk[rows, 128 * q:128 * q + 128],
                                                qk[rows, 256:256 + n], start=True, stop=True)
                last.then_inc(scored, 1)

            def transpose_probs(h):
                if h >= 1:
                    pe.wait_ge(at_act, h)
                if h in (5, 7):
                    pe.wait_ge(modrow_made, 4 if h == 5 else 5)
                    mod_transpose(0, bank(2)[:, 384:392])
                if h == 6:
                    pe.wait_ge(modcol_made, 3)
                pe.wait_ge(mixed, h + 1)
                for i in range(3):
                    last = nc.tensor.transpose(bank(2)[:, 128 * i:128 * i + 128], s_diff[:, h % 2, 0, 128 * i:128 * i + 128], ident)
                last.then_inc(at_done, 1)

            def weigh_values(h):
                pe.wait_ge(at_act, h + 1)
                if h >= 1:
                    pe.wait_ge(o_made, h)
                a = at_diff[:, h % 2, :]
                v = slice(P * h, P * h + P)
                nc.tensor.matmul(bank(3)[:, 0:128], a[:, 0:128], v_sb[:, 0, v], start=True, stop=True)
                nc.tensor.matmul(bank(3)[:, 128:256], a[:, 128:256], v_sb[:, 0, v], start=True, stop=False)
                nc.tensor.matmul(bank(3)[:, 128:256], a[:, 256:384], v_sb[:, 1, v], start=False, stop=True).then_inc(pv_done, 1)

            def transpose_out(h):
                pe.wait_ge(o_made, h + 1)
                if h >= 1:
                    pe.wait_ge(o_lo_made, h)
                for q in range(QT):
                    last = nc.tensor.transpose(bank(1)[:, 128 * q:128 * q + 128], o_diff[:, q, :], ident)
                last.then_inc(ot_done, 1)

            def head_ada(t, i):
                c = head_groups[t][i] if t < HEADS else side(5) + i
                e, k = c // 8, c % 8
                if t == 0 and i == 0:
                    pe.wait_ge(v_act, 1)
                    pe.wait_ge(v_dve, 1)
                elif k == 0:
                    pe.wait_ge(modrow_made, e)
                ada_chunk(e, k, bank(0)[:, 0:256])

            qk_diff = kv_sb[:, 0:1024].rearrange("p (s n) -> p s n", s=2)
            for t in range(HEADS):
                project(t)
                head_ada(t, 0)
                if t >= 2:
                    transpose_probs(t - 2)
                if t >= 1:
                    score(t - 1)
                head_ada(t, 1)
                if t >= 3:
                    transpose_out(t - 3)
                if t not in (2, 5):
                    head_ada(t, 2)
                if t >= 2:
                    weigh_values(t - 2)
                if t >= 6:
                    head_ada(t, 3)
            score(7)
            for i in range(3):
                head_ada(8, i)
            transpose_probs(6)
            transpose_out(5)
            head_ada(8, 3)
            weigh_values(6)

            def out_product(layer, k):
                pe.wait_ge(o_lo_made, HEADS * layer + k + 1)
                row_product(R_OUT[layer] + k, o_hi[:, k, :], o_lo[:, k, :], 4, k == 0, False)

            def last_out_products(layer):
                last_row_products([R_OUT[layer] + k for k in range(8 - LAST, 8)], range(8 - LAST, 8), 4, o_lo_made, HEADS * layer + 9 - LAST)

            pe.wait_ge(biased, 4 * HEADS)
            out_product(0, 0)
            head_ada(8, 4)
            transpose_probs(7)
            out_product(0, 1)
            transpose_out(6)
            weigh_values(7)
            head_ada(8, 5)
            pe.wait_ge(at_act, 8)
            pe.wait_ge(modcol_made, 4)
            gate_part(1, bank(2), 0)
            out_product(0, 2)
            out_product(0, 3)
            transpose_out(7)
            head_ada(8, 6)
            out_product(0, 4)
            head_ada(8, 7)
            pe.wait_ge(gate_made, 1)
            gate_part(1, bank(2), 1)
            last_out_products(0)

            def transpose_rows(n, y0, ybank):
                pe.wait_ge(z_made, 4 * n + 2)
                group_beside_norm(n, ybank, range(4))
                for q in range(QT):
                    pe.wait_ge((rows0_made, rows1_made)[q], n + 1)
                    if n == 0 and q == 0:
                        pe.wait_ge(modrow_made, 6)
                        pe.wait_ge(gate_made, 2)
                        pe.wait_ge(o_lo_made, HEADS)
                    for k in range(KT):
                        if q == 1 and k == 4:
                            pe.wait_ge(rows1_end_made, n + 1)
                        o = 128 * (k % 4)
                        last = nc.tensor.transpose(bank(y0 + 2 * (k // 4) + q)[:, o:o + 128], xn[:, q, 128 * k:128 * k + 128], ident)
                    last.then_inc(xt_done, 1)
                    if q == 0:
                        group_beside_norm(n, ybank, (4,))

            def group_beside_norm(n, ybank, chunks):
                for k in chunks:
                    ada_chunk(GROUP_BESIDE_NORM[n], k, bank(ybank)[:, 0:256])

            def ffn(layer):
                c0, r0, j0 = C_FFN[layer], R_DOWN[layer], HT * layer

                def hidden(j, b=None, stage=None):
                    if j >= 2:
                        pe.wait_ge(hid_made, at(j0 + j - 1, b))
                    col_product(c0 + j, bank(6 + j % 2), b, stage)

                def down(j, b=None):
                    pe.wait_ge(act_lo_made, at(j0 + j + 1, b))
                    s = j % FFN_SLOTS
                    row_product(r0 + j, o_hi[:, s, :], o_lo[:, s, :], 0, False, False, b, skip_group_check=True)

                hidden(0, stage=2 * layer + 1)
                if layer == 0:
                    pe.wait_ge(zero_ready, 1)
                for i in range(4):
                    nc.tensor.matmul(bank(i), zeros[:, :], h_hi[:, 0:2, :].rearrange("p k n -> p (k n)"),
                                     start=True, stop=False, skip_group_check=True)
                group_beside_norm(2 * layer, 5, (5, 6))
                hidden(1)
                group_beside_norm(2 * layer, 5, (7,))
                with pe.Fori(0, 3) as b:
                    for i in (1, 2, 3):
                        hidden(2 * i, b)
                        hidden(2 * i + 1, b)
                        down(2 * i - 2, b)
                        down(2 * i - 1, b)
                pe.wait_ge(modrow_made, 7 if layer == 0 else 12)
                gate_part(2, bank(4), 0)
                hidden(20)
                pe.wait_ge(gate_made, 4 * layer + 3)
                gate_part(2, bank(4), 1)
                down(18)
                if layer == 0:
                    for k in range(4):
                        ada_chunk(7, k, bank(5)[:, 0:256])
                    pe.wait_ge(gate_made, 4)
                    mod_transpose(0, bank(4))
                hidden(21)
                if layer == 0:
                    for k in range(4, 8):
                        ada_chunk(7, k, bank(5)[:, 0:256])
                last_row_products([r0 + j for j in range(HT - LAST, HT)], [j % FFN_SLOTS for j in range(HT - LAST, HT)],
                                  0, act_lo_made, j0 + HT - LAST + 1, skip_group_check=True)
                if layer == 0:
                    pe.wait_ge(modrow_made, 8)
                    pe.wait_ge(modcol_made, 5)
                    mod_transpose(1, bank(4))

            transpose_rows(0, 0, 5)
            ffn(0)
            pe.wait_ge(modcol_made, 6)
            transpose_rows(1, 4, 1)

            for i in range(6):
                if i >= 2:
                    pe.wait_ge(kv_evac, i - 1)
                if i < 4:
                    col_product(C_NSA + i, bank(2 * (i % 2)), None, 2 if i == 0 else None)
                else:
                    col_product_natural(C_NSA + i, bank(2 * (i % 2)))
                if i == 0:
                    pe.wait_ge(nsa_small_in, 48)
                    for q in range(QT):
                        for k in range(KT):
                            last = nc.tensor.matmul(bank(5)[:, 48 * q:48 * q + 48], h_f[:, k, 128 * q:128 * q + 128],
                                                    gate_wsb[:, k, :], start=(k == 0), stop=(k == KT - 1))
                    last.then_inc(gates_done, 1)
                if i < 2:
                    group_beside_norm(1, 1, ((5, 6), (7,))[i])
            blocks = blk.rearrange("p (v n l) -> p v n l", v=2, l=16)
            for v in range(2):
                pe.wait_ge(blk_made, 4 * v + 4)
                for half_ in range(2):
                    c = SIDE_W1 + 2 * v + half_
                    pe.wait_ge(side_loaded[c % SIDE_RING], 16 * (c // SIDE_RING + 1))
                    for i in range(8):
                        l = 8 * half_ + i
                        last = nc.tensor.matmul(bank(3)[:, 64 * v:64 * v + 60], side_raw[:, c % SIDE_RING, 128 * i:128 * i + 128],
                                                blocks[:, v, :, l], start=(l == 0), stop=(l == 15))
                    last.then_inc(side_used, 1)

            def compressed_scores(pairs):
                pe.wait_ge(qk_made, HEADS + pairs[-1] // 2 + 1)
                for q in range(QT):
                    for t in pairs:
                        o = 256 * q + 32 * t
                        last = nc.tensor.matmul(bank(0)[:, o:o + 32], q_all[:, t, 128 * q:128 * q + 128],
                                                kcb[:, t // 4, :, :].rearrange("p u n -> p (u n)"), start=True, stop=True)
                return last

            def query_product(i):
                if i == 1:
                    pe.wait_ge(kv_evac, 6)
                if i >= 2:
                    pe.wait_ge(qk_made, HEADS + i - 1)
                col_product(C_Q + i, bank(4 - 2 * (i % 2)))

            query_product(0)
            query_product(1)
            pe.wait_ge(gelu_made, 2)
            nc.tensor.matmul(bank(3)[:, 128:192], w2_sb[:, 0:128], gel[:, 0, :, :].rearrange("p g n -> p (g n)"),
                             start=True, stop=True)
            pe.wait_ge(gel_spread, 1)
            for g in range(4):
                last = nc.tensor.matmul(bank(3)[:, 192 + 64 * g:256 + 64 * g], gel_rep[:, g, :],
                                        w2_sb[:, 128:192], start=True, stop=True)
            last.then_inc(w2_done, 1)
            query_product(2)
            pe.wait_ge(cmp_evac, 1)
            compressed_scores((0, 1, 2, 3))

            def nsa_score(t, between=None):
                pe.wait_ge(qk_made, HEADS + t // 2 + 1)
                if t == 0:
                    pe.wait_ge(kv_evac, 6)
                if t >= 1:
                    pe.wait_ge(biased, 4 * HEADS + 8 * t)
                gp = t // 4

                def keys(u, q):
                    rows = slice(64 * u, 64 * u + 64)
                    for s in range(2):
                        if q == 0:
                            dst = bank(5)[:, 256 * u + 128 * s:256 * u + 128 * s + 128]
                        else:
                            dst = bank(6 + u)[:, 256 * s:256 * s + 256]
                        last = nc.tensor.matmul(dst, q_all[rows, t, 128 * q:128 * q + 128],
                                                kk[rows, s, gp, 0:128 * (q + 1)], start=True, stop=True)
                    return last

                keys(0, 0).then_inc(first_scored, 1)
                keys(1, 1)
                if between is not None:
                    between()
                keys(0, 1)
                pe.wait_ge(first_scored, t + 1)
                keys(1, 0).then_inc(scored, 1)

            def nsa_transpose(t, u):
                if t == 0 and u == 0:
                    pe.wait_ge(modrow_made, 9)
                    pe.wait_ge(qk_made, HEADS + 4)
                else:
                    pe.wait_ge(at_act, HEADS + 2 * t + u)
                if t == 4 and u == 0:
                    pe.wait_ge(modrow_made, 10)
                    mod_transpose(0, bank(1)[:, 384:392])
                if t == 4 and u == 1:
                    pe.wait_ge(modcol_made, 7)
                pe.wait_ge(p_scaled, 2 * t + u + 1)
                for s in range(2):
                    for i in range(3):
                        last = nc.tensor.transpose(bank(1 + s)[:, 128 * i:128 * i + 128],
                                                   s_nsa[:, u, s, 128 * i:128 * i + 128], ident)
                last.then_inc(at_done, 1)

            def nsa_weigh(t):
                if t >= 1:
                    pe.wait_ge(o_lo_made, HEADS + t)
                pe.wait_ge(at_act, HEADS + 2 * t + 2)
                for s in range(2):
                    for k in range(2):
                        lo, n = ((0, 256), (256, 128))[k]
                        for u in range(2):
                            cols = slice(64 * (2 * (t // 4) + u), 64 * (2 * (t // 4) + u) + 64)
                            nc.tensor.matmul(bank(3)[64 * u:64 * u + 64, 256 - n:256], vv[:, s, k, cols],
                                             at_nsa[:, u, s, lo:lo + n], start=(s == 0 and k == 0), stop=False,
                                             tile_position=(0, 64 * u), skip_group_check=True)
                if t == 0:
                    pe.wait_ge(c_evac, 1)
                rows = slice(32 * (t % 4), 32 * (t % 4) + 32)
                nc.tensor.matmul(bank(3)[:, 0:256], vcb[rows, t // 4, :], sc[rows, 256 * (t // 4):256 * (t // 4) + 256],
                                 start=False, stop=True, tile_position=(32 * (t % 4), 0), skip_group_check=True)\
                    .then_inc(pv_done, 1)

            def nsa_ada(t, i):
                if t == 4 and i == 0:
                    pe.wait_ge(modrow_made, 10)
                if t == 0 and i == 0:
                    pe.wait_ge(qk_made, HEADS + 3)
                ada_chunk(9 + t // 4, 2 * (t % 4) + i, bank(4)[:, 0:256])

            nsa_score(0)
            query_product(3)
            compressed_scores((4, 5))
            compressed_scores((6, 7)).then_inc(c_scored, 1)
            nsa_ada(0, 0)
            nsa_ada(0, 1)
            for t in range(1, TILES):
                nsa_score(t, between=lambda: nsa_transpose(t - 1, 0))
                nsa_transpose(t - 1, 1)
                nsa_ada(t, 0)
                nsa_ada(t, 1)
                if t == 1:
                    pe.wait_ge(c_made, 1)
                    for gp in range(2):
                        for q in range(QT):
                            i = 2 * gp + q
                            o = 256 * q + 128 * gp
                            last = nc.tensor.transpose(bank(0)[:, 128 * i:128 * i + 128], sc[:, o:o + 128], ident)
                    last.then_inc(c_tr, 1)
                nsa_weigh(t - 1)

            pe.wait_ge(biased, 4 * HEADS + 8 * TILES)
            pe.wait_ge(modrow_made, 11)
            out_product(1, 0)
            nsa_transpose(TILES - 1, 0)
            out_product(1, 1)
            nsa_transpose(TILES - 1, 1)
            out_product(1, 2)
            nsa_weigh(TILES - 1)
            mod_transpose(0, bank(1))
            gate_part(1, bank(2), 0)
            out_product(1, 3)
            out_product(1, 4)
            pe.wait_ge(gate_made, 5)
            gate_part(1, bank(2), 1)
            last_out_products(1)
            pe.wait_ge(gate_made, 6)
            pe.wait_ge(modcol_made, 8)
            transpose_rows(2, 0, 5)
            ffn(1)

        @block.scalar
        def _(act):
            def split_col(c, b=None):
                act.wait_ge(col_loaded[c % COL_RING], loads(c, COL_RING, b))
                if c >= COL_SPLIT:
                    act.wait_ge(col_used, at(c - COL_SPLIT + 1, b))
                nc.scalar.activation(col_hi[:, c % COL_SPLIT, :], col_raw[:, c % COL_RING, :], ACT.Copy).then_inc(col_hi_made, 1)

            def split_row(c, b=None):
                act.wait_ge(row_loaded[c % ROW_RING], loads(c, ROW_RING, b))
                if c >= ROW_SPLIT:
                    act.wait_ge(row_used, at(c - ROW_SPLIT + 1, b))
                nc.scalar.activation(row_hi[:, c % ROW_SPLIT, :], row_raw[:, c % ROW_RING, :], ACT.Copy).then_inc(row_hi_made, 1)

            def copy_modcol(n, e, src):
                act.wait_ge(modT_done, n + 1)
                nc.scalar.activation(modcol[:, e, :].rearrange("p (j i) -> p i j", j=4),
                                     src[:, 0:8].rearrange("p (i j) -> p i j", i=2), ACT.Copy).then_inc(modcol_made, 1)

            act.dma_start(cols_sb[:, :, :], cols).then_inc(cols_in, 16)
            act.dma_start(h_f[:, :, :], xT).then_inc(xT_in, 16)
            act.dma_start(ident, consts[:, 0:P]).then_inc(consts_in, 16)
            act.wait_ge(cols_in, 16)
            nc.scalar.activation(silu_sb8[:, :], cols_sb[:, 0, :], ACT.Silu).then_inc(silu_c, 1)
            act.wait_ge(lam_sum, 1)
            nc.scalar.activation(lam_exps, lam_sums, ACT.Exp).then_inc(lam_exp, 1)

            def input_tiles(stage):
                act.wait_ge(fold_made, stage + 1)
                if stage == 0:
                    act.wait_ge(xT_in, 16)
                else:
                    act.wait_ge(xt_done, 2 * stage)
                    y0 = 4 if stage == 2 else 0
                def affine(k):
                    src = h_f[:, k, :] if stage == 0 else \
                        bank(y0 + 2 * (k // 4), 2).rearrange("p (q n) -> p q n", q=2)[:, :, 128 * (k % 4):128 * (k % 4) + 128]
                    dst = h_f[:, k, :] if stage == 0 else h_f[:, k, :].rearrange("p (q n) -> p q n", q=2)
                    nc.scalar.activation(dst, src, ACT.Identity, scale=fold[:, stage, 0, k:k + 1],
                                         bias=fold[:, stage, 1, k:k + 1]).then_inc(aff_act, 1)

                for k in range(KT):
                    if k < 4:
                        act.wait_ge(aff_dve, 4 * stage + k + 1)
                    else:
                        act.wait_ge(aff_act, 4 * stage + k - 3)
                    nc.scalar.activation(h_hi[:, k, :], h_f[:, k, :], ACT.Copy).then_inc(h_hi_made, 1)
                    if k < 4:
                        affine(4 + k)

            split_row(0)
            split_row(1)
            input_tiles(0)
            for c in range(2, 8):
                split_row(c)
            split_col(0)
            split_col(1)
            act.wait_ge(row_used, 8)
            nc.scalar.activation(v_sb[:, 0, :], bank(0, 2), ACT.Copy).then_inc(v_act, 1)

            qk_diff = kv_sb[:, 0:1024].rearrange("p (s n) -> p s n", s=2)

            def copy_probs(h):
                act.wait_ge(at_done, h + 1)
                if h >= 2:
                    act.wait_ge(pv_done, h - 1)
                nc.scalar.activation(at_diff[:, h % 2, :], bank(2)[:, 0:384], ACT.Copy).then_inc(at_act, 1)

            def exps(h):
                act.wait_ge(max_made, h + 1)
                for c in range(2):
                    for q, lo, n in ((0, 0, 128), (1, 128, 256)):
                        s = s_diff[:, h % 2, c, lo:lo + n]
                        i = 2 * c + q
                        nc.scalar.activation(s, s, ACT.Exp, scale=SCALE, bias=sml[:, h, 4 + i:5 + i],
                                             accum_out=sml[:, h, 8 + i:9 + i]).then_inc(exp_made, 1)

            def squares(h):
                act.wait_ge(pv_done, h + 1)
                for q in range(QT):
                    nc.scalar.activation(sq_junk[:, h % 2, q, :], bank(3)[:, 128 * q:128 * q + 128], ACT.Square,
                                         scale=sml[:, h, 12 + q:13 + q], accum_out=sml[:, h, 18 + q:19 + q]).then_inc(squared, 1)

            def out_hi(h):
                act.wait_ge(ot_done, h + 1)
                nc.scalar.activation(o_hi[:, h, :], bank(1)[:, 0:256], ACT.Copy).then_inc(o_hi_made, 1)

            for t in range(9):
                if t < HEADS:
                    act.wait_ge(col_used, t + 1)
                    if t >= 2:
                        act.wait_ge(scored, t - 1)
                    nc.scalar.activation(qk_diff[:, t % 2, :], bank(4 + t % 2), ACT.Copy).then_inc(qk_made, 1)
                if t >= 2:
                    copy_probs(t - 2)
                if t == 7:
                    copy_modcol(2, 3, bank(2)[:, 384:392])
                if t >= 1:
                    exps(t - 1)
                if t >= 3:
                    out_hi(t - 3)
                if t >= 2:
                    squares(t - 2)
                if t < HEADS:
                    split_col(C_HEAD + t + 2)
                if t >= 6:
                    split_row(R_OUT[0] + t - 6)

            def normalise(n):
                for q, lo, done in ((0, BANK if n == 3 else 0, rows0_made), (1, BANK, rows1_end_made)):
                    if n == 3 and q == 1:
                        break
                    act.wait_ge(shift_made, 2 * n + q + 1)
                    z, st = xn[:, q, lo:D], stats[:, q, :]
                    nc.scalar.activation(z, z, ACT.Identity, scale=st[:, 15:16], bias=st[:, 16:17]).then_inc(done, 1)

            def copy_gate(i, src, r):
                act.wait_ge(gate_spread, i + 1)
                nc.scalar.activation(gate_row[:, BANK * r:BANK * r + BANK], src, ACT.Copy).then_inc(gate_made, 1)

            copy_probs(7)
            copy_modcol(3, 4, bank(2)[:, 384:392])
            split_row(R_OUT[0] + 3)
            out_hi(6)
            squares(7)
            copy_gate(0, bank(2), 0)
            split_row(R_OUT[0] + 4)
            split_row(R_OUT[0] + 5)
            out_hi(7)
            split_row(R_OUT[0] + 6)
            split_row(R_OUT[0] + 7)
            copy_gate(1, bank(2), 1)

            def ffn(layer):
                c0, r0, j0 = C_FFN[layer], R_DOWN[layer], HT * layer

                def silu(j, b=None):
                    act.wait_ge(col_used, at(c0 + j + 1, b))
                    if j >= 2:
                        act.wait_ge(hid_made, at(j0 + j - 1, b))
                    nc.scalar.activation(silu_sb[:, j % 2, :], bank(6 + j % 2)[:, 0:256], ACT.Silu).then_inc(silu_made, 1)

                def hid_hi(j, b=None):
                    act.wait_ge(hid_made, at(j0 + j + 1, b))
                    if j >= FFN_SLOTS:
                        act.wait_ge(row_used, at(r0 + j - FFN_SLOTS + 1, b))
                    nc.scalar.activation(o_hi[:, j % FFN_SLOTS, :], hid_sb[:, j % 2, :], ACT.Copy).then_inc(act_hi_made, 1)

                def step(i, b=None):
                    silu(2 * i, b)
                    split_col(c0 + 2 * i + 2, b)
                    hid_hi(2 * i - 1, b)
                    silu(2 * i + 1, b)
                    split_col(c0 + 2 * i + 3, b)
                    hid_hi(2 * i, b)
                    split_row(r0 + 2 * i, b)
                    split_row(r0 + 2 * i + 1, b)

                silu(0)
                split_col(c0 + 2)
                silu(1)
                split_col(c0 + 3)
                hid_hi(0)
                split_row(r0)
                split_row(r0 + 1)
                with act.Fori(0, 3) as b:
                    for i in (1, 2, 3):
                        step(i, b)
                copy_gate(4 * layer + 2, bank(4), 0)
                silu(20)
                copy_gate(4 * layer + 3, bank(4), 1)
                split_row(r0 + 20)
                hid_hi(19)
                hid_hi(20)
                split_row(r0 + 21)
                if layer == 0:
                    copy_modcol(4, 6, bank(4))
                    split_col(C_NSA)
                silu(21)
                hid_hi(21)
                if layer == 0:
                    copy_modcol(5, 7, bank(4))

            normalise(0)
            input_tiles(1)
            ffn(0)
            normalise(1)
            input_tiles(2)
            split_col(C_NSA + 1)

            for i in range(6):
                act.wait_ge(col_used, C_NSA + i + 1)
                if i < 2:
                    dst = kvc[:, i, :, :].rearrange("p g n -> p (g n)")
                elif i < 4:
                    dst = kk[:, i - 2, :, :].rearrange("p g n -> p (g n)")
                else:
                    dst = vv[:, i - 4, :, :].rearrange("p q n -> p (q n)")
                if i == 2:
                    act.wait_ge(x_updated, 4)
                nc.scalar.activation(dst, bank(2 * (i % 2)), ACT.Copy).then_inc(kv_evac, 1)
                split_col(C_NSA + i + 2)
                if i == 0:
                    act.wait_ge(gates_done, 1)
                    nc.scalar.activation(gate_sb[:, :], bank(5)[:, 0:96], ACT.Exp, scale=-1.0).then_inc(gates_exp, 1)
            act.wait_ge(cmp_zeroed, 1)
            act.wait_ge(side_used, SIDE_W1 + 4)
            for v in range(2):
                nc.scalar.activation(gel[:, v, :, 0:N_CMP], bank(3)[:, 64 * v:64 * v + 60].rearrange("p (g n) -> p g n", g=4),
                                     ACT.Gelu_apprx_tanh).then_inc(gelu_made, 1)
            def copy_queries(i):
                act.wait_ge(col_used, C_Q + i + 1)
                nc.scalar.activation(q_all[:, 2 * i:2 * i + 2, :].rearrange("p t n -> p (t n)"), bank(4 - 2 * (i % 2)), ACT.Copy)\
                    .then_inc(qk_made, 1)
                if i < 2:
                    split_col(C_Q + i + 2)
                else:
                    split_row(R_OUT[1] + i - 2)

            for i in range(3):
                copy_queries(i)

            def nsa_exps(t, u):
                act.wait_ge(max_made, HEADS + 2 * t + u + 1)
                for q, lo, n in ((0, 0, 128), (1, 128, 256)):
                    for s in range(2):
                        x = s_nsa[:, u, s, lo:lo + n]
                        i = (2 * u + q) * 2 + s
                        nc.scalar.activation(x, x, ACT.Exp, scale=SCALE, bias=sml[:, t, 8 + i:9 + i],
                                             accum_out=sml[:, t, 16 + i:17 + i]).then_inc(exp_made, 1)

            for t in range(TILES + 1):
                if t == 1:
                    copy_queries(3)
                    act.wait_ge(c_biased, 1)
                    nc.scalar.activation(sc[:, :], sc[:, :], ACT.Exp, scale=SCALE).then_inc(c_exp, 1)
                if t >= 1:
                    for u in range(2):
                        act.wait_ge(at_done, HEADS + 2 * (t - 1) + u + 1)
                        if t >= 2:
                            act.wait_ge(pv_done, HEADS + t - 1)
                        nc.scalar.activation(at_nsa[:, u, :, :], bank(1, 2).rearrange("p (s n) -> p s n", s=2)[:, :, 0:384],
                                             ACT.Copy).then_inc(at_act, 1)
                        if t == 5 and u == 0:
                            copy_modcol(6, 9, bank(1)[:, 384:392])
                        if t == TILES:
                            split_row(R_OUT[1] + 3 + u)
                if t == 1:
                    act.wait_ge(c_tr, 1)
                    nc.scalar.activation(sc[:, :], bank(0), ACT.Copy).then_inc(c_evac, 1)
                if t < TILES:
                    nsa_exps(t, 0)
                    nsa_exps(t, 1)
                if t == 2:
                    split_row(R_OUT[1] + t)
                if t >= 1:
                    act.wait_ge(pv_done, HEADS + t)
                    nc.scalar.activation(o_hi[:, t - 1, :], bank(3)[:, 0:256], ACT.Copy).then_inc(o_hi_made, 1)

            copy_modcol(7, 10, bank(1))
            copy_gate(4, bank(2), 0)
            split_row(R_OUT[1] + 5)
            split_col(C_FFN[1])
            split_row(R_OUT[1] + 6)
            split_row(R_OUT[1] + 7)
            copy_gate(5, bank(2), 1)
            split_col(C_FFN[1] + 1)
            normalise(2)
            input_tiles(3)
            ffn(1)
            normalise(3)

        @block.vector
        def _(dve):
            own = [0]

            def then(ins):
                own[0] += 1
                ins.then_inc(dve_done, 1)
                dve.wait_ge(dve_done, own[0])

            def split_col(c, b=None):
                dve.wait_ge(col_hi_made, at(c + 1, b))
                nc.vector.tensor_tensor(col_lo[:, c % COL_SPLIT, :], col_raw[:, c % COL_RING, :],
                                        col_hi[:, c % COL_SPLIT, :].bitcast(F32), ALU.subtract).then_inc(col_lo_made, 1)

            def split_row(c, b=None):
                dve.wait_ge(row_hi_made, at(c + 1, b))
                nc.vector.tensor_tensor(row_lo[:, c % ROW_SPLIT, :], row_raw[:, c % ROW_RING, :],
                                        row_hi[:, c % ROW_SPLIT, :].bitcast(F32), ALU.subtract).then_inc(row_lo_made, 1)

            def make_modrow(e, src, slot):
                one = 0.0 if e % 6 in (0, 3) else 1.0
                dve.wait_ge(bias_loaded[e % 2], 16 * (e // 2 + 1))
                dve.wait_ge(side_used, side(e) + 8)
                if e in (4, 6, 8, 9, 10):
                    dve.wait_ge(modT_done, {4: 3, 6: 4, 8: 6, 9: 5, 10: 7}[e])
                if e in (7, 11):
                    dve.wait_ge(gate_spread, {7: 2, 11: 4}[e])
                nc.vector.scalar_tensor_tensor(modrow[:, slot, :], src, one, bias_rows[:, e % 2, :], ALU.add, ALU.add)\
                    .then_inc(modrow_made, 1)

            def make_modcol(n, e, src):
                dve.wait_ge(modT_done, n + 1)
                nc.vector.tensor_copy(modcol[:, e, :].rearrange("p (j i) -> p i j", j=4),
                                      src[:, 0:8].rearrange("p (i j) -> p i j", i=2)).then_inc(modcol_made, 1)

            def make_fold(stage, shift, scale, ncol):
                a, b = fold[:, stage, 0, :], fold[:, stage, 1, :]
                dve.wait_ge(modcol_made, ncol)
                if stage == 0:
                    nc.vector.tensor_copy(a, modcol[:, scale, :])
                    nc.vector.tensor_copy(b, modcol[:, shift, :]).then_inc(fold_made, 1)
                    return
                g, s = cols_sb[:, 2 * stage - 1, :], cols_sb[:, 2 * stage, :]
                nc.vector.tensor_tensor(a, g, modcol[:, scale, :], ALU.mult)
                then(nc.vector.tensor_tensor(b, s, modcol[:, scale, :], ALU.mult))
                nc.vector.tensor_tensor(b, b, modcol[:, shift, :], ALU.add).then_inc(fold_made, 1)

            def input_tiles(stage):
                if stage == 0:
                    dve.wait_ge(xT_in, 16)
                    dve.wait_ge(fold_made, 1)
                else:
                    dve.wait_ge(xt_done, 2 * stage)
                    dve.wait_ge(fold_made, stage + 1)
                    y0 = 4 if stage == 2 else 0

                def affine(k):
                    src = h_f[:, k, :] if stage == 0 else \
                        bank(y0 + 2 * (k // 4), 2).rearrange("p (q n) -> p q n", q=2)[:, :, 128 * (k % 4):128 * (k % 4) + 128]
                    dst = h_f[:, k, :] if stage == 0 else h_f[:, k, :].rearrange("p (q n) -> p q n", q=2)
                    nc.vector.tensor_scalar(dst, src, fold[:, stage, 0, k:k + 1], fold[:, stage, 1, k:k + 1],
                                            ALU.mult, ALU.add).then_inc(aff_dve, 1)

                affine(0)
                for k in range(KT):
                    if k < 3:
                        affine(k + 1)
                    dve.wait_ge(h_hi_made, 8 * stage + k + 1)
                    nc.vector.tensor_tensor(h_lo[:, k, :], h_f[:, k, :], h_hi[:, k, :].bitcast(F32), ALU.subtract)\
                        .then_inc(h_made, 1)

            def norm(n, y0):
                row_end = (R_OUT[0] + 8, R_DOWN[0] + 22, R_OUT[1] + 8, R_DOWN[1] + 22)[n]
                dve.wait_ge(gate_made, 2 * n + 2)
                dve.wait_ge(x_in, 16)
                if n >= 1:
                    dve.wait_ge(x_updated, 2 * n)
                if n == 0:
                    dve.wait_ge(pv_done, HEADS)

                def half_rows(q, j):
                    i = 2 * q + j
                    if i < 3:
                        dve.wait_ge(y_done, 3 * n + i + 1)
                    else:
                        dve.wait_ge(row_used, row_end)
                    cols = slice(BANK * j, BANK * j + BANK)
                    z = xn[:, q, cols]
                    nc.vector.tensor_tensor(z, bank(y0 + i), gate_row[:, cols], ALU.mult).then_inc(y_read, 1)
                    dve.wait_ge(y_read, 4 * n + i + 1)
                    nc.vector.scalar_tensor_tensor(z, x_sb[:, q, cols], ALPHA, z, ALU.mult, ALU.add).then_inc(z_made, 1)
                    dve.wait_ge(z_made, 4 * n + i + 1)
                    return nc.vector.bn_stats(stats[:, q, 6 * j:6 * j + 6], z)

                def variance(q):
                    st = stats[:, q, :]
                    then(nc.vector.bn_aggr(st[:, 12:14], st[:, 0:12]))
                    nc.vector.tensor_scalar(st[:, 14:15], st[:, 13:14], LN_EPS, None, ALU.add).then_inc(var_made, 1)

                def shift_of(q):
                    st = stats[:, q, :]
                    dve.wait_ge(ln_rstd, 2 * n + q + 1)
                    nc.vector.tensor_scalar(st[:, 16:17], st[:, 12:13], st[:, 15:16], -1.0, ALU.mult, ALU.mult).then_inc(shift_made, 1)

                half_rows(0, 0)
                then(half_rows(0, 1))
                variance(0)
                half_rows(1, 0)
                shift_of(0)
                then(half_rows(1, 1))
                variance(1)
                if n < 3:
                    shift_of(1)
                    z, st = xn[:, 1, 0:BANK], stats[:, 1, :]
                    nc.vector.tensor_scalar(z, z, st[:, 12:13], st[:, 15:16], ALU.subtract, ALU.mult).then_inc(rows1_made, 1)
                if n == 1:
                    make_fold(2, 6, 7, 6)

            dve.wait_ge(silu_c, 1)
            nc.vector.tensor_copy(c_rep[:, :, :], silu_sb8[:, :].unsqueeze(2).broadcast_to([P, KT, 32])).then_inc(c_ready, 1)
            nc.vector.memset(kcb[:, :, :, :], 0.0)
            nc.vector.memset(gel[:, :, :, :], 0.0).then_inc(cmp_zeroed, 1)
            dve.wait_ge(small_in, 32)
            then(nc.vector.tensor_tensor(og[:, 0:2, :], lam_sb[:, 0:4:2, :], lam_sb[:, 1:4:2, :], ALU.mult))
            nc.vector.tensor_reduce(lam_sums, og[:, 0:2, :], op=ALU.add, axis=AX.X).then_inc(lam_sum, 1)
            dve.wait_ge(lam_exp, 1)
            then(nc.vector.tensor_tensor(neg_lam, lam_exps[:, 1:2], lam_exps[:, 0:1], ALU.subtract))
            then(nc.vector.tensor_scalar(neg_lam, neg_lam, -LAM_INIT, None, ALU.add))
            then(nc.vector.tensor_scalar(subln_sb, subln_sb, 1.0 - LAM_INIT, None, ALU.mult))
            split_row(0)
            make_modrow(0, bank(0)[:, 0:256], 0)
            split_row(1)
            make_modrow(1, bank(1)[:, 0:256], 1)
            make_modcol(0, 0, bank(2))
            make_modcol(1, 1, bank(3))
            make_fold(0, 0, 1, 2)
            input_tiles(0)
            for c in range(2, 8):
                split_row(c)
            split_col(0)
            split_col(1)
            dve.wait_ge(row_used, 8)
            nc.vector.tensor_copy(v_sb[:, 1, :], bank(2, 2)).then_inc(v_dve, 1)

            def bias_max(h):
                dve.wait_ge(scored, h + 1)
                dve.wait_ge(bias_ready, h + 1)
                if h >= 2:
                    dve.wait_ge(at_done, h - 1)
                for c in range(2):
                    for q, lo, n in ((0, 0, 128), (1, 128, 256)):
                        i = 2 * c + q
                        nc.vector.tensor_tensor_reduce(out=s_diff[:, h % 2, c, lo:lo + n], in0=bank(6 + c)[:, lo:lo + n],
                                                       in1=bias_t[:, h % 2, lo:lo + n], scale=1.0, scalar=FAR_BELOW,
                                                       op0=ALU.add, op1=ALU.max, accum_out=sml[:, h, i:i + 1]).then_inc(biased, 1)
                dve.wait_ge(biased, 4 * h + 4)
                nc.vector.tensor_scalar(sml[:, h, 4:8], sml[:, h, 0:4], -SCALE, None, ALU.mult).then_inc(max_made, 1)

            def mix(h):
                s = sml[:, h, :]
                dve.wait_ge(exp_made, 4 * h + 4)
                then(nc.vector.reciprocal(s[:, 12:16], s[:, 8:12]))
                then(nc.vector.scalar_tensor_tensor(s[:, 16:18], s[:, 8:10], neg_lam, s[:, 14:16], ALU.mult, ALU.mult))
                for q, lo, n in ((0, 0, 128), (1, 128, 256)):
                    p0 = s_diff[:, h % 2, 0, lo:lo + n]
                    last = nc.vector.scalar_tensor_tensor(p0, s_diff[:, h % 2, 1, lo:lo + n], s[:, 16 + q:17 + q], p0,
                                                          ALU.mult, ALU.add)
                last.then_inc(mixed, 1)

            def normalise(h):
                s = sml[:, h, :]
                dve.wait_ge(squared, 2 * h + 2)
                nc.vector.tensor_scalar(s[:, 20:22], s[:, 18:20], 1.0 / P, RMS_EPS, ALU.mult, ALU.add).then_inc(ms_made, 1)
                dve.wait_ge(rstd_made, h + 1)
                then(nc.vector.tensor_tensor(s[:, 24:26], s[:, 22:24], s[:, 12:14], ALU.mult))
                if h >= 1:
                    dve.wait_ge(ot_done, h)
                for q in range(QT):
                    last = nc.vector.scalar_tensor_tensor(o_diff[:, q, :], bank(3)[:, 128 * q:128 * q + 128],
                                                          s[:, 24 + q:25 + q], subln_sb, ALU.mult, ALU.mult)
                last.then_inc(o_made, 1)

            def out_lo(h):
                dve.wait_ge(o_hi_made, h + 1)
                nc.vector.tensor_tensor(o_lo[:, h, :], bank(1)[:, 0:256], o_hi[:, h, :].bitcast(F32), ALU.subtract)\
                    .then_inc(o_lo_made, 1)

            for t in range(9):
                if t >= 1:
                    bias_max(t - 1)
                if t in (2, 5, 7):
                    make_modrow({2: 2, 5: 3, 7: 4}[t], bank(0)[:, 0:256], 1 if t == 2 else 0)
                if t >= 3:
                    out_lo(t - 3)
                if t >= 1:
                    mix(t - 1)
                if t >= 2:
                    normalise(t - 2)
                if t < HEADS:
                    split_col(C_HEAD + t + 2)
                if t >= 6:
                    split_row(R_OUT[0] + t - 6)
            split_row(R_OUT[0] + 3)
            out_lo(6)
            normalise(7)
            split_row(R_OUT[0] + 4)
            split_row(R_OUT[0] + 5)
            out_lo(7)
            make_fold(1, 3, 4, 4)
            split_row(R_OUT[0] + 6)
            split_row(R_OUT[0] + 7)
            make_modrow(5, bank(0)[:, 0:256], 2)

            def ffn(layer):
                c0, r0, j0 = C_FFN[layer], R_DOWN[layer], HT * layer

                def hid(j, b=None):
                    dve.wait_ge(silu_made, at(j0 + j + 1, b))
                    if j >= 2:
                        dve.wait_ge(act_lo_made, at(j0 + j - 1, b))
                    nc.vector.tensor_tensor(hid_sb[:, j % 2, :], bank(6 + j % 2)[:, 256:512], silu_sb[:, j % 2, :], ALU.mult)\
                        .then_inc(hid_made, 1)

                def hid_lo(j, b=None):
                    dve.wait_ge(act_hi_made, at(j0 + j + 1, b))
                    nc.vector.tensor_tensor(o_lo[:, j % FFN_SLOTS, :], hid_sb[:, j % 2, :], o_hi[:, j % FFN_SLOTS, :].bitcast(F32), ALU.subtract)\
                        .then_inc(act_lo_made, 1)

                def step(i, b=None):
                    hid(2 * i, b)
                    split_col(c0 + 2 * i + 2, b)
                    hid_lo(2 * i - 1, b)
                    hid(2 * i + 1, b)
                    split_col(c0 + 2 * i + 3, b)
                    hid_lo(2 * i, b)
                    split_row(r0 + 2 * i, b)
                    split_row(r0 + 2 * i + 1, b)

                hid(0)
                split_col(c0 + 2)
                hid(1)
                split_col(c0 + 3)
                hid_lo(0)
                if layer == 0:
                    make_modrow(6, bank(5)[:, 0:256], 0)
                else:
                    make_modrow(11, bank(5)[:, 0:256], 2)
                split_row(r0)
                split_row(r0 + 1)
                with dve.Fori(0, 3) as b:
                    for i in (1, 2, 3):
                        step(i, b)
                hid(20)
                split_row(r0 + 20)
                hid_lo(19)
                hid_lo(20)
                split_row(r0 + 21)
                if layer == 0:
                    split_col(C_NSA)
                hid(21)
                hid_lo(21)
                if layer == 0:
                    make_modrow(7, bank(5)[:, 0:256], 1)

            norm(0, 4)
            input_tiles(1)
            ffn(0)
            norm(1, 0)
            input_tiles(2)
            split_col(C_NSA + 1)

            def make_blocks(v):
                for par in range(2):
                    rows = slice(64 * par, 64 * par + 64)
                    for u in range(2):
                        src = (kvc if u == par else kvs)[rows, v, :, :]
                        for gp in range(2):
                            win = src[:, gp, :]
                            o = (v * 4 + 2 * gp + u) * 240
                            dst = blk[rows, o:o + 240].rearrange("p (n l) -> p n l", l=16)
                            lo_half = win[:, 0:240].rearrange("p (n l e) -> p n l e", l=8, e=2)[:, :, :, par]
                            hi_half = win[:, 16:256].rearrange("p (n l e) -> p n l e", l=8, e=2)[:, :, :, par]
                            pb = pos_sb[rows, v, :]
                            nc.vector.tensor_tensor(dst[:, :, 0:8], lo_half, pb[:, 0:8].unsqueeze(1).broadcast_to([64, N_CMP, 8]), ALU.add)
                            last = nc.vector.tensor_tensor(dst[:, :, 8:16], hi_half, pb[:, 8:16].unsqueeze(1).broadcast_to([64, N_CMP, 8]), ALU.add)
                        if u == 1:
                            last.then_inc(blk_made, 2)

            dve.wait_ge(nsa_small_in, 48)
            for c in range(6):
                if c == 2:
                    make_modrow(8, bank(1)[:, 0:256], 1)
                if c == 1:
                    dve.wait_ge(gates_exp, 1)
                    then(nc.vector.tensor_scalar(gate_sb[:, :], gate_sb[:, :], 1.0, None, ALU.add))
                    nc.vector.reciprocal(gate_sb[:, :], gate_sb[:, :]).then_inc(gates_made, 1)
                if c == 3:
                    dve.wait_ge(swapped, 32)
                    dve.wait_ge(x_updated, 4)
                if c in (3, 4):
                    make_blocks(c - 3)
                split_col(C_NSA + c + 2)
            dve.wait_ge(gelu_made, 2)
            nc.vector.tensor_copy(gel_rep.rearrange("p g (r n) -> p g r n", r=8),
                                  gel[:, 1, :, :].unsqueeze(2).broadcast_to([P, 4, 8, 16])).then_inc(gel_spread, 1)
            split_col(C_Q + 2)
            dve.wait_ge(w2_done, 1)
            for u in range(2):
                rows = slice(64 * u, 64 * u + 64)
                nc.vector.tensor_copy(kcb[rows, :, u, :], bank(3)[rows, 128:192].rearrange("p (g u n) -> p g u n", g=2, u=2)[:, :, u, :])
            nc.vector.tensor_tensor(vcb.rearrange("p g (u d) -> p g u d", u=2),
                                    bank(3)[:, 192:448].rearrange("p (g u d) -> p g u d", g=2, u=2),
                                    own_half.unsqueeze(1).unsqueeze(3).broadcast_to([P, 2, 2, 64]), ALU.mult).then_inc(cmp_evac, 1)
            split_col(C_Q + 3)
            split_row(R_OUT[1])

            def nsa_bias_max(t, u):
                dve.wait_ge(scored, HEADS + t + 1)
                dve.wait_ge(bias_ready, HEADS + 2 * t + u + 1)
                if t >= 1:
                    dve.wait_ge(at_done, HEADS + 2 * (t - 1) + u + 1)
                for q, lo, n in ((0, 0, 128), (1, 128, 256)):
                    for s in range(2):
                        i = (2 * u + q) * 2 + s
                        src = bank(5)[:, 256 * u + 128 * s:256 * u + 128 * s + 128] if q == 0 else bank(6 + u)[:, 256 * s:256 * s + 256]
                        nc.vector.tensor_tensor_reduce(out=s_nsa[:, u, s, lo:lo + n], in0=src, in1=bias_t[:, u, lo:lo + n],
                                                       scale=1.0, scalar=FAR_BELOW, op0=ALU.add, op1=ALU.max,
                                                       accum_out=sml[:, t, i:i + 1]).then_inc(biased, 1)
                dve.wait_ge(biased, 4 * HEADS + 8 * t + 4 * u + 4)
                nc.vector.tensor_scalar(sml[:, t, 8 + 4 * u:12 + 4 * u], sml[:, t, 4 * u:4 * u + 4], -SCALE, None, ALU.mult)\
                    .then_inc(max_made, 1)

            def scale_probs(t, u):
                s = sml[:, t, :]
                dve.wait_ge(exp_made, 4 * HEADS + 8 * t + 4 * u + 4)
                then(nc.vector.reciprocal(s[:, 24 + 4 * u:28 + 4 * u], s[:, 16 + 4 * u:20 + 4 * u]))
                g = gate_sb[:, :].rearrange("p (q s h) -> p q s h", q=2, s=3)[:, :, 1:3, 2 * t + u]
                then(nc.vector.tensor_tensor(s[:, 32 + 4 * u:36 + 4 * u].rearrange("p (q s) -> p q s", q=2),
                                             s[:, 24 + 4 * u:28 + 4 * u].rearrange("p (q s) -> p q s", q=2), g, ALU.mult))
                for q, lo, n in ((0, 0, 128), (1, 128, 256)):
                    for b in range(2):
                        i = 32 + 4 * u + 2 * q + b
                        p = s_nsa[:, u, b, lo:lo + n]
                        last = nc.vector.tensor_scalar(p, p, s[:, i:i + 1], None, ALU.mult)
                last.then_inc(p_scaled, 1)

            s3 = sc[:, :].rearrange("p (h n) -> p h n", n=16)
            for t in range(TILES + 1):
                if t < TILES:
                    nsa_bias_max(t, 0)
                if t < TILES:
                    nsa_bias_max(t, 1)
                    if t == TILES - 1:
                        make_modrow(10, bank(4)[:, 0:256], 0)
                    scale_probs(t, 0)
                    scale_probs(t, 1)
                if t == 0:
                    dve.wait_ge(c_scored, 1)
                    then(nc.vector.tensor_tensor(sc[:, :], bank(0), dist_c, ALU.add))
                    then(nc.vector.tensor_reduce(smc[:, 0, :], s3, op=ALU.max, axis=AX.X))
                    nc.vector.tensor_tensor(s3, s3, smc[:, 0, :].unsqueeze(2).broadcast_to([P, 32, 16]), ALU.subtract).then_inc(c_biased, 1)
                    dve.wait_ge(c_exp, 1)
                    then(nc.vector.tensor_reduce(smc[:, 1, :], s3, op=ALU.add, axis=AX.X))
                    then(nc.vector.reciprocal(smc[:, 2, :], smc[:, 1, :]))
                    g = gate_sb[:, :].rearrange("p (q s h) -> p q s h", q=2, s=3)[:, :, 0, :]
                    then(nc.vector.tensor_tensor(smc[:, 3, :].rearrange("p (q h) -> p q h", q=2),
                                                 smc[:, 2, :].rearrange("p (q h) -> p q h", q=2), g, ALU.mult))
                    then(nc.vector.scalar_tensor_tensor(sc[:, :], dist_c, -1.0e29, sc[:, :], ALU.is_gt, ALU.mult))
                    nc.vector.tensor_tensor(s3, s3, smc[:, 3, :].unsqueeze(2).broadcast_to([P, 32, 16]), ALU.mult).then_inc(c_made, 1)
                if t == 3:
                    make_modrow(9, bank(4)[:, 0:256], 0)
                if t == TILES:
                    split_row(R_OUT[1] + 3)
                    split_row(R_OUT[1] + 4)
                if t in (1, 2):
                    split_row(R_OUT[1] + t)
                if t >= 1:
                    dve.wait_ge(o_hi_made, HEADS + t)
                    nc.vector.tensor_tensor(o_lo[:, t - 1, :], bank(3)[:, 0:256], o_hi[:, t - 1, :].bitcast(F32), ALU.subtract)\
                        .then_inc(o_lo_made, 1)
            split_row(R_OUT[1] + 5)
            split_col(C_FFN[1])
            make_fold(3, 9, 10, 8)
            split_row(R_OUT[1] + 6)
            split_row(R_OUT[1] + 7)
            split_col(C_FFN[1] + 1)
            norm(2, 4)
            input_tiles(3)
            ffn(1)
            norm(3, 0)
            def last_rows_part(q, lo, n):
                z, st = xn[:, q, lo:lo + n], stats[:, q, :]
                then(nc.vector.scalar_tensor_tensor(z, z, st[:, 12:13], kv_sb[:, lo:lo + n], ALU.subtract, ALU.mult))
                dve.wait_ge(ln_rstd, 7 + q)
                nc.vector.scalar_tensor_tensor(x_sb[:, q, lo:lo + n], z, st[:, 15:16], kv_sb[:, D + lo:D + lo + n], ALU.mult, ALU.add)\
                    .then_inc(last_rows, 1)

            dve.wait_ge(lnrow_in, 64)
            last_rows_part(0, 0, BANK)
            last_rows_part(1, 0, BANK)
            last_rows_part(1, BANK, BANK)

        @block.gpsimd
        def _(pool):
            own = [0]

            def then(ins):
                own[0] += 1
                ins.then_inc(pool_done, 1)
                pool.wait_ge(pool_done, own[0])

            pool.dma_start(lam_sb.rearrange("p a n -> p (a n)"), lam[0, :].partition_broadcast(P)).then_inc(small_in, 16)
            pool.dma_start(subln_sb, subln[0, :].partition_broadcast(P)).then_inc(small_in, 16)
            nc.gpsimd.memset(zeros[:, :].bitcast(F32), 0.0).then_inc(zero_ready, 1)
            then(nc.gpsimd.memset(half[:, :], -0.5))
            pool.wait_ge(masks_in, 16)

            def bias(slot, slope, n):
                nc.gpsimd.tensor_scalar(bias_t[:, slot, :], dist, slope / SCALE, 1.0, ALU.mult, ALU.mult).then_inc(bias_ready, 1)

            def rstd(dst, src):
                return nc.gpsimd.tensor_tensor(dst, src, half[:, :].broadcast_to([P, dst.shape[1]]), ALU.pow)

            def row_rstd(h):
                pool.wait_ge(ms_made, h + 1)
                rstd(sml[:, h, 22:24], sml[:, h, 20:22]).then_inc(rstd_made, 1)

            for h in range(HEADS):
                if h >= 2:
                    pool.wait_ge(biased, 4 * (h - 1))
                bias(h % 2, 2.0 ** -(h + 1), h)
                if h >= 3:
                    row_rstd(h - 3)
            for h in range(HEADS - 3, HEADS):
                row_rstd(h)

            def norm(n):
                for q in range(QT):
                    pool.wait_ge(var_made, 2 * n + q + 1)
                    rstd(stats[:, q, 15:16], stats[:, q, 14:15]).then_inc(ln_rstd, 1)
                pool.wait_ge(lnrow_in, 16 * (n + 1))
                for q in range(QT if n < 3 else 1):
                    pool.wait_ge((rows0_made, rows1_made)[q], n + 1)
                    if q == 1:
                        pool.wait_ge(rows1_end_made, n + 1)
                    lo = 0 if n < 3 else BANK
                    x = x_sb[:, q, lo:D]
                    nc.gpsimd.tensor_tensor(x, xn[:, q, lo:D], kv_sb[:, lo:D], ALU.mult).then_inc(x_scaled, 1)
                    pool.wait_ge(x_scaled, 2 * n + q + 1)
                    nc.gpsimd.tensor_tensor(x, x, kv_sb[:, D + lo:2 * D], ALU.add).then_inc(x_updated, 1)

            norm(0)
            norm(1)
            pool.wait_ge(kv_evac, 2)
            pool.dma_start(kvs[64:128, :, :, :].rearrange("p v g n -> p (v g n)"), kvc[0:64, :, :, :].rearrange("p v g n -> p (v g n)")).then_inc(swapped, 16)
            pool.dma_start(kvs[0:64, :, :, :].rearrange("p v g n -> p (v g n)"), kvc[64:128, :, :, :].rearrange("p v g n -> p (v g n)")).then_inc(swapped, 16)
            for t in range(TILES):
                for u in range(2):
                    if t >= 1:
                        pool.wait_ge(biased, 4 * HEADS + 8 * (t - 1) + 4 * u + 4)
                    else:
                        pool.wait_ge(biased, 4 * HEADS)
                    head = 4 * (2 * (t // 4) + u) + t % 4
                    bias(u, 2.0 ** (-0.5 * (head + 1)), t)
            norm(2)
            norm(3)


def kernel(x, c, diff_w_in, diff_w_out, diff_lam_q1, diff_lam_k1, diff_lam_q2, diff_lam_k2, diff_subln_g,
           nsa_w_in, nsa_cmp_pos_k, nsa_cmp_pos_v, nsa_cmp_k_w1, nsa_cmp_k_w2, nsa_cmp_v_w1, nsa_cmp_v_w2,
           nsa_w_out, ada_w, ada_b, ln_mix_g, ln_mix_b, ln_ffn_g, ln_ffn_b, ffn_w_gu, ffn_w_down):
    import numpy as np
    import concourse.bacc as bacc
    from concourse.bass_utils import run_bass_kernel_spmd

    def arr(a):
        return np.asarray(a)

    def pairs(w, blocks):
        cols = np.concatenate([w[:, a:a + n] for a, n in blocks], axis=1)
        return cols.reshape(KT, P, 256).transpose(1, 0, 2).reshape(P, KT * 256)

    def column(v):
        return v.reshape(-1, P).T

    w_in, w_nsa = arr(diff_w_in)[0], arr(nsa_w_in)[0]
    gu, dn = arr(ffn_w_gu), arr(ffn_w_down)
    heads = [(8 * (t // 4) + t % 4, 8 * (t // 4) + 4 + t % 4) for t in range(TILES)]
    flat_heads = [h for pair in heads for h in pair]
    col_chunks = [pairs(w_in, [(P * h, P), (D + P * h, P)]) for h in range(HEADS)]
    col_chunks += [pairs(gu[0], [(P * j, P), (HID + P * j, P)]) for j in range(HT)]
    col_chunks += [pairs(w_nsa, [(o, 256)]) for o in (1024, 1280, 1536, 2048, 1792, 2304)]
    for i in range(4):
        a, b, e, f = heads[2 * i] + heads[2 * i + 1]
        col_chunks.append(pairs(w_nsa, [(64 * a, 64), (64 * b, 64), (64 * e, 64), (64 * f, 64)]))
    col_chunks += [pairs(gu[1], [(P * j, P), (HID + P * j, P)]) for j in range(HT)]
    w_o = np.concatenate([arr(nsa_w_out)[0][64 * h:64 * h + 64] for h in flat_heads], axis=0)
    row_chunks = np.concatenate([w_in[:, 2 * D:3 * D], arr(diff_w_out)[0], dn[0], w_o, dn[1]], axis=0).reshape(N_ROW, P, D)
    ada = arr(ada_w).reshape(2, KT, P, 6, D).transpose(0, 3, 1, 2, 4).reshape(96, P, D)
    w1 = [arr(w)[0].reshape(2, 8, P, P).transpose(0, 2, 1, 3).reshape(2, P, D) for w in (nsa_cmp_k_w1, nsa_cmp_v_w1)]
    side_chunks = np.concatenate([ada[:SIDE_W1]] + w1 + [ada[SIDE_W1:]], axis=0)
    ada_bias = np.repeat(arr(ada_b).reshape(12, 4, 256), 32, axis=1)
    norms = [(arr(g)[i], arr(b)[i]) for i in range(2) for g, b in ((ln_mix_g, ln_mix_b), (ln_ffn_g, ln_ffn_b))]
    cols = np.stack([column(arr(c)[0])] + [column(v) for pair in norms for v in pair], axis=1)
    xs = arr(x)[0]
    gate_cols = [2560 + 3 * h + s for s in range(3) for h in flat_heads]
    gate_w = np.stack([w_nsa[:, i] for i in gate_cols], axis=1).reshape(KT, P, 48).transpose(1, 0, 2)
    pos = np.stack([arr(p)[0].reshape(16, P).T for p in (nsa_cmp_pos_k, nsa_cmp_pos_v)], axis=1)
    k2, v2 = arr(nsa_cmp_k_w2)[0], arr(nsa_cmp_v_w2)[0]
    w2 = np.concatenate([k2, k2, v2], axis=1)
    lam = np.concatenate([arr(v) for v in (diff_lam_q1, diff_lam_k1, diff_lam_q2, diff_lam_k2)], axis=1)
    ln_rows = np.stack([np.concatenate(pair) for pair in norms])

    p = np.arange(P)

    def masked(d):
        return np.where(d >= 0, -d, -1e30)

    dist = np.concatenate([masked(p[:, None] - p[None, :]), masked(P + p[:, None] - np.arange(T)[None, :])], axis=1)
    dist_c = np.full((P, QT, TILES, 2, 16), -1e30)
    for q in range(QT):
        for t in range(TILES):
            for u in range(2):
                d = (P * q + p)[:, None] - (16 * np.arange(N_CMP) + 31)[None, :]
                slope = 2.0 ** (-0.5 * (heads[t][u] + 1)) / SCALE
                dist_c[:, q, t, u, :N_CMP] = np.where(d >= 0, -d * slope, -1e30)
    own = (p[:, None] // 16 % 2 == np.arange(2)[None, :]) * 1.0
    consts = np.concatenate([np.eye(P), dist, dist_c.reshape(P, 512), own], axis=1).astype(np.float32)

    arrays = {
        "col_w": np.stack(col_chunks), "row_w": row_chunks, "side": side_chunks, "ada_bias": ada_bias, "cols": cols,
        "xT": xs.T.reshape(KT, P, T).transpose(1, 0, 2), "x_nat": xs.reshape(QT, P, D).transpose(1, 0, 2),
        "ln_rows": ln_rows, "lam": lam, "subln": arr(diff_subln_g), "gate_w": gate_w, "pos": pos, "w2": w2, "consts": consts,
    }
    arrays = {f"in_{n}": np.ascontiguousarray(a) for n, a in arrays.items()}
    nc = bacc.Bacc("TRN2", target_bir_lowering=False, num_devices=1)
    args = [nc.dram_tensor(n, a.shape, mybir.dt.from_np(a.dtype), kind="ExternalInput").ap() for n, a in arrays.items()]
    args.append(nc.dram_tensor("out_x", (QT, P, D), F32, kind="ExternalOutput").ap())
    decoder(nc, *args)
    r = run_bass_kernel_spmd(nc, [arrays], core_ids=[0])
    return r.results[0]["out_x"].reshape(1, T, D)
```

```python
from contextlib import ExitStack

import concourse.bass as bass
from concourse import mybir

F32 = mybir.dt.float32
F32R = mybir.dt.float32r
ALU = mybir.AluOpType
ACT = mybir.ActivationFunctionType
AX = mybir.AxisListType

P = 128
D = 1024
T = 256
KT = D // P
QT = T // P
HID = 2816
HT = HID // P
HEADS = 8
TILES = 8
N_CMP = 15
BANK = 512
ALPHA = 4.0 ** 0.25
LN_EPS = 1e-5
RMS_EPS = 1e-5
SCALE = 0.125
LAM_INIT = 0.8 - 0.6
FAR_BELOW = -3.0e38

C_HEAD = 0
C_FFN = (8, 40)
C_NSA = 30
C_Q = 36
N_COL = 62
R_V, R_OUT, R_DOWN = 0, (8, 38), (16, 46)
N_ROW = 68
SIDE_W1 = 72
COL_RING, ROW_RING, SIDE_RING = 3, 3, 4
COL_SPLIT, ROW_SPLIT = 2, 3
FFN_SLOTS = 6
LOOP_TILES = 6
GROUP_BESIDE_NORM = {0: 6, 1: 8, 2: 11}
LAST = 3


def side(e):
    return 8 * e if 8 * e < SIDE_W1 else 8 * e + 4


def decoder(nc, col_w, row_w, side_w, ada_bias, cols, xT, x_nat, ln_rows, lam, subln, gate_w, pos, w2, consts, out):
    ctx = ExitStack()
    with ctx:
        def sb(name, shape, dt=F32):
            return ctx.enter_context(nc.sbuf_tensor(name, shape, dt))

        def sem(name):
            return ctx.enter_context(nc.semaphore(name))

        col_raw = sb("col_raw", [P, COL_RING, KT * 256])
        row_raw = sb("row_raw", [P, ROW_RING, D])
        col_hi = sb("col_hi", [P, COL_SPLIT, KT * 256], F32R)
        col_lo = sb("col_lo", [P, COL_SPLIT, KT * 256], F32R)
        row_hi = sb("row_hi", [P, ROW_SPLIT, D], F32R)
        row_lo = sb("row_lo", [P, ROW_SPLIT, D], F32R)
        side_raw = sb("side_raw", [P, SIDE_RING, D])
        x_sb = sb("x_sb", [P, QT, D])
        xn = sb("xn", [P, QT, D])
        h_f = sb("h_f", [P, KT, T])
        h_hi = sb("h_hi", [P, KT, T], F32R)
        h_lo = sb("h_lo", [P, KT, T], F32R)
        o_hi = sb("o_hi", [P, KT, T], F32R)
        o_lo = sb("o_lo", [P, KT, T], F32R)
        kv_sb = sb("kv_sb", [P, 2 * D])
        scratch = sb("scratch", [P, 3072])
        bias_t = sb("bias_t", [P, 2, 384])
        modrow = sb("modrow", [P, 3, 256])
        bias_rows = sb("bias_rows", [P, 2, 256])
        consts_sb = sb("consts_sb", [P, 128 + 384 + 512 + 2])
        cols_sb = sb("cols_sb", [P, 9, KT])
        c_rep = sb("c_rep", [P, KT, 32])
        zeros = sb("zeros", [P, P], F32R)
        modcol = sb("modcol", [P, 12, KT])
        fold = sb("fold", [P, 4, 2, KT])
        gate_sb = sb("gate_sb", [P, QT * 48])
        gate_wsb = sb("gate_wsb", [P, KT, 48])
        pos_sb = sb("pos_sb", [P, 2, 16])
        w2_sb = sb("w2_sb", [P, 192])
        gel = sb("gel", [P, 2, 4, 16])
        kcb = sb("kcb", [P, 2, 2, 16])
        sc = sb("sc", [P, 512])
        sml = sb("sml", [P, 8, 40])
        stats = sb("stats", [P, QT, 20])
        silu_sb8 = sb("silu_c_cols", [P, KT])
        lam_t = sb("lam_t", [P, 5])
        lam_sums, lam_exps, neg_lam = lam_t[:, 0:2], lam_t[:, 2:4], lam_t[:, 4:5]
        half = sb("half", [P, 1])
        small = sb("small", [P, 8, 64])

        ident = consts_sb[:, 0:128]
        dist = consts_sb[:, 128:512]
        dist_c = consts_sb[:, 512:1024]
        own_half = consts_sb[:, 1024:1026]
        gate_row = scratch[:, 0:1024]
        silu_sb = scratch[:, 1024:1536].rearrange("p (s n) -> p s n", s=2)
        hid_sb = scratch[:, 1536:2048].rearrange("p (s n) -> p s n", s=2)
        v_sb = xn
        lam_sb, subln_sb = small[:, 4:8, :], small[:, 2:4, :].rearrange("p a n -> p (a n)")
        gel_rep = small[:, :, :].rearrange("p a n -> p (a n)").rearrange("p (g n) -> p g n", g=4)
        gate_flat = gate_wsb[:, :, :].rearrange("p k n -> p (k n)")
        vcb = gate_flat[:, 0:256].rearrange("p (g n) -> p g n", g=2)
        smc = gate_flat[:, 256:384].rearrange("p (a n) -> p a n", a=4)
        s_diff = scratch[:, 0:1536].rearrange("p (s c n) -> p s c n", s=2, c=2)
        at_diff = scratch[:, 1536:2304].rearrange("p (s n) -> p s n", s=2)
        o_diff = scratch[:, 2304:2560].rearrange("p (q n) -> p q n", q=2)
        sq_junk = scratch[:, 2560:3072].rearrange("p (s q n) -> p s q n", s=2, q=2)
        q_all = h_f
        kk = kv_sb[:, 0:1024].rearrange("p (b g n) -> p b g n", b=2, g=2)
        vv = kv_sb[:, 1024:2048].rearrange("p (b q n) -> p b q n", b=2, q=2)
        s_nsa = scratch[:, 0:1536].rearrange("p (u b n) -> p u b n", u=2, b=2)
        at_nsa = scratch[:, 1536:3072].rearrange("p (u b n) -> p u b n", u=2, b=2)
        kvc = scratch[:, 0:1024].rearrange("p (v g n) -> p v g n", v=2, g=2)
        kvs = scratch[:, 1024:2048].rearrange("p (v g n) -> p v g n", v=2, g=2)
        blk = xn[:, :, :].rearrange("p q n -> p (q n)")[:, 0:1920]

        psum = ctx.enter_context(nc.psum_tensor("psum", [P, 8 * BANK], F32))

        def bank(i, n=1):
            return psum[:, i * BANK:(i + n) * BANK]

        col_loaded = [sem(f"col_loaded{i}") for i in range(COL_RING)]
        row_loaded = [sem(f"row_loaded{i}") for i in range(ROW_RING)]
        side_loaded = [sem(f"side_loaded{i}") for i in range(SIDE_RING)]
        bias_loaded = [sem(f"bias_loaded{i}") for i in range(2)]
        cols_in, xT_in, xT_rest_in, x_in, consts_in, lnrow_in = (
            sem(n) for n in ("cols_in", "xT_in", "xT_rest_in", "x_in", "consts_in", "lnrow_in"))
        small_in, masks_in, nsa_small_in = sem("small_in"), sem("masks_in"), sem("nsa_small_in")
        c_ready, zero_ready = sem("c_ready"), sem("zero_ready")
        silu_c = sem("silu_c")
        col_hi_made, col_lo_made, col_used = sem("col_hi_made"), sem("col_lo_made"), sem("col_used")
        row_hi_made, row_lo_made, row_used = sem("row_hi_made"), sem("row_lo_made"), sem("row_used")
        side_used, modrow_made, modT_done, modcol_made = (sem(n) for n in ("side_used", "modrow_made", "modT_done", "modcol_made"))
        gate_spread, gate_made = sem("gate_spread"), sem("gate_made")
        fold_made = sem("fold_made")
        aff_dve, aff_act, h_hi_made, h_made = (sem(n) for n in ("aff_dve", "aff_act", "h_hi_made", "h_made"))
        v_act, v_dve = sem("v_act"), sem("v_dve")
        lam_sum, lam_exp = sem("lam_sum"), sem("lam_exp")
        qk_made, scored, biased, bias_ready, max_made, exp_made, mixed = (
            sem(n) for n in ("qk_made", "scored", "biased", "bias_ready", "max_made", "exp_made", "mixed"))
        at_done, at_act, pv_done, squared, ms_made, rstd_made, o_made, ot_done, o_hi_made, o_lo_made = (
            sem(n) for n in ("at_done", "at_act", "pv_done", "squared", "ms_made", "rstd_made", "o_made",
                             "ot_done", "o_hi_made", "o_lo_made"))
        y_done, y_read, z_made, var_made, ln_rstd, shift_made = (
            sem(n) for n in ("y_done", "y_read", "z_made", "var_made", "ln_rstd", "shift_made"))
        rows0_made, rows1_made, rows1_end_made, xt_low_done, xt_done, x_scaled, x_updated = (
            sem(n) for n in ("rows0_made", "rows1_made", "rows1_end_made", "xt_low_done", "xt_done", "x_scaled", "x_updated"))
        silu_made, hid_made, act_hi_made, act_lo_made = (sem(n) for n in ("silu_made", "hid_made", "act_hi_made", "act_lo_made"))
        gates_done, gates_exp = sem("gates_done"), sem("gates_exp")
        kv_evac, swapped, blk_made = sem("kv_evac"), sem("swapped"), sem("blk_made")
        last_rows = sem("last_rows")
        cmp_zeroed, gelu_made, gel_spread, w2_done, cmp_evac = (
            sem(n) for n in ("cmp_zeroed", "gelu_made", "gel_spread", "w2_done", "cmp_evac"))
        c_scored, c_biased, c_exp, c_made, c_tr, c_evac = (
            sem(n) for n in ("c_scored", "c_biased", "c_exp", "c_made", "c_tr", "c_evac"))
        p_scaled = sem("p_scaled")
        first_scored = sem("first_scored")
        dve_done = sem("dve_done")
        pool_done = sem("pool_done")
        out_stored = sem("out_stored")

        def at(base, b):
            return base if b is None else b * LOOP_TILES + base

        def loads(c, ring, b):
            n = 16 * (c // ring + 1)
            return n if b is None else b * (16 * LOOP_TILES // ring) + n

        head_groups = []
        for n in (3, 3, 2, 3, 3, 2, 4, 4):
            first = side(2) if not head_groups else head_groups[-1][-1] + 1
            head_groups.append(range(first, first + n))

        block = ctx.enter_context(nc.Block())

        @block.sync
        def _(sp):
            def load_col(c, b=None):
                if c >= COL_RING:
                    sp.wait_ge(col_lo_made, at(c - COL_RING + 1, b))
                src = col_w[c, :, :] if b is None else \
                    col_w[bass.ds(b * LOOP_TILES + c, 1), :, :].rearrange("a p n -> p (a n)")
                sp.dma_start(col_raw[:, c % COL_RING, :], src).then_inc(col_loaded[c % COL_RING], 16)

            def load_row(c, b=None):
                if c >= ROW_RING:
                    sp.wait_ge(row_lo_made, at(c - ROW_RING + 1, b))
                src = row_w[c, :, :] if b is None else \
                    row_w[bass.ds(b * LOOP_TILES + c, 1), :, :].rearrange("a p n -> p (a n)")
                sp.dma_start(row_raw[:, c % ROW_RING, :], src).then_inc(row_loaded[c % ROW_RING], 16)

            def load_side(*chunks):
                for c in chunks:
                    for e in range(12):
                        if c == side(e):
                            if e >= 2:
                                sp.wait_ge(modrow_made, e - 1)
                            sp.dma_start(bias_rows[:, e % 2, :], ada_bias[e, :, :]).then_inc(bias_loaded[e % 2], 16)
                    if c >= SIDE_RING:
                        sp.wait_ge(side_used, c - SIDE_RING + 1)
                    sp.dma_start(side_raw[:, c % SIDE_RING, :], side_w[c, :, :]).then_inc(side_loaded[c % SIDE_RING], 16)

            def load_ln_rows(n):
                sp.dma_start(kv_sb[:, :], ln_rows[n, :].partition_broadcast(P)).then_inc(lnrow_in, 16)

            load_side(*range(8))
            load_row(R_V)
            load_side(8, 9, 10)
            load_row(R_V + 1)
            load_side(11, 12, 13)
            load_row(R_V + 2)
            load_side(14, 15)
            load_row(R_V + 3)
            sp.dma_start(h_f[:, 4:KT, :], xT[:, 4:KT, :]).then_inc(xT_rest_in, 16)
            for c in (4, 5, 6, 7):
                load_row(R_V + c)
            load_col(C_HEAD)
            load_col(C_HEAD + 1)
            sp.dma_start(consts_sb[:, P:], consts[:, P:]).then_inc(masks_in, 16)
            for h in range(HEADS):
                load_col(C_HEAD + h + 2)
                if h in (2, 3, 4):
                    load_row(R_OUT[0] + h - 2)
                load_side(*head_groups[h])
                if h == 2:
                    sp.dma_start(gate_wsb[:, :, :], gate_w).then_inc(nsa_small_in, 16)
                    sp.dma_start(pos_sb[:, :, :], pos).then_inc(nsa_small_in, 16)
                    sp.dma_start(w2_sb[:, :], w2).then_inc(nsa_small_in, 16)
                if h == 5:
                    sp.dma_start(x_sb[:, :, :], x_nat).then_inc(x_in, 16)
            load_side(*range(side(5), side(5) + 2))
            load_row(R_OUT[0] + 3)
            load_side(*range(side(5) + 2, side(5) + 4))

            for layer in range(2):
                c0, r0 = C_FFN[layer], R_DOWN[layer]
                load_row(R_OUT[layer] + 4)
                if layer == 0:
                    load_side(*range(side(5) + 4, side(5) + 6))
                load_row(R_OUT[layer] + 5)
                if layer == 0:
                    load_side(*range(side(5) + 6, side(5) + 8))
                load_row(R_OUT[layer] + 6)
                load_row(R_OUT[layer] + 7)
                if layer == 0:
                    sp.wait_ge(scored, HEADS)
                else:
                    sp.wait_ge(pv_done, HEADS + TILES)
                load_ln_rows(2 * layer)
                load_col(c0 + 2)
                load_side(*range(side(GROUP_BESIDE_NORM[2 * layer]), side(GROUP_BESIDE_NORM[2 * layer]) + 4))
                load_side(*range(side(GROUP_BESIDE_NORM[2 * layer]) + 4, side(GROUP_BESIDE_NORM[2 * layer]) + 8))
                load_row(r0)
                load_row(r0 + 1)
                load_col(c0 + 3)
                with sp.Fori(0, 3) as b:
                    for i in (1, 2, 3):
                        load_col(c0 + 2 * i + 2, b)
                        load_row(r0 + 2 * i, b)
                        load_row(r0 + 2 * i + 1, b)
                        load_col(c0 + 2 * i + 3, b)
                load_row(r0 + 20)
                sp.wait_ge(x_updated, 4 * layer + 2)
                load_ln_rows(2 * layer + 1)
                if layer == 0:
                    load_side(*range(side(7), side(7) + 4))
                    load_col(C_NSA)
                load_row(r0 + 21)
                if layer == 0:
                    load_side(*range(side(7) + 4, side(7) + 8))
                    load_col(C_NSA + 1)
                    load_side(*range(side(8), side(8) + 8))
                    load_col(C_NSA + 2)
                    for c in range(C_NSA + 3, C_NSA + 6):
                        load_col(c)
                    load_side(*range(SIDE_W1, SIDE_W1 + 4))
                    for i in range(3):
                        load_row(R_OUT[1] + i)
                    for i in range(4):
                        load_col(C_Q + i)
                    load_side(*range(side(9), side(9) + 4))
                    load_col(C_FFN[1])
                    load_col(C_FFN[1] + 1)
                    load_row(R_OUT[1] + 3)
                    load_side(*range(side(9) + 4, side(10) + 8))
            for i, cols in enumerate((slice(0, BANK), slice(BANK, D))):
                sp.wait_ge(last_rows, 1 + i)
                sp.dma_start(out[1, :, cols], x_sb[:, 1, cols]).then_inc(out_stored, 16)
            sp.wait_ge(out_stored, 64)

        @block.tensor
        def _(pe):
            def three(dst, sh, sl, mh, ml, start, stop, **kw):
                nc.tensor.matmul(dst, sh, mh, start=start, stop=False, **kw)
                nc.tensor.matmul(dst, sh, ml, start=False, stop=False, **kw)
                return nc.tensor.matmul(dst, sl, mh, start=False, stop=stop, **kw)

            def col_views(c):
                return (col_hi[:, c % COL_SPLIT, :].rearrange("p (k n) -> p k n", k=KT),
                        col_lo[:, c % COL_SPLIT, :].rearrange("p (k n) -> p k n", k=KT))

            def col_product(c, dst, b=None, stage=None):
                pe.wait_ge(col_lo_made, at(c + 1, b))
                wh, wl = col_views(c)
                order = [(i, k) for i in range(2) for k in range(KT)]
                if stage is not None:
                    order = [(i, k) for k in range(KT) for i in range(2)]
                for i, k in order:
                    if stage is not None and i == 0:
                        pe.wait_ge(h_made, 8 * stage + k + 1)
                    last = three(dst[:, 256 * i:256 * i + 256], wh[:, k, 128 * i:128 * i + 128],
                                 wl[:, k, 128 * i:128 * i + 128], h_hi[:, k, :], h_lo[:, k, :],
                                 k == 0 and (stage is None or i == 0), k == KT - 1, skip_group_check=stage is not None)
                last.then_inc(col_used, 1)

            def col_product_natural(c, dst):
                pe.wait_ge(col_lo_made, c + 1)
                wh, wl = col_views(c)
                for q in range(QT):
                    for k in range(KT):
                        last = three(dst[:, 256 * q:256 * q + 256], h_hi[:, k, 128 * q:128 * q + 128],
                                     h_lo[:, k, 128 * q:128 * q + 128], wh[:, k, :], wl[:, k, :], k == 0, k == KT - 1)
                last.then_inc(col_used, 1)

            def row_tile(c, q, j, sh, sl, y0, start, stop, **kw):
                cols = slice(BANK * j, BANK * j + BANK)
                return three(bank(y0 + 2 * q + j), sh[:, 128 * q:128 * q + 128], sl[:, 128 * q:128 * q + 128],
                             row_hi[:, c % ROW_SPLIT, cols], row_lo[:, c % ROW_SPLIT, cols], start, stop, **kw)

            def row_product(c, sh, sl, y0, start, stop, b=None, **kw):
                pe.wait_ge(row_lo_made, at(c + 1, b))
                for q in range(QT):
                    for j in range(2):
                        last = row_tile(c, q, j, sh, sl, y0, start, stop, **kw)
                last.then_inc(row_used, 1)

            def last_row_products(chunks, slots, y0, ready, first_ready, **kw):
                for q in range(QT):
                    for j in range(2):
                        for n, c in enumerate(chunks):
                            if q == 0 and j == 0:
                                pe.wait_ge(row_lo_made, c + 1)
                                pe.wait_ge(ready, first_ready + n)
                            last = row_tile(c, q, j, o_hi[:, slots[n], :], o_lo[:, slots[n], :], y0, False,
                                            n == len(chunks) - 1, **kw)
                        if q == 0 or j == 0:
                            last.then_inc(y_done, 1)
                        else:
                            last.then_inc(row_used, len(chunks))

            def ada_chunk(e, k, dst):
                c = side(e) + k
                pe.wait_ge(side_loaded[c % SIDE_RING], 16 * (c // SIDE_RING + 1))
                for j in range(4):
                    last = nc.tensor.matmul(dst[32 * j:32 * j + 32, :], c_rep[:, k, :],
                                            side_raw[:, c % SIDE_RING, 256 * j:256 * j + 256],
                                            start=(k == 0), stop=(k == 7), tile_position=(0, 32 * j))
                last.then_inc(side_used, 1)

            def mod_transpose(slot, dst):
                for i in range(2):
                    last = nc.tensor.matmul(dst[:, 4 * i:4 * i + 4], modrow[:, slot, 128 * i:128 * i + 128],
                                            ident[:, 0:P:32], start=True, stop=True)
                last.then_inc(modT_done, 1)

            def gate_part(slot, dst, r):
                for i in range(2):
                    j = 2 * r + i
                    last = nc.tensor.matmul(dst[:, 256 * i:256 * i + 256], ident[:, 32 * j:32 * j + 1].broadcast_to([P, P]),
                                            modrow[:, slot, :], start=True, stop=True)
                last.then_inc(gate_spread, 1)

            pe.wait_ge(c_ready, 1)
            for k in range(KT):
                ada_chunk(0, k, bank(4)[:, 0:256])
            pe.wait_ge(consts_in, 16)
            pe.wait_ge(modrow_made, 1)
            mod_transpose(0, bank(6))

            def second_half(*ks):
                for k in ks:
                    ada_chunk(1, k, bank(5)[:, 0:256])

            second_half(0, 1)
            for k in range(KT):
                pe.wait_ge(h_made, k + 1)
                row_product(R_V + k, h_hi[:, k, :], h_lo[:, k, :], 0, k == 0, k == KT - 1)
                if k == 0:
                    second_half(2, 3)
                if k == 1:
                    second_half(4, 5, 6, 7)
                    pe.wait_ge(modrow_made, 2)
                    mod_transpose(1, bank(7))

            def project(h):
                if h >= 2:
                    pe.wait_ge(qk_made, h - 1)
                col_product(C_HEAD + h, bank(4 + h % 2))

            def score(h):
                pe.wait_ge(qk_made, h + 1)
                if h >= 1:
                    pe.wait_ge(biased, 4 * h)
                qk = qk_diff[:, h % 2, :]
                for q, lo, n in ((0, 0, 128), (1, 128, 256)):
                    for c in range(2):
                        rows = slice(64 * c, 64 * c + 64)
                        last = nc.tensor.matmul(bank(6 + c)[:, lo:lo + n], qk[rows, 128 * q:128 * q + 128],
                                                qk[rows, 256:256 + n], start=True, stop=True)
                last.then_inc(scored, 1)

            def transpose_probs(h):
                if h >= 1:
                    pe.wait_ge(at_act, h)
                if h in (5, 7):
                    pe.wait_ge(modrow_made, 4 if h == 5 else 5)
                    mod_transpose(0, bank(2)[:, 384:392])
                if h == 6:
                    pe.wait_ge(modcol_made, 1)
                pe.wait_ge(mixed, h + 1)
                for i in range(3):
                    last = nc.tensor.transpose(bank(2)[:, 128 * i:128 * i + 128], s_diff[:, h % 2, 0, 128 * i:128 * i + 128], ident)
                last.then_inc(at_done, 1)

            def weigh_values(h):
                pe.wait_ge(at_act, h + 1)
                if h >= 1:
                    pe.wait_ge(o_made, h)
                a = at_diff[:, h % 2, :]
                v = slice(P * h, P * h + P)
                nc.tensor.matmul(bank(3)[:, 0:128], a[:, 0:128], v_sb[:, 0, v], start=True, stop=True)
                nc.tensor.matmul(bank(3)[:, 128:256], a[:, 128:256], v_sb[:, 0, v], start=True, stop=False)
                nc.tensor.matmul(bank(3)[:, 128:256], a[:, 256:384], v_sb[:, 1, v], start=False, stop=True).then_inc(pv_done, 1)

            def transpose_out(h):
                pe.wait_ge(o_made, h + 1)
                if h >= 1:
                    pe.wait_ge(o_lo_made, h)
                for q in range(QT):
                    last = nc.tensor.transpose(bank(1)[:, 128 * q:128 * q + 128], o_diff[:, q, :], ident)
                last.then_inc(ot_done, 1)

            def head_ada(t, i):
                c = head_groups[t][i] if t < HEADS else side(5) + i
                e, k = c // 8, c % 8
                if t == 0 and i == 0:
                    pe.wait_ge(v_act, 1)
                    pe.wait_ge(v_dve, 1)
                elif k == 0:
                    pe.wait_ge(modrow_made, e)
                ada_chunk(e, k, bank(0)[:, 0:256])

            qk_diff = kv_sb[:, 0:1024].rearrange("p (s n) -> p s n", s=2)
            for t in range(HEADS):
                project(t)
                head_ada(t, 0)
                if t >= 2:
                    transpose_probs(t - 2)
                if t >= 1:
                    score(t - 1)
                head_ada(t, 1)
                if t >= 3:
                    transpose_out(t - 3)
                if t not in (2, 5):
                    head_ada(t, 2)
                if t >= 2:
                    weigh_values(t - 2)
                if t >= 6:
                    head_ada(t, 3)
            score(7)
            head_ada(8, 0)
            head_ada(8, 1)
            transpose_probs(6)
            transpose_out(5)
            weigh_values(6)
            head_ada(8, 2)

            def out_product(layer, k):
                pe.wait_ge(o_lo_made, HEADS * layer + k + 1)
                row_product(R_OUT[layer] + k, o_hi[:, k, :], o_lo[:, k, :], 4, k == 0, False)

            def last_out_products(layer):
                last_row_products([R_OUT[layer] + k for k in range(8 - LAST, 8)], range(8 - LAST, 8), 4, o_lo_made, HEADS * layer + 9 - LAST)

            pe.wait_ge(biased, 4 * HEADS)
            out_product(0, 0)
            head_ada(8, 3)
            transpose_probs(7)
            head_ada(8, 4)
            out_product(0, 1)
            transpose_out(6)
            weigh_values(7)
            head_ada(8, 5)
            pe.wait_ge(at_act, 8)
            pe.wait_ge(modcol_made, 2)
            gate_part(1, bank(2), 0)
            out_product(0, 2)
            out_product(0, 3)
            transpose_out(7)
            head_ada(8, 6)
            out_product(0, 4)
            head_ada(8, 7)
            pe.wait_ge(gate_made, 1)
            gate_part(1, bank(2), 1)
            last_out_products(0)

            def transpose_rows(n, y0, ybank):
                pe.wait_ge(y_read, 4 * n + 2)
                group_beside_norm(n, ybank, range(4))
                for q in range(QT):
                    pe.wait_ge((rows0_made, rows1_made)[q], n + 1)
                    if n == 0 and q == 0:
                        pe.wait_ge(modrow_made, 6)
                        pe.wait_ge(gate_made, 2)
                        pe.wait_ge(o_lo_made, HEADS)
                    for k in range(KT):
                        if q == 1 and k == 4:
                            pe.wait_ge(rows1_end_made, n + 1)
                        o = 128 * (k % 4)
                        last = nc.tensor.transpose(bank(y0 + 2 * (k // 4) + q)[:, o:o + 128], xn[:, q, 128 * k:128 * k + 128], ident)
                        if q == 1 and k == 3:
                            last.then_inc(xt_low_done, 1)
                    if q == 1:
                        last.then_inc(xt_done, 1)
                    group_beside_norm(n, ybank, (4 + q,))

            def group_beside_norm(n, ybank, chunks):
                for k in chunks:
                    ada_chunk(GROUP_BESIDE_NORM[n], k, bank(ybank)[:, 0:256])

            def ffn(layer):
                c0, r0, j0 = C_FFN[layer], R_DOWN[layer], HT * layer

                def hidden(j, b=None, stage=None):
                    if j >= 2:
                        pe.wait_ge(hid_made, at(j0 + j - 1, b))
                    col_product(c0 + j, bank(6 + j % 2), b, stage)

                def down(j, b=None):
                    pe.wait_ge(act_lo_made, at(j0 + j + 1, b))
                    s = j % FFN_SLOTS
                    row_product(r0 + j, o_hi[:, s, :], o_lo[:, s, :], 0, False, False, b, skip_group_check=True)

                hidden(0, stage=2 * layer + 1)
                if layer == 0:
                    pe.wait_ge(zero_ready, 1)
                for i in range(4):
                    nc.tensor.matmul(bank(i), zeros[:, :], h_hi[:, 0:2, :].rearrange("p k n -> p (k n)"),
                                     start=True, stop=False, skip_group_check=True)
                hidden(1)
                group_beside_norm(2 * layer, 5, (6, 7))
                with pe.Fori(0, 3) as b:
                    for i in (1, 2, 3):
                        hidden(2 * i, b)
                        hidden(2 * i + 1, b)
                        down(2 * i - 2, b)
                        down(2 * i - 1, b)
                pe.wait_ge(modrow_made, 7 if layer == 0 else 12)
                gate_part(2, bank(4), 0)
                hidden(20)
                if layer == 0:
                    pe.wait_ge(gate_made, 3)
                    gate_part(2, bank(4), 1)
                down(18)
                if layer == 0:
                    for k in range(4):
                        ada_chunk(7, k, bank(5)[:, 0:256])
                    pe.wait_ge(gate_made, 4)
                    mod_transpose(0, bank(4))
                hidden(21)
                if layer == 0:
                    for k in range(4, 8):
                        ada_chunk(7, k, bank(5)[:, 0:256])
                else:
                    pe.wait_ge(gate_made, 7)
                    gate_part(2, bank(4), 1)
                last_row_products([r0 + j for j in range(HT - LAST, HT)], [j % FFN_SLOTS for j in range(HT - LAST, HT)],
                                  0, act_lo_made, j0 + HT - LAST + 1, skip_group_check=True)
                if layer == 0:
                    pe.wait_ge(modrow_made, 8)
                    pe.wait_ge(modcol_made, 3)
                    mod_transpose(1, bank(4))

            transpose_rows(0, 0, 5)
            ffn(0)
            pe.wait_ge(modcol_made, 4)
            transpose_rows(1, 4, 1)

            for i in range(6):
                if i >= 2:
                    pe.wait_ge(kv_evac, i - 1)
                if i < 4:
                    col_product(C_NSA + i, bank(2 * (i % 2)), None, 2 if i == 0 else None)
                else:
                    col_product_natural(C_NSA + i, bank(2 * (i % 2)))
                if i == 0:
                    pe.wait_ge(nsa_small_in, 48)
                    for q in range(QT):
                        for k in range(KT):
                            last = nc.tensor.matmul(bank(5)[:, 48 * q:48 * q + 48], h_f[:, k, 128 * q:128 * q + 128],
                                                    gate_wsb[:, k, :], start=(k == 0), stop=(k == KT - 1))
                    last.then_inc(gates_done, 1)
                if i == 1:
                    group_beside_norm(1, 1, (6, 7))
            blocks = blk.rearrange("p (v n l) -> p v n l", v=2, l=16)
            for v in range(2):
                pe.wait_ge(blk_made, 4 * v + 4)
                for half_ in range(2):
                    c = SIDE_W1 + 2 * v + half_
                    pe.wait_ge(side_loaded[c % SIDE_RING], 16 * (c // SIDE_RING + 1))
                    for i in range(8):
                        l = 8 * half_ + i
                        last = nc.tensor.matmul(bank(3)[:, 64 * v:64 * v + 60], side_raw[:, c % SIDE_RING, 128 * i:128 * i + 128],
                                                blocks[:, v, :, l], start=(l == 0), stop=(l == 15))
                    last.then_inc(side_used, 1)

            def compressed_scores(pairs):
                pe.wait_ge(qk_made, HEADS + pairs[-1] // 2 + 1)
                for q in range(QT):
                    for t in pairs:
                        o = 256 * q + 32 * t
                        last = nc.tensor.matmul(bank(0)[:, o:o + 32], q_all[:, t, 128 * q:128 * q + 128],
                                                kcb[:, t // 4, :, :].rearrange("p u n -> p (u n)"), start=True, stop=True)
                return last

            def query_product(i):
                if i == 1:
                    pe.wait_ge(kv_evac, 6)
                if i >= 2:
                    pe.wait_ge(qk_made, HEADS + i - 1)
                col_product(C_Q + i, bank(4 - 2 * (i % 2)))

            query_product(0)
            query_product(1)
            pe.wait_ge(gelu_made, 2)
            nc.tensor.matmul(bank(3)[:, 128:192], w2_sb[:, 0:128], gel[:, 0, :, :].rearrange("p g n -> p (g n)"),
                             start=True, stop=True)
            pe.wait_ge(gel_spread, 1)
            for g in range(4):
                last = nc.tensor.matmul(bank(3)[:, 192 + 64 * g:256 + 64 * g], gel_rep[:, g, :],
                                        w2_sb[:, 128:192], start=True, stop=True)
            last.then_inc(w2_done, 1)
            query_product(2)
            pe.wait_ge(cmp_evac, 1)
            compressed_scores((0, 1, 2, 3))

            def nsa_score(t, between=None):
                pe.wait_ge(qk_made, HEADS + t // 2 + 1)
                if t == 0:
                    pe.wait_ge(kv_evac, 6)
                if t >= 1:
                    pe.wait_ge(biased, 4 * HEADS + 8 * t)
                gp = t // 4

                def keys(u, q):
                    rows = slice(64 * u, 64 * u + 64)
                    for s in range(2):
                        if q == 0:
                            dst = bank(5)[:, 256 * u + 128 * s:256 * u + 128 * s + 128]
                        else:
                            dst = bank(6 + u)[:, 256 * s:256 * s + 256]
                        last = nc.tensor.matmul(dst, q_all[rows, t, 128 * q:128 * q + 128],
                                                kk[rows, s, gp, 0:128 * (q + 1)], start=True, stop=True)
                    return last

                keys(0, 0).then_inc(first_scored, 1)
                keys(1, 1)
                if between is not None:
                    between()
                keys(0, 1)
                pe.wait_ge(first_scored, t + 1)
                keys(1, 0).then_inc(scored, 1)

            def nsa_transpose(t, u):
                if t == 0 and u == 0:
                    pe.wait_ge(modrow_made, 9)
                    pe.wait_ge(qk_made, HEADS + 4)
                else:
                    pe.wait_ge(at_act, HEADS + 2 * t + u)
                if t == 4 and u == 0:
                    pe.wait_ge(modrow_made, 10)
                    mod_transpose(0, bank(1)[:, 384:392])
                if t == 4 and u == 1:
                    pe.wait_ge(modcol_made, 5)
                pe.wait_ge(p_scaled, 2 * t + u + 1)
                for s in range(2):
                    for i in range(3):
                        last = nc.tensor.transpose(bank(1 + s)[:, 128 * i:128 * i + 128],
                                                   s_nsa[:, u, s, 128 * i:128 * i + 128], ident)
                last.then_inc(at_done, 1)

            def nsa_weigh(t):
                if t >= 1:
                    pe.wait_ge(o_lo_made, HEADS + t)
                pe.wait_ge(at_act, HEADS + 2 * t + 2)
                for s in range(2):
                    for k in range(2):
                        lo, n = ((0, 256), (256, 128))[k]
                        for u in range(2):
                            cols = slice(64 * (2 * (t // 4) + u), 64 * (2 * (t // 4) + u) + 64)
                            nc.tensor.matmul(bank(3)[64 * u:64 * u + 64, 256 - n:256], vv[:, s, k, cols],
                                             at_nsa[:, u, s, lo:lo + n], start=(s == 0 and k == 0), stop=False,
                                             tile_position=(0, 64 * u), skip_group_check=True)
                if t == 0:
                    pe.wait_ge(c_evac, 1)
                rows = slice(32 * (t % 4), 32 * (t % 4) + 32)
                nc.tensor.matmul(bank(3)[:, 0:256], vcb[rows, t // 4, :], sc[rows, 256 * (t // 4):256 * (t // 4) + 256],
                                 start=False, stop=True, tile_position=(32 * (t % 4), 0), skip_group_check=True)\
                    .then_inc(pv_done, 1)

            def nsa_ada(t, i):
                if t == 4 and i == 0:
                    pe.wait_ge(modrow_made, 10)
                if t == 0 and i == 0:
                    pe.wait_ge(qk_made, HEADS + 3)
                ada_chunk(9 + t // 4, 2 * (t % 4) + i, bank(4)[:, 0:256])

            nsa_score(0)
            query_product(3)
            compressed_scores((4, 5))
            compressed_scores((6, 7)).then_inc(c_scored, 1)
            nsa_ada(0, 0)
            nsa_ada(0, 1)
            for t in range(1, TILES):
                nsa_score(t, between=lambda: nsa_transpose(t - 1, 0))
                nsa_transpose(t - 1, 1)
                nsa_ada(t, 0)
                nsa_ada(t, 1)
                if t == 1:
                    pe.wait_ge(c_made, 1)
                    for gp in range(2):
                        for q in range(QT):
                            i = 2 * gp + q
                            o = 256 * q + 128 * gp
                            last = nc.tensor.transpose(bank(0)[:, 128 * i:128 * i + 128], sc[:, o:o + 128], ident)
                    last.then_inc(c_tr, 1)
                nsa_weigh(t - 1)

            pe.wait_ge(biased, 4 * HEADS + 8 * TILES)
            pe.wait_ge(modrow_made, 11)
            out_product(1, 0)
            nsa_transpose(TILES - 1, 0)
            out_product(1, 1)
            nsa_transpose(TILES - 1, 1)
            out_product(1, 2)
            nsa_weigh(TILES - 1)
            gate_part(1, bank(2), 0)
            out_product(1, 3)
            out_product(1, 4)
            pe.wait_ge(gate_made, 5)
            gate_part(1, bank(2), 1)
            mod_transpose(0, bank(1))
            last_out_products(1)
            pe.wait_ge(gate_made, 6)
            pe.wait_ge(modcol_made, 6)
            transpose_rows(2, 0, 5)
            ffn(1)

        @block.scalar
        def _(act):
            def split_col(c, b=None):
                act.wait_ge(col_loaded[c % COL_RING], loads(c, COL_RING, b))
                if c >= COL_SPLIT:
                    act.wait_ge(col_used, at(c - COL_SPLIT + 1, b))
                nc.scalar.activation(col_hi[:, c % COL_SPLIT, :], col_raw[:, c % COL_RING, :], ACT.Copy).then_inc(col_hi_made, 1)

            def split_row(c, b=None):
                act.wait_ge(row_loaded[c % ROW_RING], loads(c, ROW_RING, b))
                if c >= ROW_SPLIT:
                    act.wait_ge(row_used, at(c - ROW_SPLIT + 1, b))
                nc.scalar.activation(row_hi[:, c % ROW_SPLIT, :], row_raw[:, c % ROW_RING, :], ACT.Copy).then_inc(row_hi_made, 1)

            def copy_modcol(n, e, src):
                act.wait_ge(modT_done, n + 1)
                nc.scalar.activation(modcol[:, e, :].rearrange("p (j i) -> p i j", j=4),
                                     src[:, 0:8].rearrange("p (i j) -> p i j", i=2), ACT.Copy).then_inc(modcol_made, 1)

            act.dma_start(cols_sb[:, :, :], cols).then_inc(cols_in, 16)
            act.dma_start(h_f[:, 0:4, :], xT[:, 0:4, :]).then_inc(xT_in, 16)
            act.dma_start(ident, consts[:, 0:P]).then_inc(consts_in, 16)
            act.wait_ge(cols_in, 16)
            nc.scalar.activation(silu_sb8[:, :], cols_sb[:, 0, :], ACT.Silu).then_inc(silu_c, 1)
            act.wait_ge(lam_sum, 1)
            nc.scalar.activation(lam_exps, lam_sums, ACT.Exp).then_inc(lam_exp, 1)

            def input_tiles(stage):
                act.wait_ge(fold_made, stage)
                y0 = 4 if stage == 2 else 0

                def affine(k):
                    if k == 4:
                        act.wait_ge(xt_done, stage)
                    src = bank(y0 + 2 * (k // 4), 2).rearrange("p (q n) -> p q n", q=2)[:, :, 128 * (k % 4):128 * (k % 4) + 128]
                    nc.scalar.activation(h_f[:, k, :].rearrange("p (q n) -> p q n", q=2), src, ACT.Identity,
                                         scale=fold[:, stage, 0, k:k + 1], bias=fold[:, stage, 1, k:k + 1]).then_inc(aff_act, 1)

                for k in range(KT):
                    if k < 4:
                        act.wait_ge(aff_dve, 4 * stage + k + 5)
                    else:
                        act.wait_ge(aff_act, 4 * stage + k - 7)
                    nc.scalar.activation(h_hi[:, k, :], h_f[:, k, :], ACT.Copy).then_inc(h_hi_made, 1)
                    if k < 4:
                        affine(4 + k)

            split_row(R_V)
            for k in range(KT):
                act.wait_ge(aff_dve, k + 1)
                nc.scalar.activation(h_hi[:, k, :], h_f[:, k, :], ACT.Copy).then_inc(h_hi_made, 1)
                if k == 3:
                    for c in (1, 2, 3):
                        split_row(R_V + c)
                if k == 6:
                    split_row(R_V + 4)
            for c in range(5, 8):
                split_row(R_V + c)
            split_col(0)
            split_col(1)
            act.wait_ge(row_used, 8)
            nc.scalar.activation(v_sb[:, 0, :], bank(0, 2), ACT.Copy).then_inc(v_act, 1)

            qk_diff = kv_sb[:, 0:1024].rearrange("p (s n) -> p s n", s=2)

            def copy_probs(h):
                act.wait_ge(at_done, h + 1)
                if h >= 2:
                    act.wait_ge(pv_done, h - 1)
                nc.scalar.activation(at_diff[:, h % 2, :], bank(2)[:, 0:384], ACT.Copy).then_inc(at_act, 1)

            def exps(h):
                act.wait_ge(max_made, h + 1)
                for c in range(2):
                    for q, lo, n in ((0, 0, 128), (1, 128, 256)):
                        s = s_diff[:, h % 2, c, lo:lo + n]
                        i = 2 * c + q
                        nc.scalar.activation(s, s, ACT.Exp, scale=SCALE, bias=sml[:, h, 4 + i:5 + i],
                                             accum_out=sml[:, h, 8 + i:9 + i]).then_inc(exp_made, 1)

            def squares(h):
                act.wait_ge(pv_done, h + 1)
                for q in range(QT):
                    nc.scalar.activation(sq_junk[:, h % 2, q, :], bank(3)[:, 128 * q:128 * q + 128], ACT.Square,
                                         scale=sml[:, h, 12 + q:13 + q], accum_out=sml[:, h, 18 + q:19 + q]).then_inc(squared, 1)

            def out_hi(h):
                act.wait_ge(ot_done, h + 1)
                nc.scalar.activation(o_hi[:, h, :], bank(1)[:, 0:256], ACT.Copy).then_inc(o_hi_made, 1)

            for t in range(9):
                if t < HEADS:
                    act.wait_ge(col_used, t + 1)
                    if t >= 2:
                        act.wait_ge(scored, t - 1)
                    nc.scalar.activation(qk_diff[:, t % 2, :], bank(4 + t % 2), ACT.Copy).then_inc(qk_made, 1)
                if t >= 2:
                    copy_probs(t - 2)
                if t == 7:
                    copy_modcol(2, 3, bank(2)[:, 384:392])
                if t >= 1:
                    exps(t - 1)
                if t >= 3:
                    out_hi(t - 3)
                if t >= 2:
                    squares(t - 2)
                if t < HEADS - 1:
                    split_col(C_HEAD + t + 2)
                if t >= 6:
                    split_row(R_OUT[0] + t - 6)

            def normalise(n):
                for q, lo, done in ((0, 0, rows0_made), (1, BANK, rows1_end_made)):
                    if n == 3 and q == 1:
                        break
                    act.wait_ge(shift_made, 2 * n + q + 1)
                    z, st = xn[:, q, lo:D], stats[:, q, :]
                    nc.scalar.activation(z, z, ACT.Identity, scale=st[:, 15:16], bias=st[:, 16:17]).then_inc(done, 1)

            def copy_gate(i, src, r):
                act.wait_ge(gate_spread, i + 1)
                nc.scalar.activation(gate_row[:, BANK * r:BANK * r + BANK], src, ACT.Copy).then_inc(gate_made, 1)

            copy_probs(7)
            copy_modcol(3, 4, bank(2)[:, 384:392])
            split_row(R_OUT[0] + 3)
            out_hi(6)
            squares(7)
            copy_gate(0, bank(2), 0)
            split_row(R_OUT[0] + 4)
            split_row(R_OUT[0] + 5)
            out_hi(7)
            split_row(R_OUT[0] + 6)
            split_row(R_OUT[0] + 7)
            copy_gate(1, bank(2), 1)
            split_col(C_FFN[0] + 1)

            def ffn(layer):
                c0, r0, j0 = C_FFN[layer], R_DOWN[layer], HT * layer

                def silu(j, b=None):
                    act.wait_ge(col_used, at(c0 + j + 1, b))
                    if j >= 2:
                        act.wait_ge(hid_made, at(j0 + j - 1, b))
                    nc.scalar.activation(silu_sb[:, j % 2, :], bank(6 + j % 2)[:, 0:256], ACT.Silu).then_inc(silu_made, 1)

                def hid_hi(j, b=None):
                    act.wait_ge(hid_made, at(j0 + j + 1, b))
                    if j >= FFN_SLOTS:
                        act.wait_ge(row_used, at(r0 + j - FFN_SLOTS + 1, b))
                    nc.scalar.activation(o_hi[:, j % FFN_SLOTS, :], hid_sb[:, j % 2, :], ACT.Copy).then_inc(act_hi_made, 1)

                def step(i, b=None):
                    silu(2 * i, b)
                    split_col(c0 + 2 * i + 2, b)
                    hid_hi(2 * i - 1, b)
                    silu(2 * i + 1, b)
                    split_col(c0 + 2 * i + 3, b)
                    hid_hi(2 * i, b)
                    split_row(r0 + 2 * i, b)
                    split_row(r0 + 2 * i + 1, b)

                silu(0)
                split_col(c0 + 2)
                silu(1)
                split_col(c0 + 3)
                hid_hi(0)
                split_row(r0)
                split_row(r0 + 1)
                with act.Fori(0, 3) as b:
                    for i in (1, 2, 3):
                        step(i, b)
                copy_gate(4 * layer + 2, bank(4), 0)
                silu(20)
                if layer == 0:
                    copy_gate(3, bank(4), 1)
                split_row(r0 + 20)
                hid_hi(19)
                hid_hi(20)
                split_row(r0 + 21)
                if layer == 0:
                    copy_modcol(4, 6, bank(4))
                    split_col(C_NSA)
                silu(21)
                hid_hi(21)
                if layer == 0:
                    copy_modcol(5, 7, bank(4))
                else:
                    copy_gate(7, bank(4), 1)

            normalise(0)
            input_tiles(1)
            ffn(0)
            normalise(1)
            input_tiles(2)
            split_col(C_NSA + 1)

            for i in range(6):
                act.wait_ge(col_used, C_NSA + i + 1)
                if i < 2:
                    dst = kvc[:, i, :, :].rearrange("p g n -> p (g n)")
                elif i < 4:
                    dst = kk[:, i - 2, :, :].rearrange("p g n -> p (g n)")
                else:
                    dst = vv[:, i - 4, :, :].rearrange("p q n -> p (q n)")
                if i == 2:
                    act.wait_ge(x_updated, 4)
                nc.scalar.activation(dst, bank(2 * (i % 2)), ACT.Copy).then_inc(kv_evac, 1)
                split_col(C_NSA + i + 2)
                if i == 0:
                    act.wait_ge(gates_done, 1)
                    nc.scalar.activation(gate_sb[:, :], bank(5)[:, 0:96], ACT.Exp, scale=-1.0).then_inc(gates_exp, 1)
            act.wait_ge(cmp_zeroed, 1)
            act.wait_ge(side_used, SIDE_W1 + 4)
            for v in range(2):
                nc.scalar.activation(gel[:, v, :, 0:N_CMP], bank(3)[:, 64 * v:64 * v + 60].rearrange("p (g n) -> p g n", g=4),
                                     ACT.Gelu_apprx_tanh).then_inc(gelu_made, 1)
            for i in range(3):
                split_row(R_OUT[1] + i)

            def copy_queries(i):
                act.wait_ge(col_used, C_Q + i + 1)
                nc.scalar.activation(q_all[:, 2 * i:2 * i + 2, :].rearrange("p t n -> p (t n)"), bank(4 - 2 * (i % 2)), ACT.Copy)\
                    .then_inc(qk_made, 1)
                if i < 2:
                    split_col(C_Q + i + 2)

            for i in range(3):
                copy_queries(i)

            def nsa_exps(t, u):
                act.wait_ge(max_made, HEADS + 2 * t + u + 1)
                for q, lo, n in ((0, 0, 128), (1, 128, 256)):
                    for s in range(2):
                        x = s_nsa[:, u, s, lo:lo + n]
                        i = (2 * u + q) * 2 + s
                        nc.scalar.activation(x, x, ACT.Exp, scale=SCALE, bias=sml[:, t, 8 + i:9 + i],
                                             accum_out=sml[:, t, 16 + i:17 + i]).then_inc(exp_made, 1)

            for t in range(TILES + 1):
                if t == 1:
                    copy_queries(3)
                    act.wait_ge(c_biased, 1)
                    nc.scalar.activation(sc[:, :], sc[:, :], ACT.Exp, scale=SCALE).then_inc(c_exp, 1)
                if t >= 1:
                    for u in range(2):
                        act.wait_ge(at_done, HEADS + 2 * (t - 1) + u + 1)
                        if t >= 2:
                            act.wait_ge(pv_done, HEADS + t - 1)
                        nc.scalar.activation(at_nsa[:, u, :, :], bank(1, 2).rearrange("p (s n) -> p s n", s=2)[:, :, 0:384],
                                             ACT.Copy).then_inc(at_act, 1)
                        if t == 5 and u == 0:
                            copy_modcol(6, 9, bank(1)[:, 384:392])
                        if t == TILES:
                            split_row(R_OUT[1] + 3 + u)
                if t == 1:
                    act.wait_ge(c_tr, 1)
                    nc.scalar.activation(sc[:, :], bank(0), ACT.Copy).then_inc(c_evac, 1)
                if t < TILES:
                    nsa_exps(t, 0)
                    nsa_exps(t, 1)
                if t == TILES:
                    split_col(C_FFN[1])
                if t >= 1:
                    act.wait_ge(pv_done, HEADS + t)
                    nc.scalar.activation(o_hi[:, t - 1, :], bank(3)[:, 0:256], ACT.Copy).then_inc(o_hi_made, 1)

            copy_gate(4, bank(2), 0)
            split_row(R_OUT[1] + 5)
            split_row(R_OUT[1] + 6)
            split_row(R_OUT[1] + 7)
            copy_gate(5, bank(2), 1)
            copy_modcol(7, 10, bank(1))
            split_col(C_FFN[1] + 1)
            normalise(2)
            input_tiles(3)
            ffn(1)
            normalise(3)
            for i, half_ in enumerate((slice(0, BANK), slice(BANK, D))):
                act.wait_ge(x_updated, 7 + i)
                act.dma_start(out[0, :, half_], x_sb[:, 0, half_]).then_inc(out_stored, 16)

        @block.vector
        def _(dve):
            own = [0]

            def then(ins):
                own[0] += 1
                ins.then_inc(dve_done, 1)
                dve.wait_ge(dve_done, own[0])

            def split_col(c, b=None):
                dve.wait_ge(col_hi_made, at(c + 1, b))
                nc.vector.tensor_tensor(col_lo[:, c % COL_SPLIT, :], col_raw[:, c % COL_RING, :],
                                        col_hi[:, c % COL_SPLIT, :].bitcast(F32), ALU.subtract).then_inc(col_lo_made, 1)

            def split_row(c, b=None):
                dve.wait_ge(row_hi_made, at(c + 1, b))
                nc.vector.tensor_tensor(row_lo[:, c % ROW_SPLIT, :], row_raw[:, c % ROW_RING, :],
                                        row_hi[:, c % ROW_SPLIT, :].bitcast(F32), ALU.subtract).then_inc(row_lo_made, 1)

            def make_modrow(e, src, slot):
                one = 0.0 if e in (0, 1) or e % 6 in (0, 3) else 1.0
                dve.wait_ge(bias_loaded[e % 2], 16 * (e // 2 + 1))
                dve.wait_ge(side_used, side(e) + 8)
                if e in (4, 6, 8, 9, 10):
                    dve.wait_ge(modT_done, {4: 3, 6: 4, 8: 6, 9: 5, 10: 7}[e])
                if e in (7, 11):
                    dve.wait_ge(gate_spread, {7: 2, 11: 4}[e])
                nc.vector.scalar_tensor_tensor(modrow[:, slot, :], src, one, bias_rows[:, e % 2, :], ALU.add, ALU.add)\
                    .then_inc(modrow_made, 1)

            def make_first_fold(e):
                dve.wait_ge(modT_done, e + 1)
                src = bank(6 + e)[:, 0:8].rearrange("p (i j) -> p i j", i=2)
                shift, scale = (fold[:, 0, a, 4 * e:4 * e + 4].rearrange("p (j i) -> p i j", j=2) for a in (1, 0))
                nc.vector.tensor_copy(shift, src[:, :, 0:2])
                then(nc.vector.tensor_scalar(scale, src[:, :, 2:4], 1.0, None, ALU.add))

            def make_fold(stage, shift, scale, ncol):
                a, b = fold[:, stage, 0, :], fold[:, stage, 1, :]
                dve.wait_ge(modcol_made, ncol)
                g, s = cols_sb[:, 2 * stage - 1, :], cols_sb[:, 2 * stage, :]
                nc.vector.tensor_tensor(a, g, modcol[:, scale, :], ALU.mult)
                then(nc.vector.tensor_tensor(b, s, modcol[:, scale, :], ALU.mult))
                nc.vector.tensor_tensor(b, b, modcol[:, shift, :], ALU.add).then_inc(fold_made, 1)

            def input_tiles(stage):
                dve.wait_ge(xt_low_done, stage)
                dve.wait_ge(fold_made, stage)
                y0 = 4 if stage == 2 else 0

                def affine(k):
                    src = bank(y0, 2).rearrange("p (q n) -> p q n", q=2)[:, :, 128 * k:128 * k + 128]
                    nc.vector.tensor_scalar(h_f[:, k, :].rearrange("p (q n) -> p q n", q=2), src, fold[:, stage, 0, k:k + 1],
                                            fold[:, stage, 1, k:k + 1], ALU.mult, ALU.add).then_inc(aff_dve, 1)

                affine(0)
                for k in range(KT):
                    if k < 3:
                        affine(k + 1)
                    input_lo(stage, k)

            def input_lo(stage, k):
                dve.wait_ge(h_hi_made, 8 * stage + k + 1)
                nc.vector.tensor_tensor(h_lo[:, k, :], h_f[:, k, :], h_hi[:, k, :].bitcast(F32), ALU.subtract)\
                    .then_inc(h_made, 1)

            def last_rows_part(lo, n):
                z, st = xn[:, 1, lo:lo + n], stats[:, 1, :]
                dve.wait_ge(lnrow_in, 64)
                then(nc.vector.scalar_tensor_tensor(z, z, st[:, 12:13], kv_sb[:, lo:lo + n], ALU.subtract, ALU.mult))
                dve.wait_ge(ln_rstd, 8)
                nc.vector.scalar_tensor_tensor(x_sb[:, 1, lo:lo + n], z, st[:, 15:16], kv_sb[:, D + lo:D + lo + n], ALU.mult, ALU.add)\
                    .then_inc(last_rows, 1)

            def norm(n, y0):
                row_end = (R_OUT[0] + 8, R_DOWN[0] + 22, R_OUT[1] + 8, R_DOWN[1] + 22)[n]
                dve.wait_ge(gate_made, 2 * n + 2)
                dve.wait_ge(x_in, 16)
                if n >= 1:
                    dve.wait_ge(x_updated, 2 * n)
                if n == 0:
                    dve.wait_ge(pv_done, HEADS)

                def half_rows(q, j):
                    i = 2 * q + j
                    if i < 3:
                        dve.wait_ge(y_done, 3 * n + i + 1)
                    else:
                        dve.wait_ge(row_used, row_end)
                    cols = slice(BANK * j, BANK * j + BANK)
                    z = xn[:, q, cols]
                    nc.vector.tensor_tensor(z, bank(y0 + i), gate_row[:, cols], ALU.mult).then_inc(y_read, 1)
                    dve.wait_ge(y_read, 4 * n + i + 1)
                    nc.vector.scalar_tensor_tensor(z, x_sb[:, q, cols], ALPHA, z, ALU.mult, ALU.add).then_inc(z_made, 1)
                    dve.wait_ge(z_made, 4 * n + i + 1)
                    return nc.vector.bn_stats(stats[:, q, 6 * j:6 * j + 6], z)

                def variance(q):
                    st = stats[:, q, :]
                    then(nc.vector.bn_aggr(st[:, 12:14], st[:, 0:12]))
                    nc.vector.tensor_scalar(st[:, 17:18], st[:, 12:13], -1.0, None, ALU.mult)
                    nc.vector.tensor_scalar(st[:, 14:15], st[:, 13:14], LN_EPS, None, ALU.add).then_inc(var_made, 1)

                half_rows(0, 0)
                then(half_rows(0, 1))
                variance(0)
                half_rows(1, 0)
                then(half_rows(1, 1))
                variance(1)
                if n < 3:
                    dve.wait_ge(ln_rstd, 2 * n + 2)
                    z, st = xn[:, 1, 0:BANK], stats[:, 1, :]
                    nc.vector.tensor_scalar(z, z, st[:, 12:13], st[:, 15:16], ALU.subtract, ALU.mult).then_inc(rows1_made, 1)
                if n == 1:
                    make_fold(2, 6, 7, 4)

            dve.wait_ge(silu_c, 1)
            nc.vector.tensor_copy(c_rep[:, :, :], silu_sb8[:, :].unsqueeze(2).broadcast_to([P, KT, 32])).then_inc(c_ready, 1)
            nc.vector.memset(kcb[:, :, :, :], 0.0)
            nc.vector.memset(gel[:, :, :, :], 0.0).then_inc(cmp_zeroed, 1)
            dve.wait_ge(small_in, 32)
            then(nc.vector.tensor_tensor(small[:, 0:2, :], lam_sb[:, 0:4:2, :], lam_sb[:, 1:4:2, :], ALU.mult))
            nc.vector.tensor_reduce(lam_sums, small[:, 0:2, :], op=ALU.add, axis=AX.X).then_inc(lam_sum, 1)
            dve.wait_ge(lam_exp, 1)
            then(nc.vector.tensor_tensor(neg_lam, lam_exps[:, 1:2], lam_exps[:, 0:1], ALU.subtract))
            then(nc.vector.tensor_scalar(neg_lam, neg_lam, -LAM_INIT, None, ALU.add))
            then(nc.vector.tensor_scalar(subln_sb, subln_sb, 1.0 - LAM_INIT, None, ALU.mult))
            def first_affine(k):
                nc.vector.tensor_scalar(h_f[:, k, :], h_f[:, k, :], fold[:, 0, 0, k:k + 1], fold[:, 0, 1, k:k + 1],
                                        ALU.mult, ALU.add).then_inc(aff_dve, 1)

            make_modrow(0, bank(4)[:, 0:256], 0)
            make_first_fold(0)
            dve.wait_ge(xT_in, 16)
            for k in range(4):
                first_affine(k)
                if k == 1:
                    split_row(R_V)
                    input_lo(0, 0)
            for k in range(1, 4):
                input_lo(0, k)
            split_row(R_V + 1)
            split_row(R_V + 2)
            make_modrow(1, bank(5)[:, 0:256], 1)
            make_first_fold(1)
            dve.wait_ge(xT_rest_in, 16)
            first_affine(4)
            first_affine(5)
            split_row(R_V + 3)
            input_lo(0, 4)
            first_affine(6)
            input_lo(0, 5)
            first_affine(7)
            input_lo(0, 6)
            split_row(R_V + 4)
            input_lo(0, 7)
            for c in range(5, 8):
                split_row(R_V + c)
            split_col(0)
            split_col(1)
            dve.wait_ge(row_used, 8)
            nc.vector.tensor_copy(v_sb[:, 1, :], bank(2, 2)).then_inc(v_dve, 1)

            def bias_max(h):
                dve.wait_ge(scored, h + 1)
                dve.wait_ge(bias_ready, h + 1)
                if h >= 2:
                    dve.wait_ge(at_done, h - 1)
                for c in range(2):
                    for q, lo, n in ((0, 0, 128), (1, 128, 256)):
                        i = 2 * c + q
                        nc.vector.tensor_tensor_reduce(out=s_diff[:, h % 2, c, lo:lo + n], in0=bank(6 + c)[:, lo:lo + n],
                                                       in1=bias_t[:, h % 2, lo:lo + n], scale=1.0, scalar=FAR_BELOW,
                                                       op0=ALU.add, op1=ALU.max, accum_out=sml[:, h, i:i + 1]).then_inc(biased, 1)
                dve.wait_ge(biased, 4 * h + 4)
                nc.vector.tensor_scalar(sml[:, h, 4:8], sml[:, h, 0:4], -SCALE, None, ALU.mult).then_inc(max_made, 1)

            def mix(h):
                s = sml[:, h, :]
                dve.wait_ge(exp_made, 4 * h + 4)
                then(nc.vector.reciprocal(s[:, 12:16], s[:, 8:12]))
                then(nc.vector.scalar_tensor_tensor(s[:, 16:18], s[:, 8:10], neg_lam, s[:, 14:16], ALU.mult, ALU.mult))
                for q, lo, n in ((0, 0, 128), (1, 128, 256)):
                    p0 = s_diff[:, h % 2, 0, lo:lo + n]
                    last = nc.vector.scalar_tensor_tensor(p0, s_diff[:, h % 2, 1, lo:lo + n], s[:, 16 + q:17 + q], p0,
                                                          ALU.mult, ALU.add)
                last.then_inc(mixed, 1)

            def normalise(h):
                s = sml[:, h, :]
                dve.wait_ge(squared, 2 * h + 2)
                nc.vector.tensor_scalar(s[:, 20:22], s[:, 18:20], 1.0 / P, RMS_EPS, ALU.mult, ALU.add).then_inc(ms_made, 1)
                dve.wait_ge(rstd_made, h + 1)
                then(nc.vector.tensor_tensor(s[:, 24:26], s[:, 22:24], s[:, 12:14], ALU.mult))
                if h >= 1:
                    dve.wait_ge(ot_done, h)
                for q in range(QT):
                    last = nc.vector.scalar_tensor_tensor(o_diff[:, q, :], bank(3)[:, 128 * q:128 * q + 128],
                                                          s[:, 24 + q:25 + q], subln_sb, ALU.mult, ALU.mult)
                last.then_inc(o_made, 1)

            def out_lo(h):
                dve.wait_ge(o_hi_made, h + 1)
                nc.vector.tensor_tensor(o_lo[:, h, :], bank(1)[:, 0:256], o_hi[:, h, :].bitcast(F32), ALU.subtract)\
                    .then_inc(o_lo_made, 1)

            for t in range(9):
                if t >= 1:
                    bias_max(t - 1)
                if t in (2, 5, 7):
                    make_modrow({2: 2, 5: 3, 7: 4}[t], bank(0)[:, 0:256], 1 if t == 2 else 0)
                if t >= 3:
                    out_lo(t - 3)
                if t >= 1:
                    mix(t - 1)
                if t >= 2:
                    normalise(t - 2)
                if t < HEADS - 1:
                    split_col(C_HEAD + t + 2)
                if t >= 6:
                    split_row(R_OUT[0] + t - 6)
            split_row(R_OUT[0] + 3)
            out_lo(6)
            normalise(7)
            split_row(R_OUT[0] + 4)
            split_row(R_OUT[0] + 5)
            out_lo(7)
            make_fold(1, 3, 4, 2)
            split_row(R_OUT[0] + 6)
            split_row(R_OUT[0] + 7)
            make_modrow(5, bank(0)[:, 0:256], 2)

            def ffn(layer):
                c0, r0, j0 = C_FFN[layer], R_DOWN[layer], HT * layer

                def hid(j, b=None):
                    dve.wait_ge(silu_made, at(j0 + j + 1, b))
                    if j >= 2:
                        dve.wait_ge(act_lo_made, at(j0 + j - 1, b))
                    nc.vector.tensor_tensor(hid_sb[:, j % 2, :], bank(6 + j % 2)[:, 256:512], silu_sb[:, j % 2, :], ALU.mult)\
                        .then_inc(hid_made, 1)

                def hid_lo(j, b=None):
                    dve.wait_ge(act_hi_made, at(j0 + j + 1, b))
                    nc.vector.tensor_tensor(o_lo[:, j % FFN_SLOTS, :], hid_sb[:, j % 2, :], o_hi[:, j % FFN_SLOTS, :].bitcast(F32), ALU.subtract)\
                        .then_inc(act_lo_made, 1)

                def step(i, b=None):
                    hid(2 * i, b)
                    split_col(c0 + 2 * i + 2, b)
                    hid_lo(2 * i - 1, b)
                    hid(2 * i + 1, b)
                    split_col(c0 + 2 * i + 3, b)
                    hid_lo(2 * i, b)
                    split_row(r0 + 2 * i, b)
                    split_row(r0 + 2 * i + 1, b)

                hid(0)
                split_col(c0 + 2)
                hid(1)
                split_col(c0 + 3)
                hid_lo(0)
                if layer == 0:
                    make_modrow(6, bank(5)[:, 0:256], 0)
                else:
                    make_modrow(11, bank(5)[:, 0:256], 2)
                split_row(r0)
                split_row(r0 + 1)
                with dve.Fori(0, 3) as b:
                    for i in (1, 2, 3):
                        step(i, b)
                hid(20)
                split_row(r0 + 20)
                hid_lo(19)
                hid_lo(20)
                split_row(r0 + 21)
                if layer == 0:
                    split_col(C_NSA)
                hid(21)
                hid_lo(21)
                if layer == 0:
                    make_modrow(7, bank(5)[:, 0:256], 1)

            norm(0, 4)
            input_tiles(1)
            split_col(C_FFN[0] + 1)
            ffn(0)
            norm(1, 0)
            input_tiles(2)
            split_col(C_NSA + 1)

            def make_blocks(v):
                for par in range(2):
                    rows = slice(64 * par, 64 * par + 64)
                    for u in range(2):
                        src = (kvc if u == par else kvs)[rows, v, :, :]
                        for gp in range(2):
                            win = src[:, gp, :]
                            o = (v * 4 + 2 * gp + u) * 240
                            dst = blk[rows, o:o + 240].rearrange("p (n l) -> p n l", l=16)
                            lo_half = win[:, 0:240].rearrange("p (n l e) -> p n l e", l=8, e=2)[:, :, :, par]
                            hi_half = win[:, 16:256].rearrange("p (n l e) -> p n l e", l=8, e=2)[:, :, :, par]
                            pb = pos_sb[rows, v, :]
                            nc.vector.tensor_tensor(dst[:, :, 0:8], lo_half, pb[:, 0:8].unsqueeze(1).broadcast_to([64, N_CMP, 8]), ALU.add)
                            last = nc.vector.tensor_tensor(dst[:, :, 8:16], hi_half, pb[:, 8:16].unsqueeze(1).broadcast_to([64, N_CMP, 8]), ALU.add)
                        if u == 1:
                            last.then_inc(blk_made, 2)

            dve.wait_ge(nsa_small_in, 48)
            for c in range(6):
                if c == 2:
                    make_modrow(8, bank(1)[:, 0:256], 1)
                if c == 1:
                    dve.wait_ge(gates_exp, 1)
                    then(nc.vector.tensor_scalar(gate_sb[:, :], gate_sb[:, :], 1.0, None, ALU.add))
                    then(nc.vector.reciprocal(gate_sb[:, :], gate_sb[:, :]))
                split_col(C_NSA + c + 2)
                if c == 2:
                    dve.wait_ge(swapped, 32)
                    dve.wait_ge(x_updated, 4)
                if c in (2, 3):
                    make_blocks(c - 2)
            dve.wait_ge(gelu_made, 2)
            nc.vector.tensor_copy(gel_rep.rearrange("p g (r n) -> p g r n", r=8),
                                  gel[:, 1, :, :].unsqueeze(2).broadcast_to([P, 4, 8, 16])).then_inc(gel_spread, 1)
            for i in range(3):
                split_row(R_OUT[1] + i)
            split_col(C_Q + 2)
            dve.wait_ge(w2_done, 1)
            for u in range(2):
                rows = slice(64 * u, 64 * u + 64)
                nc.vector.tensor_copy(kcb[rows, :, u, :], bank(3)[rows, 128:192].rearrange("p (g u n) -> p g u n", g=2, u=2)[:, :, u, :])
            nc.vector.tensor_tensor(vcb.rearrange("p g (u d) -> p g u d", u=2),
                                    bank(3)[:, 192:448].rearrange("p (g u d) -> p g u d", g=2, u=2),
                                    own_half.unsqueeze(1).unsqueeze(3).broadcast_to([P, 2, 2, 64]), ALU.mult).then_inc(cmp_evac, 1)
            split_col(C_Q + 3)

            def nsa_bias_max(t, u):
                dve.wait_ge(scored, HEADS + t + 1)
                dve.wait_ge(bias_ready, HEADS + 2 * t + u + 1)
                if t >= 1:
                    dve.wait_ge(at_done, HEADS + 2 * (t - 1) + u + 1)
                for q, lo, n in ((0, 0, 128), (1, 128, 256)):
                    for s in range(2):
                        i = (2 * u + q) * 2 + s
                        src = bank(5)[:, 256 * u + 128 * s:256 * u + 128 * s + 128] if q == 0 else bank(6 + u)[:, 256 * s:256 * s + 256]
                        nc.vector.tensor_tensor_reduce(out=s_nsa[:, u, s, lo:lo + n], in0=src, in1=bias_t[:, u, lo:lo + n],
                                                       scale=1.0, scalar=FAR_BELOW, op0=ALU.add, op1=ALU.max,
                                                       accum_out=sml[:, t, i:i + 1]).then_inc(biased, 1)
                dve.wait_ge(biased, 4 * HEADS + 8 * t + 4 * u + 4)
                nc.vector.tensor_scalar(sml[:, t, 8 + 4 * u:12 + 4 * u], sml[:, t, 4 * u:4 * u + 4], -SCALE, None, ALU.mult)\
                    .then_inc(max_made, 1)

            def scale_probs(t, u):
                s = sml[:, t, :]
                dve.wait_ge(exp_made, 4 * HEADS + 8 * t + 4 * u + 4)
                then(nc.vector.reciprocal(s[:, 24 + 4 * u:28 + 4 * u], s[:, 16 + 4 * u:20 + 4 * u]))
                g = gate_sb[:, :].rearrange("p (q s h) -> p q s h", q=2, s=3)[:, :, 1:3, 2 * t + u]
                then(nc.vector.tensor_tensor(s[:, 32 + 4 * u:36 + 4 * u].rearrange("p (q s) -> p q s", q=2),
                                             s[:, 24 + 4 * u:28 + 4 * u].rearrange("p (q s) -> p q s", q=2), g, ALU.mult))
                for q, lo, n in ((0, 0, 128), (1, 128, 256)):
                    for b in range(2):
                        i = 32 + 4 * u + 2 * q + b
                        p = s_nsa[:, u, b, lo:lo + n]
                        last = nc.vector.tensor_scalar(p, p, s[:, i:i + 1], None, ALU.mult)
                last.then_inc(p_scaled, 1)

            s3 = sc[:, :].rearrange("p (h n) -> p h n", n=16)
            for t in range(TILES + 1):
                if t < TILES:
                    nsa_bias_max(t, 0)
                if t < TILES:
                    nsa_bias_max(t, 1)
                    if t == TILES - 1:
                        make_modrow(10, bank(4)[:, 0:256], 0)
                    scale_probs(t, 0)
                    scale_probs(t, 1)
                if t == 0:
                    dve.wait_ge(c_scored, 1)
                    then(nc.vector.tensor_tensor(sc[:, :], bank(0), dist_c, ALU.add))
                    then(nc.vector.tensor_reduce(smc[:, 0, :], s3, op=ALU.max, axis=AX.X))
                    nc.vector.tensor_tensor(s3, s3, smc[:, 0, :].unsqueeze(2).broadcast_to([P, 32, 16]), ALU.subtract).then_inc(c_biased, 1)
                    dve.wait_ge(c_exp, 1)
                    then(nc.vector.tensor_reduce(smc[:, 1, :], s3, op=ALU.add, axis=AX.X))
                    then(nc.vector.reciprocal(smc[:, 2, :], smc[:, 1, :]))
                    g = gate_sb[:, :].rearrange("p (q s h) -> p q s h", q=2, s=3)[:, :, 0, :]
                    then(nc.vector.tensor_tensor(smc[:, 3, :].rearrange("p (q h) -> p q h", q=2),
                                                 smc[:, 2, :].rearrange("p (q h) -> p q h", q=2), g, ALU.mult))
                    then(nc.vector.scalar_tensor_tensor(sc[:, :], dist_c, -1.0e29, sc[:, :], ALU.is_gt, ALU.mult))
                    nc.vector.tensor_tensor(s3, s3, smc[:, 3, :].unsqueeze(2).broadcast_to([P, 32, 16]), ALU.mult).then_inc(c_made, 1)
                if t == 3:
                    make_modrow(9, bank(4)[:, 0:256], 0)
                if t == TILES:
                    split_row(R_OUT[1] + 3)
                    split_row(R_OUT[1] + 4)
                if t >= 1:
                    dve.wait_ge(o_hi_made, HEADS + t)
                    nc.vector.tensor_tensor(o_lo[:, t - 1, :], bank(3)[:, 0:256], o_hi[:, t - 1, :].bitcast(F32), ALU.subtract)\
                        .then_inc(o_lo_made, 1)
            split_col(C_FFN[1])
            split_row(R_OUT[1] + 5)
            split_row(R_OUT[1] + 6)
            split_row(R_OUT[1] + 7)
            make_fold(3, 9, 10, 6)
            norm(2, 4)
            input_tiles(3)
            split_col(C_FFN[1] + 1)
            ffn(1)
            norm(3, 0)
            last_rows_part(0, BANK)
            last_rows_part(BANK, BANK)

        @block.gpsimd
        def _(pool):
            own = [0]

            def then(ins):
                own[0] += 1
                ins.then_inc(pool_done, 1)
                pool.wait_ge(pool_done, own[0])

            pool.dma_start(lam_sb.rearrange("p a n -> p (a n)"), lam[0, :].partition_broadcast(P)).then_inc(small_in, 16)
            pool.dma_start(subln_sb, subln[0, :].partition_broadcast(P)).then_inc(small_in, 16)
            nc.gpsimd.memset(zeros[:, :].bitcast(F32), 0.0).then_inc(zero_ready, 1)
            then(nc.gpsimd.memset(half[:, :], -0.5))
            pool.wait_ge(masks_in, 16)

            def bias(slot, slope):
                nc.gpsimd.tensor_scalar(bias_t[:, slot, :], dist, slope / SCALE, 1.0, ALU.mult, ALU.mult).then_inc(bias_ready, 1)

            def rstd(dst, src):
                return nc.gpsimd.tensor_tensor(dst, src, half[:, :].broadcast_to([P, dst.shape[1]]), ALU.pow)

            def row_rstd(h):
                pool.wait_ge(ms_made, h + 1)
                rstd(sml[:, h, 22:24], sml[:, h, 20:22]).then_inc(rstd_made, 1)

            for h in range(HEADS):
                if h >= 2:
                    pool.wait_ge(biased, 4 * (h - 1))
                bias(h % 2, 2.0 ** -(h + 1))
                if h >= 3:
                    row_rstd(h - 3)
            for h in range(HEADS - 3, HEADS):
                row_rstd(h)

            def norm(n):
                def tile_rstd(q):
                    pool.wait_ge(var_made, 2 * n + q + 1)
                    st = stats[:, q, :]
                    rstd(st[:, 15:16], st[:, 14:15]).then_inc(ln_rstd, 1)
                    if n < 3 or q == 0:
                        pool.wait_ge(ln_rstd, 2 * n + q + 1)
                        nc.gpsimd.tensor_tensor(st[:, 16:17], st[:, 17:18], st[:, 15:16], ALU.mult).then_inc(shift_made, 1)

                def scale_rows(q):
                    pool.wait_ge(lnrow_in, 16 * (n + 1))
                    pool.wait_ge((rows0_made, rows1_made)[q], n + 1)
                    if q == 1:
                        pool.wait_ge(rows1_end_made, n + 1)
                    nc.gpsimd.tensor_tensor(x_sb[:, q, :], xn[:, q, :], kv_sb[:, 0:D], ALU.mult).then_inc(x_scaled, 1)

                def shift_rows(q, lo=0, hi=D):
                    pool.wait_ge(x_scaled, 2 * n + q + 1)
                    nc.gpsimd.tensor_tensor(x_sb[:, q, lo:hi], x_sb[:, q, lo:hi], kv_sb[:, D + lo:D + hi], ALU.add).then_inc(x_updated, 1)

                tile_rstd(0)
                if n < 3:
                    tile_rstd(1)
                    for q in range(QT):
                        scale_rows(q)
                        shift_rows(q)
                else:
                    scale_rows(0)
                    tile_rstd(1)
                    shift_rows(0, 0, BANK)
                    shift_rows(0, BANK, D)

            norm(0)
            norm(1)
            pool.wait_ge(kv_evac, 2)
            pool.dma_start(kvs[64:128, :, :, :].rearrange("p v g n -> p (v g n)"), kvc[0:64, :, :, :].rearrange("p v g n -> p (v g n)")).then_inc(swapped, 16)
            pool.dma_start(kvs[0:64, :, :, :].rearrange("p v g n -> p (v g n)"), kvc[64:128, :, :, :].rearrange("p v g n -> p (v g n)")).then_inc(swapped, 16)
            for t in range(TILES):
                for u in range(2):
                    if t >= 1:
                        pool.wait_ge(biased, 4 * HEADS + 8 * (t - 1) + 4 * u + 4)
                    else:
                        pool.wait_ge(biased, 4 * HEADS)
                    head = 4 * (2 * (t // 4) + u) + t % 4
                    bias(u, 2.0 ** (-0.5 * (head + 1)))
            norm(2)
            norm(3)


def kernel(x, c, diff_w_in, diff_w_out, diff_lam_q1, diff_lam_k1, diff_lam_q2, diff_lam_k2, diff_subln_g,
           nsa_w_in, nsa_cmp_pos_k, nsa_cmp_pos_v, nsa_cmp_k_w1, nsa_cmp_k_w2, nsa_cmp_v_w1, nsa_cmp_v_w2,
           nsa_w_out, ada_w, ada_b, ln_mix_g, ln_mix_b, ln_ffn_g, ln_ffn_b, ffn_w_gu, ffn_w_down):
    import numpy as np
    import concourse.bacc as bacc
    from concourse.bass_utils import run_bass_kernel_spmd

    def arr(a):
        return np.asarray(a)

    def pairs(w, blocks):
        cols = np.concatenate([w[:, a:a + n] for a, n in blocks], axis=1)
        return cols.reshape(KT, P, 256).transpose(1, 0, 2).reshape(P, KT * 256)

    def column(v):
        return v.reshape(-1, P).T

    w_in, w_nsa = arr(diff_w_in)[0], arr(nsa_w_in)[0]
    gu, dn = arr(ffn_w_gu), arr(ffn_w_down)
    heads = [(8 * (t // 4) + t % 4, 8 * (t // 4) + 4 + t % 4) for t in range(TILES)]
    flat_heads = [h for pair in heads for h in pair]
    col_chunks = [pairs(w_in, [(P * h, P), (D + P * h, P)]) for h in range(HEADS)]
    col_chunks += [pairs(gu[0], [(P * j, P), (HID + P * j, P)]) for j in range(HT)]
    col_chunks += [pairs(w_nsa, [(o, 256)]) for o in (1024, 1280, 1536, 2048, 1792, 2304)]
    for i in range(4):
        a, b, e, f = heads[2 * i] + heads[2 * i + 1]
        col_chunks.append(pairs(w_nsa, [(64 * a, 64), (64 * b, 64), (64 * e, 64), (64 * f, 64)]))
    col_chunks += [pairs(gu[1], [(P * j, P), (HID + P * j, P)]) for j in range(HT)]
    w_o = np.concatenate([arr(nsa_w_out)[0][64 * h:64 * h + 64] for h in flat_heads], axis=0)
    row_chunks = np.concatenate([w_in[:, 2 * D:3 * D], arr(diff_w_out)[0], dn[0], w_o, dn[1]], axis=0).reshape(N_ROW, P, D)
    ada = arr(ada_w).reshape(2, KT, P, 6, D).transpose(0, 3, 1, 2, 4).reshape(96, P, D)
    w1 = [arr(w)[0].reshape(2, 8, P, P).transpose(0, 2, 1, 3).reshape(2, P, D) for w in (nsa_cmp_k_w1, nsa_cmp_v_w1)]
    first = ada[:16].reshape(2, KT, P, 2, BANK).transpose(3, 1, 2, 0, 4).reshape(16, P, D)
    side_chunks = np.concatenate([first, ada[16:SIDE_W1]] + w1 + [ada[SIDE_W1:]], axis=0)
    ada_rows = arr(ada_b).reshape(12, D)
    ada_rows = np.concatenate([ada_rows[:2].reshape(2, 2, BANK).transpose(1, 0, 2).reshape(2, D), ada_rows[2:]], axis=0)
    ada_bias = np.repeat(ada_rows.reshape(12, 4, 256), 32, axis=1)
    norms = [(arr(g)[i], arr(b)[i]) for i in range(2) for g, b in ((ln_mix_g, ln_mix_b), (ln_ffn_g, ln_ffn_b))]
    cols = np.stack([column(arr(c)[0])] + [column(v) for pair in norms for v in pair], axis=1)
    xs = arr(x)[0]
    gate_cols = [2560 + 3 * h + s for s in range(3) for h in flat_heads]
    gate_w = np.stack([w_nsa[:, i] for i in gate_cols], axis=1).reshape(KT, P, 48).transpose(1, 0, 2)
    pos = np.stack([arr(p)[0].reshape(16, P).T for p in (nsa_cmp_pos_k, nsa_cmp_pos_v)], axis=1)
    k2, v2 = arr(nsa_cmp_k_w2)[0], arr(nsa_cmp_v_w2)[0]
    w2 = np.concatenate([k2, k2, v2], axis=1)
    lam = np.concatenate([arr(v) for v in (diff_lam_q1, diff_lam_k1, diff_lam_q2, diff_lam_k2)], axis=1)
    ln_rows = np.stack([np.concatenate(pair) for pair in norms])

    p = np.arange(P)

    def masked(d):
        return np.where(d >= 0, -d, -1e30)

    dist = np.concatenate([masked(p[:, None] - p[None, :]), masked(P + p[:, None] - np.arange(T)[None, :])], axis=1)
    dist_c = np.full((P, QT, TILES, 2, 16), -1e30)
    for q in range(QT):
        for t in range(TILES):
            for u in range(2):
                d = (P * q + p)[:, None] - (16 * np.arange(N_CMP) + 31)[None, :]
                slope = 2.0 ** (-0.5 * (heads[t][u] + 1)) / SCALE
                dist_c[:, q, t, u, :N_CMP] = np.where(d >= 0, -d * slope, -1e30)
    own = (p[:, None] // 16 % 2 == np.arange(2)[None, :]) * 1.0
    consts = np.concatenate([np.eye(P), dist, dist_c.reshape(P, 512), own], axis=1).astype(np.float32)

    arrays = {
        "col_w": np.stack(col_chunks), "row_w": row_chunks, "side": side_chunks, "ada_bias": ada_bias, "cols": cols,
        "xT": xs.T.reshape(KT, P, T).transpose(1, 0, 2), "x_nat": xs.reshape(QT, P, D).transpose(1, 0, 2),
        "ln_rows": ln_rows, "lam": lam, "subln": arr(diff_subln_g), "gate_w": gate_w, "pos": pos, "w2": w2, "consts": consts,
    }
    arrays = {f"in_{n}": np.ascontiguousarray(a) for n, a in arrays.items()}
    nc = bacc.Bacc("TRN2", target_bir_lowering=False, num_devices=1)
    args = [nc.dram_tensor(n, a.shape, mybir.dt.from_np(a.dtype), kind="ExternalInput").ap() for n, a in arrays.items()]
    args.append(nc.dram_tensor("out_x", (QT, P, D), F32, kind="ExternalOutput").ap())
    decoder(nc, *args)
    r = run_bass_kernel_spmd(nc, [arrays], core_ids=[0])
    return r.results[0]["out_x"].reshape(1, T, D)
```
